# Optimizing a Trainium2 kernel written in Bass

```python
import math
import jax, jax.numpy as jnp
from jax import lax
import numpy as np

D_MODEL = 1024
BATCH = 1
SEQ = 512
DEPTH = 2

HEAD_DIM = 64
QBLOCK = 128
N_A = 8
N_B = 8
N_B_KV = 2
WINDOW = 128
N_C = 8
N_IDX = 8
D_IDX = 32
TOPK_MAX = 256
N_D = 8
Q_LORA = 256
KV_LORA = 128
QK_NOPE = 64
QK_ROPE = 32
V_DIM = 64
ROPE_THETA = 10000.0
REL_BUCKETS = 32
REL_MAX_EXACT = 16
REL_MAX_DIST = 128
REL_SLOTS = N_B + N_C
D_FF = 4 * D_MODEL
EPS = 1e-6

EVEN_SIZES = (N_A * HEAD_DIM, N_A * HEAD_DIM, N_A * HEAD_DIM, N_A,
              N_B * HEAD_DIM, N_B_KV * HEAD_DIM, N_B_KV * HEAD_DIM)
EVEN_IN = sum(EVEN_SIZES)
EVEN_OUT = N_A * HEAD_DIM + N_B * HEAD_DIM
ODD_SIZES = (N_C * HEAD_DIM, HEAD_DIM, HEAD_DIM,
             N_IDX * D_IDX, D_IDX, N_IDX,
             Q_LORA, KV_LORA, QK_ROPE)
ODD_IN = sum(ODD_SIZES)
ODD_OUT = N_C * HEAD_DIM + N_D * V_DIM

kernel_name = "hybrid_fox_swa_dsa_mla_trunk"

def _split(h, sizes):
    outs, off = [], 0
    for s in sizes:
        outs.append(h[..., off:off + s])
        off += s
    return outs

def _rmsnorm(x, g):
    xf = x.astype(jnp.float32)
    y = xf * lax.rsqrt(jnp.mean(xf * xf, axis=-1, keepdims=True) + EPS)
    return (y * g.astype(jnp.float32)).astype(x.dtype)

def _t5_bucket(n):
    nf = n.astype(jnp.float32)
    large = REL_MAX_EXACT + (jnp.log(jnp.maximum(nf, float(REL_MAX_EXACT)) / REL_MAX_EXACT)
                             / math.log(REL_MAX_DIST / REL_MAX_EXACT)
                             * (REL_BUCKETS - REL_MAX_EXACT)).astype(jnp.int32)
    large = jnp.minimum(large, REL_BUCKETS - 1)
    return jnp.where(n < REL_MAX_EXACT, n, large)

def _rope_tables(S, dim):
    pos = jnp.arange(S, dtype=jnp.float32)
    inv = ROPE_THETA ** (-jnp.arange(0, dim, 2, dtype=jnp.float32) / dim)
    ang = pos[:, None] * inv[None, :]
    return jnp.cos(ang), jnp.sin(ang)

def _rope(x, cos, sin):
    half = x.shape[-1] // 2
    x1, x2 = x[..., :half], x[..., half:]
    c = cos[None, :, None, :].astype(x.dtype)
    s = sin[None, :, None, :].astype(x.dtype)
    return jnp.concatenate([x1 * c - x2 * s, x1 * s + x2 * c], axis=-1)

def _blocked_causal_attn(q, k, v, log_f_cum=None):
    B, S, H, dq = q.shape
    nb = S // QBLOCK
    scale = dq ** -0.5
    key_pos = jnp.arange(S)
    q_blocks = q.reshape(B, nb, QBLOCK, H, dq).transpose(1, 0, 2, 3, 4)
    starts = jnp.arange(nb) * QBLOCK
    if log_f_cum is not None:
        F_keys = log_f_cum.transpose(0, 2, 1)
        F_blocks = log_f_cum.reshape(B, nb, QBLOCK, H).transpose(1, 0, 2, 3)
        xs = (q_blocks, starts, F_blocks)
    else:
        xs = (q_blocks, starts)

    def one_block(blk):
        qb, start = blk[0], blk[1]
        logits = jnp.einsum("bqhd,bshd->bhqs", qb, k).astype(jnp.float32) * scale
        if log_f_cum is not None:
            Fq = blk[2].astype(jnp.float32).transpose(0, 2, 1)
            logits = logits + Fq[..., None] - F_keys[:, :, None, :].astype(jnp.float32)
        q_pos = start + jnp.arange(QBLOCK)
        mask = key_pos[None, :] <= q_pos[:, None]
        logits = jnp.where(mask[None, None], logits, -jnp.inf)
        p = jax.nn.softmax(logits, axis=-1)
        return jnp.einsum("bhqs,bshd->bqhd", p.astype(v.dtype), v)

    out = lax.map(one_block, xs)
    return out.transpose(1, 0, 2, 3, 4).reshape(B, S, H * v.shape[-1])

def _swa_with_sinks(q, k, v, sinks, bias_table):
    B, S, Hq, d = q.shape
    Hkv = k.shape[2]
    G = Hq // Hkv
    W = WINDOW
    nb = S // W
    qb = q.reshape(B, nb, W, Hkv, G, d)

    def band(a):
        prev = jnp.pad(a, ((0, 0), (W, 0), (0, 0), (0, 0)))[:, :S]
        return jnp.concatenate([prev.reshape(B, nb, W, Hkv, d), a.reshape(B, nb, W, Hkv, d)], axis=2)

    kb, vb = band(k), band(v)
    logits = jnp.einsum("bnqhgd,bnkhd->bnhgqk", qb, kb).astype(jnp.float32) * (d ** -0.5)
    dist = jnp.arange(W)[:, None] + W - jnp.arange(2 * W)[None, :]
    key_pos = jnp.arange(nb)[:, None] * W - W + jnp.arange(2 * W)[None, :]
    mask = ((dist >= 0) & (dist < W))[None] & (key_pos >= 0)[:, None, :]
    bias = bias_table[_t5_bucket(jnp.maximum(dist, 0))]
    bias = bias.reshape(W, 2 * W, Hkv, G).transpose(2, 3, 0, 1).astype(jnp.float32)
    logits = jnp.where(mask[None, :, None, None], logits + bias, -jnp.inf)
    sink = jnp.broadcast_to(sinks.astype(jnp.float32).reshape(Hkv, G, 1, 1), logits.shape[:-1] + (1,))
    p = jax.nn.softmax(jnp.concatenate([logits, sink], axis=-1), axis=-1)[..., :-1]
    out = jnp.einsum("bnhgqk,bnkhd->bnqhgd", p.astype(v.dtype), vb)
    return out.reshape(B, S, Hq * d)

def _dsa_sparse_attn(q, k_c, v_c, q_idx, k_idx, w_idx, bias_table, topk):
    B, S, H, d = q.shape
    nb = S // QBLOCK
    key_pos = jnp.arange(S)
    gather = jax.vmap(lambda a, i: a[i])
    xs = (q.reshape(B, nb, QBLOCK, H, d).transpose(1, 0, 2, 3, 4),
          q_idx.reshape(B, nb, QBLOCK, N_IDX, D_IDX).transpose(1, 0, 2, 3, 4),
          w_idx.reshape(B, nb, QBLOCK, N_IDX).transpose(1, 0, 2, 3),
          jnp.arange(nb) * QBLOCK)

    def one_block(blk):
        qb, qib, wib, start = blk
        q_pos = start + jnp.arange(QBLOCK)
        rel = jax.nn.relu(jnp.einsum("bqhe,bse->bqhs", qib, k_idx).astype(jnp.float32) * (D_IDX ** -0.5))
        score = jnp.einsum("bqhs,bqh->bqs", rel, wib.astype(jnp.float32) * (N_IDX ** -0.5))
        causal = key_pos[None, :] <= q_pos[:, None]
        score = jnp.where(causal[None], score, -jnp.inf)
        _, idx = lax.top_k(score, topk)
        k_sel = gather(k_c, idx)
        v_sel = gather(v_c, idx)
        logits = jnp.einsum("bqhd,bqkd->bqhk", qb, k_sel).astype(jnp.float32) * (d ** -0.5)
        dist = q_pos[None, :, None] - idx
        bias = bias_table[_t5_bucket(jnp.maximum(dist, 0))].transpose(0, 1, 3, 2).astype(jnp.float32)
        logits = jnp.where((dist >= 0)[:, :, None, :], logits + bias, -jnp.inf)
        p = jax.nn.softmax(logits, axis=-1)
        return jnp.einsum("bqhk,bqkd->bqhd", p.astype(v_c.dtype), v_sel)

    out = lax.map(one_block, xs)
    return out.transpose(1, 0, 2, 3, 4).reshape(B, S, H * d)

def _even_mixer(h, w_in, b_f, sinks, w_out, rel_bias):
    B, S, _ = h.shape
    proj = h @ w_in
    qa, ka, va, fa, qb, kb, vb = _split(proj, EVEN_SIZES)
    log_f = jax.nn.log_sigmoid((fa + b_f).astype(jnp.float32))
    F = jnp.cumsum(log_f, axis=1)
    out_a = _blocked_causal_attn(qa.reshape(B, S, N_A, HEAD_DIM), ka.reshape(B, S, N_A, HEAD_DIM),
                                 va.reshape(B, S, N_A, HEAD_DIM), F)
    out_b = _swa_with_sinks(qb.reshape(B, S, N_B, HEAD_DIM), kb.reshape(B, S, N_B_KV, HEAD_DIM),
                            vb.reshape(B, S, N_B_KV, HEAD_DIM), sinks, rel_bias[:, :N_B])
    return jnp.concatenate([out_a, out_b], axis=-1) @ w_out

def _odd_mixer(h, w_in, norm_cq, norm_ckv, w_uq, w_ukv, w_out, rel_bias, topk):
    B, S, _ = h.shape
    proj = h @ w_in
    qc, kc, vc, qi, ki, wi, cq, ckv, kr = _split(proj, ODD_SIZES)
    out_c = _dsa_sparse_attn(qc.reshape(B, S, N_C, HEAD_DIM), kc, vc,
                             qi.reshape(B, S, N_IDX, D_IDX), ki, wi, rel_bias[:, N_B:], topk)
    q_d = (_rmsnorm(cq, norm_cq) @ w_uq).reshape(B, S, N_D, QK_NOPE + QK_ROPE)
    kv_d = (_rmsnorm(ckv, norm_ckv) @ w_ukv).reshape(B, S, N_D, QK_NOPE + V_DIM)
    cos, sin = _rope_tables(S, QK_ROPE)
    q_nope, q_rope = q_d[..., :QK_NOPE], _rope(q_d[..., QK_NOPE:], cos, sin)
    k_nope, v_d = kv_d[..., :QK_NOPE], kv_d[..., QK_NOPE:]
    k_rope = jnp.broadcast_to(_rope(kr[:, :, None, :], cos, sin), (B, S, N_D, QK_ROPE))
    out_d = _blocked_causal_attn(jnp.concatenate([q_nope, q_rope], axis=-1),
                                 jnp.concatenate([k_nope, k_rope], axis=-1), v_d)
    return jnp.concatenate([out_c, out_d], axis=-1) @ w_out

def _mlp(h, w1, w2):
    return jnp.square(jax.nn.relu(h @ w1)) @ w2

def setup_inputs(seed: int = 0) -> dict:
    key = jax.random.key(seed)
    ks = jax.random.split(key, 20)
    NE = (DEPTH + 1) // 2
    NO = DEPTH // 2
    f32 = jnp.float32

    def nrm(k, shape, fan_in):
        return jax.random.normal(k, shape, f32) * (fan_in ** -0.5)

    def gain(k, shape):
        return 1.0 + 0.02 * jax.random.normal(k, shape, f32)

    return {
        "x": jax.random.normal(ks[0], (BATCH, SEQ, D_MODEL), f32),
        "norm_mix_e": gain(ks[1], (NE, D_MODEL)),
        "w_in_e": nrm(ks[2], (NE, D_MODEL, EVEN_IN), D_MODEL),
        "b_forget": 2.0 + 0.5 * jax.random.normal(ks[3], (NE, N_A), f32),
        "sink_logits": 0.5 * jax.random.normal(ks[4], (NE, N_B), f32),
        "w_out_e": nrm(ks[5], (NE, EVEN_OUT, D_MODEL), EVEN_OUT),
        "norm_mix_o": gain(ks[6], (NO, D_MODEL)),
        "w_in_o": nrm(ks[7], (NO, D_MODEL, ODD_IN), D_MODEL),
        "norm_cq": gain(ks[8], (NO, Q_LORA)),
        "norm_ckv": gain(ks[9], (NO, KV_LORA)),
        "w_uq": nrm(ks[10], (NO, Q_LORA, N_D * (QK_NOPE + QK_ROPE)), Q_LORA),
        "w_ukv": nrm(ks[11], (NO, KV_LORA, N_D * (QK_NOPE + V_DIM)), KV_LORA),
        "w_out_o": nrm(ks[12], (NO, ODD_OUT, D_MODEL), ODD_OUT),
        "norm_mlp": gain(ks[13], (DEPTH, D_MODEL)),
        "w_mlp1": nrm(ks[14], (DEPTH, D_MODEL, D_FF), D_MODEL),
        "w_mlp2": nrm(ks[15], (DEPTH, D_FF, D_MODEL), D_FF),
        "rel_bias": 0.5 * jax.random.normal(ks[16], (REL_BUCKETS, REL_SLOTS), f32),
        "norm_final": gain(ks[17], (D_MODEL,)),
    }

def reference(x, norm_mix_e, w_in_e, b_forget, sink_logits, w_out_e,
              norm_mix_o, w_in_o, norm_cq, norm_ckv, w_uq, w_ukv, w_out_o,
              norm_mlp, w_mlp1, w_mlp2, rel_bias, norm_final):
    S = x.shape[1]
    topk = min(TOPK_MAX, S // 4)
    for i in range(DEPTH):
        if i % 2 == 0:
            e = i // 2
            x = x + _even_mixer(_rmsnorm(x, norm_mix_e[e]), w_in_e[e], b_forget[e],
                                sink_logits[e], w_out_e[e], rel_bias)
        else:
            o = i // 2
            x = x + _odd_mixer(_rmsnorm(x, norm_mix_o[o]), w_in_o[o], norm_cq[o], norm_ckv[o],
                               w_uq[o], w_ukv[o], w_out_o[o], rel_bias, topk)
        x = x + _mlp(_rmsnorm(x, norm_mlp[i]), w_mlp1[i], w_mlp2[i])
    return _rmsnorm(x, norm_final)


_drawn_inputs = setup_inputs


def setup_inputs(seed=0):
    import zlib

    import numpy as np

    out = dict(_drawn_inputs(seed))
    spreads = {}
    factors = {'norm_mix_e': 4.436,
     'sink_logits': 8.0,
     'norm_mix_o': 5.97,
     'norm_cq': 8.0,
     'norm_ckv': 8.0,
     'norm_final': 2.868}
    for name, (base, spread) in spreads.items():
        noise = np.random.default_rng([zlib.crc32(name.encode()), seed]).standard_normal(out[name].shape)
        drawn = base * np.exp(spread * noise) if base else spread * noise
        out[name] = __import__('jax').numpy.asarray(drawn.astype(out[name].dtype))
    for name, factor in factors.items():
        out[name] = (out[name] * factor).astype(out[name].dtype)
    return out
```

```python
from contextlib import ExitStack

import numpy as np

import concourse.bass as bass
from concourse import mybir

F32 = mybir.dt.float32
F32R = mybir.dt.float32r
BF16 = mybir.dt.bfloat16
ALU = mybir.AluOpType
ACT = mybir.ActivationFunctionType
AX = mybir.AxisListType

P = 128
D = 1024
KT = D // P
S = 512
NQ = S // P
DFF = 4 * D
GROUPS = DFF // D
EPS = 1e-6
NEG = -1e30
TAKEN = -3e38
HD = 64
NH = 8
W = 128
N_IDX, D_IDX = 8, 32
TOPK = min(256, S // 4)
ROUNDS = TOPK // 8
EARLY_ROUNDS = 12
ROPE = 32
Q_LORA, KV_LORA = 256, 128
BUCKETS, MAX_EXACT, MAX_DIST = 32, 16, 128
EVEN_IN, ODD_IN = 2312, 1352
C_LEN, B_LEN = S + P - 1, 2 * W + P - 1


def shape_constants():
    def bucket(n):
        nf = np.float32(max(n, MAX_EXACT)) / np.float32(MAX_EXACT)
        large = MAX_EXACT + int(np.float32(np.log(nf)) / np.float32(np.log(MAX_DIST / MAX_EXACT))
                                * np.float32(BUCKETS - MAX_EXACT))
        return n if n < MAX_EXACT else min(large, BUCKETS - 1)

    onehot = np.zeros((BUCKETS + 1, 1024), np.float32)
    for i in range(C_LEN):
        dist = S - 1 - i
        onehot[bucket(dist) if dist >= 0 else BUCKETS, i] = 1
    for i in range(B_LEN):
        dist = 2 * W - 1 - i
        onehot[bucket(dist) if 0 <= dist < W else BUCKETS, C_LEN + i] = 1
    ident = np.eye(P, dtype=np.float32)
    hot = np.zeros((P, NH), np.float32)
    for q in range(4):
        hot[32 * q:32 * q + NH] = np.eye(NH)
    pos = np.arange(S, dtype=np.float32)
    inv = (np.float32(10000.0) ** (-np.arange(0, ROPE, 2, dtype=np.float32) / np.float32(ROPE))).astype(np.float32)
    ang = inv[:, None] * pos[None, :]
    cos, sin = np.cos(ang).astype(np.float32), np.sin(ang).astype(np.float32)
    rope = np.zeros((P, S), np.float32)
    rope[0:64] = 1
    rope[64:96] = np.concatenate([cos, cos])
    rope[96:128] = np.concatenate([-sin, sin])
    causal = np.where(np.arange(P)[None, :] <= np.arange(P)[:, None], 0, NEG).astype(np.float32)
    fixed = np.concatenate([ident, hot, ident[::-1], causal], axis=1)
    return {"c_onehot": onehot, "c_fixed": np.ascontiguousarray(fixed), "c_rope": rope}


N_CONST = 14
NORMS = ("mix_e", "mlp0", "mix_o", "cq", "ckv", "mlp1", "final")
NORM_TILES = (KT, KT, KT, 2, 1, KT, KT)
SQ_BEFORE = {k: sum(NORM_TILES[:i]) for i, k in enumerate(NORMS)}
ADD_BEFORE = {k: sum(NORM_TILES[:i]) - i for i, k in enumerate(NORMS)}
XG_BEFORE = {"mix_e": 0, "mlp0": KT, "mix_o": 2 * KT, "mlp1": 3 * KT, "final": 4 * KT}


def slab_plan():
    even = [("fa", 1536)] + [(f"ka{i}", 512 + P * i) for i in range(4)] + [(f"qa{i}", P * i) for i in range(4)] \
        + [(f"va{i}", 1024 + P * i) for i in range(4)] + [("kb", 2056), ("vb", 2184)] \
        + [(f"qb{i}", 1544 + P * i) for i in range(4)]
    odd = [("nar", 896), ("qi0", 640), ("qi1", 768), ("kv", 512), ("cq0", 936), ("cq1", 1064), ("ckv", 1192)] \
        + [(f"qc{i}", P * i) for i in range(4)]
    return even, odd


EVEN, ODD = slab_plan()
N_IN0 = 0
N_OUT0 = N_IN0 + len(EVEN)
N_MLP0 = N_OUT0 + KT
N_IN1 = N_MLP0 + 2 * KT * GROUPS
N_OUT1 = N_IN1 + len(ODD)
N_MLP1 = N_OUT1 + KT
N_END = N_MLP1 + 2 * KT * GROUPS
NAR = N_IN1

GAIN = {"mix_e": 0, "mlp0": 8, "mix_o": 16, "mlp1": 24, "final": 32, "cq": 40, "ckv": 42}
N_GAIN = 43


def trunk(nc, x, norm_mix_e, w_in_e, b_forget, sink_logits, w_out_e, norm_mix_o, w_in_o, norm_cq, norm_ckv,
          w_uq, w_ukv, w_out_o, norm_mlp, w_mlp1, w_mlp2, rel_bias, norm_final,
          c_onehot, c_fixed, c_rope, out):
    with ExitStack() as ctx:
        def sb(name, shape, dt=F32):
            return ctx.enter_context(nc.sbuf_tensor(name, shape, dt))

        def sem(name):
            return ctx.enter_context(nc.semaphore(name))

        bank = [ctx.enter_context(nc.psum_tensor(f"bank{i}", [P, 512], F32)) for i in range(8)]
        bias_rows = nc.dram_tensor("bias_rows", (2 * NH, 1024), F32, kind="Internal").ap()

        xT = sb("xT", [P, KT, S])
        xh = sb("xh", [P, KT, S], F32R)
        xl = sb("xl", [P, KT, S], F32R)
        raw = sb("raw", [P, 2, 1024])
        wh = sb("wh", [P, 2, 1024], F32R)
        wl = sb("wl", [P, 2, 1024], F32R)
        rstd = sb("rstd", [P, S])
        rstd_q = sb("rstd_q", [P, S])
        rstd_k = sb("rstd_k", [P, S])
        sqsum = sb("sqsum", [P, S])
        sq = sb("sq", [P, 2, S])
        tbuf = sb("tbuf", [P, 2, S])
        probs = sb("probs", [P, 2, 1280])
        probT_h = sb("probT_h", [P, 1280], F32R)
        probT_l = sb("probT_l", [P, 1280], F32R)
        strip_raw = sb("strip_raw", [P, 2, S])
        strip_h = sb("strip_h", [P, 2, S], F32R)
        strip_l = sb("strip_l", [P, 2, S], F32R)
        rope = sb("rope", [P, S])
        ident_b = sb("ident_b", [P, P], BF16)
        flip_r = sb("flip_r", [P, P], F32R)
        ones = sb("ones", [P, P])
        fixed = sb("fixed", [P, P + NH])
        ident = fixed[:, 0:P]
        hot = fixed[:, P:P + NH]
        gain = sb("gain", [P, N_GAIN])
        sinks = sb("sinks", [P, NH, 2])
        sink_in = sb("sink_in", [P, NH])
        bfor = sb("bfor", [NH, 1])
        negmax = sb("negmax", [P, 2, 4])
        expsum = sb("expsum", [P, 2, 4])
        rsum = sb("rsum", [P, 2, 4])
        widx = sb("widx", [P, NQ, N_IDX])
        best8 = sb("best8", [P, 3, 8])
        fin = sb("fin", [P, 4, NQ])
        causal = sb("causal", [P, P], BF16)
        score = sb("score", [P, 1152])
        mask_c = sb("mask_c", [P, 1152], BF16)
        USIZE = 19456
        ur = sb("ur", [P, USIZE], F32R)

        at = [0]

        def take(words):
            at[0] += words
            assert at[0] <= USIZE, at[0]
            return ur[:, at[0] - words:at[0]]

        def tiles(n, w=S):
            return take(n * w).rearrange("p (n w) -> p n w", n=n)

        qa = (tiles(4), tiles(4))
        ka = (tiles(4), tiles(4))
        va = (tiles(NQ), tiles(NQ))
        kb = (tiles(2), tiles(2))
        vb = (tiles(2), tiles(2))
        fl = take(S)
        gb = take(S)
        gf = tiles(2)
        qb = (xh[:, 4:8, :], xl[:, 4:8, :])
        at[0] = 0
        hid = (tiles(KT), tiles(KT))
        at[0] = 0
        wuq = (tiles(2, 1024), tiles(2, 1024))
        wuk = (take(512), take(512))
        wuv = (take(512), take(512))
        cq = (tiles(2), tiles(2))
        ckv = (take(S), take(S))
        qd = (tiles(2), tiles(2))
        kd = (tiles(2), tiles(2))
        vd = (tiles(NQ), tiles(NQ))
        kc = (take(S), take(S))
        vc = (tiles(NQ, P), tiles(NQ, P))
        qc = (xh[:, 0:4, :], xl[:, 0:4, :])
        qi = (qd[0], qd[1])
        ki = (kd[0][:, 0, :], kd[1][:, 0, :])
        kr = (kd[0][64:96, :, :], kd[1][64:96, :, :])

        relu = probs[:, 1, 0:1152]
        SC = {1: (0, 256), 2: (256, 384), 3: (640, 512)}
        praw = probs[:, :, :].rearrange("p a b -> p (a b)")
        uq_raw = praw[:, 0:1536].rearrange("p (k n) -> p k n", k=2)
        ukv_raw = praw[:, 1536:2560]
        x_tok = praw[:, 0:2048].rearrange("p (a n) -> p a n", a=2)
        otok = praw[:, 0:2048].rearrange("p (a n) -> p a n", a=2)
        onehot = strip_raw[0:BUCKETS + 1, :, :].rearrange("p a b -> p (a b)")
        bias_out = strip_raw[0:2 * NH, :, :].rearrange("p a b -> p (a b)")
        g_rows = rstd_q[0:N_GAIN, 0:P]
        table = rstd_q[0:BUCKETS + 1, P:P + 2 * NH]
        w_scaled = rstd_q[0:N_IDX, :]
        kr32 = strip_raw[64:96, 1, :]

        raw_loaded = [sem("raw_loaded0"), sem("raw_loaded1")]
        consts_loaded = sem("consts_loaded")
        x_loaded = [sem("x_loaded0"), sem("x_loaded1")]
        x_turned = sem("x_turned")
        x_copied = sem("x_copied")
        gains_turned = sem("gains_turned")
        bias_made = sem("bias_made")
        setup_act = sem("setup_act")
        memsets_done = sem("memsets_done")
        bias_copied = sem("bias_copied")
        bias_stored = sem("bias_stored")
        w_hi = sem("w_hi")
        w_lo = sem("w_lo")
        slab_done = sem("slab_done")
        slab_taken = sem("slab_taken")
        p_hi = sem("p_hi")
        p_lo = sem("p_lo")
        vt_ready = sem("vt_ready")
        xg_hi = sem("xg_hi")
        xg_lo = sem("xg_lo")
        sq_ready = sem("sq_ready")
        sq_added = sem("sq_added")
        sum_ready = sem("sum_ready")
        rec_ready = sem("rec_ready")
        root_ready = sem("root_ready")
        diag_ready = sem("diag_ready")
        spread_done = sem("spread_done")
        norm_ready = sem("norm_ready")
        h32 = sem("h32")
        h_hi = sem("h_hi")
        h_lo = sem("h_lo")
        step_v = sem("step_v")
        step_a = sem("step_a")
        fg_in = sem("fg_in")
        fg_out = sem("fg_out")
        scores_ready = sem("scores_ready")
        max_ready = sem("max_ready")
        exp_done = sem("exp_done")
        rsum_ready = sem("rsum_ready")
        probs_ready = sem("probs_ready")
        pt_ready = sem("pt_ready")
        pt_hi = sem("pt_hi")
        pt_lo = sem("pt_lo")
        o_ready = sem("o_ready")
        o_hi = sem("o_hi")
        o_lo = sem("o_lo")
        strip_loaded = [sem("strip_loaded0"), sem("strip_loaded1")]
        sink_set = sem("sink_set")
        strip_hi_ready = sem("strip_hi_ready")
        prep_ready = sem("prep_ready")
        low_loaded = sem("low_loaded")
        low_hi = sem("low_hi")
        low_lo = sem("low_lo")
        wi_scaled = sem("wi_scaled")
        wi_turned = sem("wi_turned")
        widx_ready = sem("widx_ready")
        idx_ready = sem("idx_ready")
        relu_ready = sem("relu_ready")
        idx_added = sem("idx_added")
        causal_cut = sem("causal_cut")
        mask_ready = sem("mask_ready")
        dv_ready = sem("dv_ready")
        dv_taken = sem("dv_taken")
        dvt_ready = sem("dvt_ready")
        dv_hi = sem("dv_hi")
        dv_lo = sem("dv_lo")
        dq_ready = sem("dq_ready")
        dq_taken = sem("dq_taken")
        dq_t = sem("dq_t")
        dq_hi = sem("dq_hi")
        dq_lo = sem("dq_lo")
        fin_turned = sem("fin_turned")
        fin_v = sem("fin_v")
        fin_a = sem("fin_a")
        fin_ready = sem("fin_ready")
        kr_rotated = sem("kr_rotated")
        kr_hi = sem("kr_hi")
        kr_ready = sem("kr_ready")
        out_stored = [sem("out_stored0"), sem("out_stored1")]

        class Steps:

            def __init__(self, eng, s):
                self.eng, self.s, self.n = eng, s, 0

            def done(self, ins):
                ins.then_inc(self.s, 1)
                self.n += 1
                return self.n

            def wait(self, n=None):
                self.eng.wait_ge(self.s, self.n if n is None else n)

            def link(self, ins):
                self.done(ins)
                self.wait()

        def weights_of(n):
            def block(w, col, width=P, row=0, rows=D):
                return w[row:row + rows, col:col + width].rearrange("(k p) n -> p k n", p=P)
            if n < N_OUT0:
                name, col = EVEN[n]
                return block(w_in_e[0], col, NH if name == "fa" else P)
            if n < N_MLP0:
                return block(w_out_e[0], P * (n - N_OUT0))
            if N_IN1 <= n < N_OUT1:
                return block(w_in_o[0], ODD[n - N_IN1][1])
            return block(w_out_o[0], P * (n - N_OUT1))

        def raw_count(n):
            extra = 48 if n >= NAR and n % 2 == NAR % 2 else 0
            return 16 * (n // 2 + 1) + extra

        def pj(n):
            return bank[4 + n % 4]

        norms = []

        def units(j):
            if attention(j) == "B":
                return [(0, 0, 0, 130, 0), (1, 0, 130, 258, 130), (2, 1, 0, 258, 388), (3, 2, 0, 258, 646)]
            return [(0, 0, 0, 128, 0), (2, 0, 128, 384, 128), (1, 1, 0, 256, 512), (3, 2, 0, 512, 768)]

        def unit_of(j, blk):
            return [u for u in units(j) if u[0] == blk][0]

        def attention(j):
            return "ABDC"[j // NH]

        def pt_parts(j):
            if attention(j) == "B":
                return [(0, 3, 0, 0, 256), (1, 3, 256, 128, 256), (2, 4, 0, 256, 256), (3, 4, 256, 384, 128)]
            return [(0, 3, 0, 0, 512), (1, 4, 0, 128, 384), (3, 4, 384, 384, 128), (2, 5, 0, 256, 256)]

        def pt_banks(j):
            return [(3, 512), (4, 384)] if attention(j) == "B" else [(3, 512), (4, 512), (5, 256)]

        PT_COL = {3: 0, 4: 512, 5: 1024}

        def pt_before(j):
            return sum(len(pt_banks(i)) for i in range(j))

        def out_tile(j):
            h = j % NH
            return {"A": 0, "B": 4, "C": 0, "D": 4}[attention(j)] + h // 2, 64 * (h % 2)

        def strip_count(j):
            return sum(1 for i in range(j + 1) if attention(i) in "BC" and i % 2 == j % 2)

        def t5_rank(j):
            return sum(1 for i in range(j) if attention(i) in "BC")

        def prep_rank(j):
            return sum(1 for i in range(j) if attention(i) in "ABC")

        def head_steps(first, last):
            return range(first - (4 if attention(first) == "D" else 3), last)

        def latent(first, j):
            return first == 2 * NH <= j < 3 * NH

        block = ctx.enter_context(nc.Block())

        @block.sync
        def _(sp):
            def load_slab(n, src=None):
                if n >= 2:
                    sp.wait_ge(w_hi, n - 1)
                    sp.wait_ge(w_lo, n - 1)
                if n == NAR:
                    w = w_in_o[0]
                    dst = raw[:, n % 2, :].rearrange("p (k n) -> p k n", k=KT)
                    for c0, c1, d0 in ((896, 960, 0), (1320, 1352, 64), (1336, 1352, 96), (1320, 1336, 112)):
                        sp.dma_start(dst[:, :, d0:d0 + c1 - c0],
                                     w[:, c0:c1].rearrange("(k p) n -> p k n", p=P)).then_inc(raw_loaded[n % 2], 16)
                    return
                src = weights_of(n)
                width = src.shape[2]
                dst = raw[:, n % 2, 0:KT * width].rearrange("p (k n) -> p k n", k=KT)
                sp.dma_start(dst, src).then_inc(raw_loaded[n % 2], 16)

            def load_mlp_group(layer, n0, g):
                base = n0 + 16 * g
                w1 = w_mlp1[layer].rearrange("(k p) n -> p k n", p=P)
                w2 = w_mlp2[layer].rearrange("(g k p) n -> p g k n", p=P, k=KT)
                for s in range(2 * KT):
                    sp.wait_ge(w_hi, base + (s - 1))
                    sp.wait_ge(w_lo, base + (s - 1))
                    slot = (n0 + s) % 2
                    dst = raw[:, slot, :].rearrange("p (k n) -> p k n", k=KT)
                    if s < KT:
                        src = w1[:, :, bass.ds(g * D + P * s, P)]
                    else:
                        src = w2[:, bass.ds(g, 1), :, P * (s - KT):P * (s - KT + 1)]
                        dst = raw[:, slot, :].rearrange("p (o k n) -> p o k n", k=KT, o=1)
                    sp.dma_start(dst, src).then_inc(raw_loaded[slot], 16)

            def load_mlp(layer, n0):
                with sp.Fori(0, GROUPS) as g:
                    load_mlp_group(layer, n0, g)

            def load_strip(j):
                slot = j % 2
                if attention(j - 2) in "BC":
                    sp.wait_ge(prep_ready, prep_rank(j - 2) + 1)
                if attention(j) == "B":
                    row, off, width, c0 = j % NH, C_LEN, 2 * W, 2
                else:
                    row, off, width, c0 = NH + j % NH, 0, S, 0
                src = bias_rows[row:row + 1, off:off + width + P - 1]
                src = bass.AP(src.tensor, src.offset, [[1, P], [1, width]])
                sp.dma_start(strip_raw[:, slot, c0:c0 + width], src).then_inc(strip_loaded[slot], 16)

            sp.dma_start(fixed[:, :], c_fixed[:, 0:P + NH]).then_inc(consts_loaded, 16)
            sp.dma_start(rstd_k[:, 0:2 * P], c_fixed[:, P + NH:3 * P + NH]).then_inc(consts_loaded, 16)
            for a in range(2):
                sp.dma_start(x_tok[:, a, :], x[0, P * a:P * (a + 1), :]).then_inc(x_loaded[a], 16)
            for key, src in (("mix_e", norm_mix_e[0]), ("mlp0", norm_mlp[0]), ("mix_o", norm_mix_o[0]),
                             ("mlp1", norm_mlp[1]), ("final", norm_final), ("cq", norm_cq[0]), ("ckv", norm_ckv[0])):
                rows = src.shape[0] // P
                sp.dma_start(g_rows[GAIN[key]:GAIN[key] + rows, :], src.rearrange("(t p) -> t p", p=P))\
                    .then_inc(consts_loaded, 16)
            load_slab(0)
            load_slab(1)
            sp.dma_start(table[0:BUCKETS, :], rel_bias).then_inc(consts_loaded, 16)
            sp.dma_start(onehot, c_onehot).then_inc(consts_loaded, 16)
            sp.dma_start(rope[:, :], c_rope).then_inc(consts_loaded, 16)
            sp.dma_start(bfor[:, :], b_forget.rearrange("a h -> h a")).then_inc(consts_loaded, 16)
            sp.dma_start(sink_in[:, :], sink_logits.to_broadcast([P, NH])).then_inc(consts_loaded, 16)
            for a in range(2, NQ):
                sp.wait_ge(x_turned, 2 * (a - 1))
                sp.dma_start(x_tok[:, a % 2, :], x[0, P * a:P * (a + 1), :]).then_inc(x_loaded[a % 2], 16)
            sp.wait_ge(bias_copied, 1)
            sp.dma_start(bias_rows, bias_out).then_inc(bias_stored, 16)
            for n in range(2, N_OUT0 + 2):
                load_slab(n)
            sp.wait_ge(bias_stored, 16)
            for j in range(NH, 2 * NH):
                load_strip(j)
            sp.wait_ge(pt_ready, pt_before(2 * NH))
            sp.dma_start(uq_raw, w_uq[0].rearrange("(k p) n -> p k n", p=P)).then_inc(low_loaded, 16)
            sp.dma_start(ukv_raw, w_ukv[0]).then_inc(low_loaded, 16)
            for n in range(N_OUT0 + 2, N_MLP0):
                load_slab(n)
            load_mlp(0, N_MLP0)
            for n in range(N_IN1, N_OUT1 + 2):
                load_slab(n)
            sp.wait_ge(kr_ready, 1)
            for j in range(3 * NH, 4 * NH):
                load_strip(j)
            for n in range(N_OUT1 + 2, N_MLP1):
                load_slab(n)
            load_mlp(1, N_MLP1)
            for a in range(NQ):
                sp.wait_ge(fin_v, a + 1)
                sp.wait_ge(fin_a, a + 1)
                sp.dma_start(out[0, P * a:P * (a + 1), :], otok[:, a % 2, :]).then_inc(out_stored[a % 2], 16)
            for a in range(2):
                sp.wait_ge(out_stored[a], 32)

        @block.tensor
        def _(pe):
            mm = nc.tensor.matmul

            def product(dst, lhs, rhs, start=True, stop=True, check=True):
                mm(dst, lhs[0], rhs[0], start=start, stop=False, skip_group_check=not check)
                mm(dst, lhs[0], rhs[1], start=False, stop=False, skip_group_check=not check)
                return mm(dst, lhs[1], rhs[0], start=False, stop=stop, skip_group_check=not check)

            def slab(n, slot, dst, acts, tile_wait=None, width=P):
                pe.wait_ge(w_hi, n + 1)
                pe.wait_ge(w_lo, n + 1)
                for k in range(KT):
                    if tile_wait:
                        tile_wait(k)
                    cols = slice(width * k, width * (k + 1))
                    last = product(dst, (wh[:, slot, cols], wl[:, slot, cols]), (acts[0][:, k, :], acts[1][:, k, :]),
                                   start=k == 0, stop=k == KT - 1)
                last.then_inc(slab_done, 1)

            def sum_squares(norm):
                if norm == "ckv":
                    pe.wait_ge(norm_ready, NORMS.index(norm))
                    pe.wait_ge(sq_ready, SQ_BEFORE[norm] + 1)
                else:
                    pe.wait_ge(sq_added, ADD_BEFORE[norm] + NORM_TILES[NORMS.index(norm)] - 1)
                for a in range(NQ):
                    last = mm(bank[0][:, a:a + 1], sqsum[:, P * a:P * (a + 1)], ones[:, 0:1], start=True, stop=True)
                last.then_inc(sum_ready, 1)

            def spread(norm):
                pe.wait_ge(diag_ready, NORMS.index(norm) + 1)
                mm(bank[0][:, :], ones[:, :], sq[:, 0, :], start=True, stop=True).then_inc(spread_done, 1)

            def turn_values(n, b):
                pe.wait_ge(slab_taken, n + 1)
                for a in range(NQ):
                    last = nc.tensor.transpose(bank[b][:, P * a:P * (a + 1)], tbuf[:, n % 2, P * a:P * (a + 1)],
                                               ident[:, :])
                last.then_inc(vt_ready, 1)

            def mlp_group(n0, H0, norm, g):
                base = n0 + 16 * g
                for s in range(2 * KT):
                    n = base + s
                    pe.wait_ge(slab_taken, n - 3)
                    if s < KT:
                        wait = (lambda k: pe.wait_ge(xg_lo, XG_BEFORE[norm] + k + 1)) if s == 0 else None
                        slab(n, (n0 + s) % 2, pj(n0 + s)[:, :], (xh, xl), wait)
                    else:
                        wait = (lambda k: pe.wait_ge(h_lo, 8 * g + (H0 + k + 1))) if s == KT else None
                        slab(n, (n0 + s) % 2, pj(n0 + s)[:, :], hid, wait)
                    if s == 0 and isinstance(g, int):
                        sum_squares(norm)
                    if s == 1 and isinstance(g, int):
                        spread(norm)

            def mlp(n0, H0, norm):
                mlp_group(n0, H0, norm, 0)
                with pe.Fori(1, GROUPS) as g:
                    mlp_group(n0, H0, norm, g)

            def scores(j):
                kind, h, slot = attention(j), j % NH, j % 2
                r = 64 * (h % 2)
                if kind in "ABC":
                    pe.wait_ge(prep_ready, prep_rank(j) + 1)
                if kind == "D":
                    pe.wait_ge(dq_lo, 2 * (h + 1))
                if j == NH:
                    pe.wait_ge(p_lo, len(EVEN))
                if j == 3 * NH:
                    pe.wait_ge(mask_ready, 1)
                if j == 2 * NH:
                    pe.wait_ge(dv_lo, 4)
                for i, (blk, b, col, width, _) in enumerate(units(j)):
                    if i == 0 or units(j)[i - 1][1] != b:
                        if j not in (0, 2 * NH):
                            pe.wait_ge(exp_done, 3 * (j - 1) + b + 1)
                    qs = slice(P * blk, P * (blk + 1))
                    last_in_bank = i + 1 == len(units(j)) or units(j)[i + 1][1] != b
                    if kind == "B":
                        t = h // 2
                        kv = h // 4
                        dst = bank[b][:, col:col + width]
                        c0 = 0 if width == 258 else 128
                        if c0 == 0:
                            mm(dst, flip_r[:, :], strip_h[:, slot, 0:258], start=True, stop=False)
                            mm(dst, flip_r[:, :], strip_l[:, slot, 0:258], start=False, stop=False)
                        else:
                            mm(dst[:, 0:2], flip_r[:, :], strip_h[:, slot, 0:2], start=True, stop=False)
                            mm(dst[:, 0:2], flip_r[:, :], strip_l[:, slot, 0:2], start=False, stop=True)
                            mm(dst[:, 2:130], flip_r[:, :], strip_h[:, slot, 130:258], start=True, stop=False)
                            mm(dst[:, 2:130], flip_r[:, :], strip_l[:, slot, 130:258], start=False, stop=False)
                        k0 = max(blk - 1, 0) * P
                        ks = slice(k0, k0 + width - 2)
                        last = product(dst[:, 2:width], (qb[0][r:r + 64, t, qs], qb[1][r:r + 64, t, qs]),
                                       (kb[0][r:r + 64, kv, ks], kb[1][r:r + 64, kv, ks]), start=False)
                    else:
                        dst = bank[b][:, col:col + width]
                        if kind == "A":
                            t = h // 2
                            mm(dst, fl[:, qs], gf[:, slot, 0:width], start=True, stop=False)
                            product(dst, (qa[0][r:r + 64, t, qs], qa[1][r:r + 64, t, qs]),
                                    (ka[0][r:r + 64, t, 0:width], ka[1][r:r + 64, t, 0:width]), start=False, stop=False)
                            last = mm(dst[:, P * blk:P * (blk + 1)], ident_b[:, :], causal[:, :], start=False, stop=True)
                        elif kind == "D":
                            product(dst, (qd[0][0:96, slot, qs], qd[1][0:96, slot, qs]),
                                    (kd[0][0:96, slot, 0:width], kd[1][0:96, slot, 0:width]), start=True, stop=False)
                            last = mm(dst[:, P * blk:P * (blk + 1)], ident_b[:, :], causal[:, :], start=False, stop=True)
                        else:
                            t = h // 2
                            off = S - width
                            mm(dst, flip_r[:, :], strip_h[:, slot, off:S], start=True, stop=False)
                            mm(dst, flip_r[:, :], strip_l[:, slot, off:S], start=False, stop=False)
                            if blk:
                                c0, w = SC[blk]
                                mm(dst, ident_b[:, :], mask_c[:, c0:c0 + w], start=False, stop=False)
                            last = product(dst, (qc[0][r:r + 64, t, qs], qc[1][r:r + 64, t, qs]),
                                           (kc[0][r:r + 64, 0:width], kc[1][r:r + 64, 0:width]), start=False)
                    if last_in_bank:
                        last.then_inc(scores_ready, 1)

            def turn_probs(j):
                slot = j % 2
                if j == 0:
                    pe.wait_ge(slab_taken, N_OUT0)
                if j == 2 * NH:
                    pe.wait_ge(slab_taken, N_OUT1)
                pe.wait_ge(probs_ready, 4 * (j + 1))
                done = None
                parts = pt_parts(j)
                for i, (kt, b, col, q0, nq) in enumerate(parts):
                    if (i == 0 or parts[i - 1][1] != b):
                        before = [x for x in range(j) if x // (2 * NH) == j // (2 * NH) and any(bb == b for bb, _ in pt_banks(x))]
                        if before:
                            x = before[-1]
                            k = [bb for bb, _ in pt_banks(x)].index(b)
                            pe.wait_ge(pt_lo, pt_before(x) + k + 1)
                    for q in range(q0, q0 + nq, P):
                        blk = q // P
                        _, _, _, width, pcol = unit_of(j, blk)
                        if attention(j) == "B":
                            c = pcol + (2 if kt == blk - 1 or blk == 0 else 130)
                        else:
                            c = pcol + P * kt
                        done = nc.tensor.transpose(bank[b][:, col + q - q0:col + q - q0 + P],
                                                   probs[:, slot, c:c + P], ident[:, :])
                    if i + 1 == len(parts) or parts[i + 1][1] != b:
                        done.then_inc(pt_ready, 1)

            def values(j):
                kind, h = attention(j), j % NH
                if j not in (0, 2 * NH):
                    pe.wait_ge(o_lo, j)
                for i, (kt, b, col, q0, nq) in enumerate(pt_parts(j)):
                    k = [bb for bb, _ in pt_banks(j)].index(b)
                    pe.wait_ge(pt_lo, pt_before(j) + k + 1)
                    pc = PT_COL[b] + col
                    t = h // 2
                    v = {"A": lambda a: va[a][:, kt, P * t:P * (t + 1)],
                         "B": lambda a: vb[a][:, h // 4, P * kt:P * (kt + 1)],
                         "D": lambda a: vd[a][:, kt, P * t:P * (t + 1)],
                         "C": lambda a: vc[a][:, kt, :]}[kind]
                    last = product(bank[6][:, q0:q0 + nq], (v(0), v(1)),
                                   (probT_h[:, pc:pc + nq], probT_l[:, pc:pc + nq]),
                                   start=i == 0, stop=i == 3, check=kind != "B")
                last.then_inc(o_ready, 1)

            def latent_query(h):
                if h:
                    pe.wait_ge(dq_taken, 2 * h)
                for k in range(2):
                    last = product(bank[7][:, :], (wuq[0][:, k, P * h:P * (h + 1)], wuq[1][:, k, P * h:P * (h + 1)]),
                                   (cq[0][:, k, :], cq[1][:, k, :]), start=k == 0, stop=k == 1)
                last.then_inc(dq_ready, 1)

            def latent_key(h):
                pe.wait_ge(dq_taken, 2 * h + 1)
                product(bank[7][0:64, :], (wuk[0][:, HD * h:HD * (h + 1)], wuk[1][:, HD * h:HD * (h + 1)]),
                        ckv).then_inc(dq_ready, 1)

            def heads(first, last):
                for s in head_steps(first, last):
                    if first <= s + 2 < last:
                        scores(s + 2)
                    if latent(first, s + 4):
                        latent_query((s + 4) % NH)
                    if first <= s:
                        values(s)
                    if first <= s + 1 < last:
                        turn_probs(s + 1)
                    if latent(first, s + 4):
                        latent_key((s + 4) % NH)

            def out_projection(n0, first, last):
                for m in range(KT):
                    n = n0 + m
                    if m == 0:
                        pe.wait_ge(pt_lo, pt_before(last))
                        pe.wait_ge(o_lo, last)
                    if m >= 4:
                        pe.wait_ge(slab_taken, n - 3)
                    slab(n, n % 2, pj(n)[:, :], (xh, xl))

            pe.wait_ge(consts_loaded, 16 * N_CONST)
            pe.wait_ge(memsets_done, 1)
            for a in range(NQ):
                pe.wait_ge(x_loaded[a % 2], 16 * (a // 2 + 1))
                for half in range(2):
                    if a >= 2:
                        pe.wait_ge(x_copied, 2 * (a - 2) + half + 1)
                    b = 2 * (a % 2) + half
                    for k in range(4):
                        c = P * (4 * half + k)
                        last = nc.tensor.transpose(bank[b][:, P * k:P * (k + 1)], x_tok[:, a % 2, c:c + P], ident[:, :])
                    last.then_inc(x_turned, 1)
                if a == 1:
                    nc.tensor.transpose(bank[4][:, 0:N_GAIN], g_rows, ident[0:N_GAIN, 0:N_GAIN]).then_inc(gains_turned, 1)
                    for c in range(2):
                        last = mm(bank[5 + c][0:2 * NH, :], table, onehot[:, 512 * c:512 * (c + 1)], start=True, stop=True)
                    last.then_inc(bias_made, 1)

            for n in range(N_OUT0):
                name = EVEN[n][0]
                if n == 0:
                    pe.wait_ge(bias_copied, 1)
                if n >= 4:
                    pe.wait_ge(slab_taken, n - 3)
                width = NH if name == "fa" else P
                dst = pj(n)[0:NH, :] if name == "fa" else pj(n)[:, :]
                slab(n, n % 2, dst, (xh, xl), (lambda k: pe.wait_ge(xg_lo, k + 1)) if n == 0 else None, width)
                if n == 0:
                    sum_squares("mix_e")
                if n == 1:
                    spread("mix_e")
                prev = EVEN[n - 1][0] if n else ""
                if prev in ("va0", "va1", "va2", "va3", "vb"):
                    v = [e[0] for e in EVEN if e[0][0] == "v"].index(prev)
                    if v >= 2:
                        pe.wait_ge(p_lo, n - 2)
                    turn_values(n - 1, 1 + v % 2)
            pe.wait_ge(p_lo, 1)
            pe.wait_ge(p_lo, len(EVEN) - 4)
            heads(0, 16)
            out_projection(N_OUT0, 0, 16)
            mlp(N_MLP0, 0, "mlp0")

            for i in range(3):
                n = N_IN1 + i
                pe.wait_ge(slab_taken, n - 3)
                slab(n, n % 2, pj(n)[:, :], (xh, xl), (lambda k: pe.wait_ge(xg_lo, 2 * KT + k + 1)) if i == 0 else None)
                if i == 0:
                    sum_squares("mix_o")
                if i == 1:
                    spread("mix_o")
            pe.wait_ge(wi_scaled, 1)
            for a in range(NQ):
                last = nc.tensor.transpose(bank[3][:, 8 * a:8 * a + 8], w_scaled[:, P * a:P * (a + 1)],
                                           ident[0:8, 0:8])
            last.then_inc(wi_turned, 1)
            pe.wait_ge(p_lo, len(EVEN) + 3)
            for i in range(N_IDX):
                r = 32 * (i % 4)
                for blk in (1, 2, 3):
                    if i:
                        pe.wait_ge(relu_ready, 3 * (i - 1) + blk)
                    w = SC[blk][1]
                    qs = slice(P * blk, P * (blk + 1))
                    product(bank[blk - 1][:, 0:w], (qi[0][r:r + 32, i // 4, qs], qi[1][r:r + 32, i // 4, qs]),
                            (ki[0][r:r + 32, 0:w], ki[1][r:r + 32, 0:w])).then_inc(idx_ready, 1)
            for i in range(3, len(ODD)):
                n = N_IN1 + i
                pe.wait_ge(slab_taken, n - 3)
                slab(n, n % 2, pj(n)[:, :], (xh, xl))
                if i == 4:
                    pe.wait_ge(widx_ready, 1)
                    turn_values(N_IN1 + 3, 3)
                if i == 6:
                    pe.wait_ge(relu_ready, 3 * N_IDX)
                    sum_squares("cq")
                if i == 7:
                    spread("cq")
                if i == 8:
                    sum_squares("ckv")
                if i == 9:
                    spread("ckv")
            def turn_latent_values(t):
                pe.wait_ge(dv_taken, t + 1)
                if t >= 2:
                    pe.wait_ge(dv_lo, t - 1)
                for a in range(NQ):
                    last = nc.tensor.transpose(bank[3 * (t % 2)][:, P * a:P * (a + 1)],
                                               tbuf[:, t % 2, P * a:P * (a + 1)], ident[:, :])
                last.then_inc(dvt_ready, 1)

            pe.wait_ge(p_lo, len(EVEN) + 7)
            pe.wait_ge(low_lo, 1)
            for t in range(4):
                if t >= 2:
                    pe.wait_ge(dv_taken, t - 1)
                product(bank[1 + t % 2][:, :], (wuv[0][:, P * t:P * (t + 1)], wuv[1][:, P * t:P * (t + 1)]), ckv)\
                    .then_inc(dv_ready, 1)
                if t:
                    turn_latent_values(t - 1)
            turn_latent_values(3)
            heads(16, 32)
            out_projection(N_OUT1, 16, 32)
            mlp(N_MLP1, KT * GROUPS, "mlp1")

            pe.wait_ge(slab_taken, N_END)
            sum_squares("final")
            pe.wait_ge(xg_hi, XG_BEFORE["final"] + KT)
            for a in range(NQ):
                for half in range(2):
                    i = 2 * a + half
                    if i >= 6:
                        pe.wait_ge((fin_v, fin_a)[half], (i - 6) // 2 + 1)
                    for k in range(4):
                        last = nc.tensor.transpose(bank[1 + i % 6][:, P * k:P * (k + 1)],
                                                   xT[:, 4 * half + k, P * a:P * (a + 1)], ident[:, :])
                    last.then_inc(fin_turned, 1)

        @block.scalar
        def _(act):
            def copy(dst, src, scale=1.0):
                return nc.scalar.activation(dst, src, ACT.Copy, scale=scale)

            def split(slot, loaded, free, width=P):
                act.wait_ge(raw_loaded[slot], loaded)
                if free is not None:
                    act.wait_ge(slab_done, free)
                copy(wh[:, slot, 0:KT * width], raw[:, slot, 0:KT * width]).then_inc(w_hi, 1)

            def split_slab(n):
                if n < N_END:
                    split(n % 2, raw_count(n), n - 1 if n >= 2 else None, NH if n == 0 else P)

            def square(norm, m, src, wait=None):
                if wait is not None:
                    act.wait_ge(*wait)
                if m == 0:
                    if NORMS.index(norm):
                        act.wait_ge(sum_ready, NORMS.index(norm))
                    dst = sqsum[:, :]
                else:
                    dst = sq[:, m % 2, :]
                    if m >= 3:
                        act.wait_ge(sq_added, ADD_BEFORE[norm] + m - 2)
                nc.scalar.activation(dst, src, ACT.Square).then_inc(sq_ready, 1)

            def root(norm):
                act.wait_ge(rec_ready, NORMS.index(norm) + 1)
                nc.scalar.activation(fin[:, 2, :], fin[:, 1, :], ACT.Sqrt).then_inc(root_ready, 1)

            def normed_hi(norm, m):
                copy(xh[:, m, :], xT[:, m, :], gain[:, GAIN[norm] + m:GAIN[norm] + m + 1]).then_inc(xg_hi, 1)

            def projected(p, name, n):
                t = tbuf[:, n % 2, :]
                if name[0] == "v":
                    v = [e[0] for e in EVEN if e[0][0] == "v"].index(name)
                    act.wait_ge(vt_ready, v + 1)
                    b = bank[1 + v % 2][:, :].rearrange("p (a c) -> p a c", a=NQ)
                    if name == "vb":
                        for kv in range(2):
                            dst = vb[0][:, kv, :].rearrange("p (a c) -> p a c", a=NQ)
                            for d in range(2):
                                last = copy(dst[:, :, HD * d:HD * (d + 1)], b[:, :, HD * kv:HD * (kv + 1)])
                    else:
                        i = int(name[2])
                        last = copy(va[0][:, :, P * i:P * (i + 1)], b)
                    last.then_inc(p_hi, 1)
                    return
                act.wait_ge(slab_taken, n + 1)
                if name == "fa":
                    forget_gate(p)
                elif name == "kb":
                    for kv in range(2):
                        for d in range(2):
                            last = copy(kb[0][HD * d:HD * (d + 1), kv, :], t[HD * kv:HD * (kv + 1), :])
                    last.then_inc(p_hi, 1)
                elif name == "nar":
                    copy(w_scaled, t[32:32 + N_IDX, :], float(N_IDX ** -0.5)).then_inc(wi_scaled, 1)
                    for r in range(0, P, 32):
                        last = copy(ki[0][r:r + 32, :], t[0:32, :])
                    last.then_inc(p_hi, 1)
                elif name == "kv":
                    for d in range(2):
                        copy(kc[0][HD * d:HD * (d + 1), :], t[0:HD, :])
                    act.wait_ge(vt_ready, 6)
                    b = bank[3][:, :].rearrange("p (a c) -> p a c", a=NQ)
                    for d in range(2):
                        last = copy(vc[0][:, :, HD * d:HD * (d + 1)], b[:, :, HD:P])
                    last.then_inc(p_hi, 1)
                elif name[0:2] == "cq" or name == "ckv":
                    norm = name[0:2] if name[0:2] == "cq" else name
                    m = int(name[2]) if norm == "cq" else 0
                    square(norm, m, t)
                    g = GAIN[norm] + m
                    copy(cq[0][:, m, :] if norm == "cq" else ckv[0], t, gain[:, g:g + 1]).then_inc(p_hi, 1)
                else:
                    i = int(name[2])
                    dst = {"ka": ka, "qa": qa, "qb": qb, "qc": qc, "qi": qi}[name[0:2]][0][:, i, :]
                    copy(dst, t).then_inc(p_hi, 1)

            def forget_gate(p):
                t0, s0, s1 = tbuf[0:NH, 0, :], sq[0:NH, 0, :], sq[0:NH, 1, :]
                act.wait_ge(fg_in, 1)
                nc.scalar.activation(s1, s0, ACT.Exp).then_inc(fg_out, 1)
                act.wait_ge(fg_in, 2)
                nc.scalar.activation(s1, s0, ACT.Ln).then_inc(fg_out, 1)
                act.wait_ge(fg_in, 3)
                copy(fl[0:NH, :], rstd_q[0:NH, :]).then_inc(p_hi, 1)

            def hidden(n, slot, H):
                act.wait_ge(h32, H + 1)
                copy(hid[0][:, slot, :], sq[:, slot % 2, :]).then_inc(h_hi, 1)

            def mlp_group(n0, H0, g, norm=None):
                for s in range(2 * KT):
                    n = 16 * g + (n0 + s)
                    if not isinstance(g, int) or n + 2 < N_END:
                        split((n0 + s) % 2, raw_count(n + 2) if isinstance(g, int) else 128 * g + raw_count(n0 + s + 2),
                              n + 1)
                    if s < KT:
                        hidden(n, s, 8 * g + (H0 + s))
                    elif norm:
                        m = s - KT
                        square(norm, m, xT[:, m, :], (slab_taken, n + 1))
                        if norm == "final":
                            copy(xT[:, m, :], xT[:, m, :], gain[:, GAIN[norm] + m:GAIN[norm] + m + 1]).then_inc(xg_hi, 1)
                        else:
                            normed_hi(norm, m)

            def mlp(n0, H0, norm, following):
                root(norm)
                with act.Fori(0, GROUPS - 1) as g:
                    mlp_group(n0, H0, g)
                mlp_group(n0, H0, GROUPS - 1, following)

            def strip(j):
                slot = j % 2
                width = 258 if attention(j) == "B" else S
                act.wait_ge(strip_loaded[slot], 16 * strip_count(j))
                if attention(j) == "B":
                    act.wait_ge(sink_set, j % NH + 1)
                if attention(j - 2) in "BC":
                    act.wait_ge(scores_ready, 3 * (j - 1))
                copy(strip_h[:, slot, 0:width], strip_raw[:, slot, 0:width]).then_inc(strip_hi_ready, 1)

            def heads(first, last):
                for s in head_steps(first, last):
                    if first <= s + 3 < last and attention(s + 3) in "BC":
                        strip(s + 3)
                    if first <= s:
                        for k, (b, w) in enumerate(pt_banks(s)):
                            act.wait_ge(pt_ready, pt_before(s) + k + 1)
                            if k == 0 and s:
                                act.wait_ge(o_ready, s)
                            copy(probT_h[:, PT_COL[b]:PT_COL[b] + w], bank[b][:, 0:w]).then_inc(pt_hi, 1)
                    if latent(first, s + 3):
                        h, slot = (s + 3) % NH, (s + 3) % 2
                        act.wait_ge(dq_t, h + 1)
                        copy(qd[0][0:96, slot, :], tbuf[0:96, 0, :]).then_inc(dq_hi, 1)
                        act.wait_ge(dq_taken, 2 * h + 2)
                        copy(kd[0][0:HD, slot, :], tbuf[0:HD, 1, :]).then_inc(dq_hi, 1)
                    if first <= s + 2 < last:
                        j = s + 2
                        slot = j % 2
                        if j >= 2:
                            act.wait_ge(pt_ready, pt_before(j - 1))
                        us = units(j)
                        for i, (blk, b, col, w, pc) in enumerate(us):
                            act.wait_ge(max_ready, 3 * j + b + 1)
                            e = nc.scalar.activation(probs[:, slot, pc:pc + w], bank[b][:, col:col + w], ACT.Exp,
                                                     bias=negmax[:, slot, blk:blk + 1],
                                                     accum_out=expsum[:, slot, blk:blk + 1])
                            if i + 1 == len(us) or us[i + 1][1] != b:
                                e.then_inc(exp_done, 1)
                    if first <= s:
                        tile, r = out_tile(s)
                        act.wait_ge(o_ready, s + 1)
                        copy(xh[r:r + HD, tile, :], bank[6][r:r + HD, :]).then_inc(o_hi, 1)

            def out_projection(n0, norm):
                for m in range(KT):
                    n = n0 + m
                    act.wait_ge(slab_done, n + 1)
                    split_slab(n + 2)
                    square(norm, m, xT[:, m, :], (slab_taken, n + 1))
                for m in range(KT):
                    normed_hi(norm, m)

            act.wait_ge(consts_loaded, 16 * N_CONST)
            act.wait_ge(memsets_done, 1)
            copy(sinks[:, :, 0], sink_in[:, :])
            copy(ident_b[:, :], ident)
            copy(flip_r[:, :], rstd_k[:, 0:P])
            copy(causal[:, :], rstd_k[:, P:2 * P])
            for a in range(2):
                for half in range(2):
                    act.wait_ge(x_turned, 2 * a + half + 1)
                    copy(xT[:, 4 * half:4 * half + 4, P * a:P * (a + 1)],
                         bank[2 * (a % 2) + half][:, :].rearrange("p (k c) -> p k c", k=4)).then_inc(x_copied, 1)
            act.wait_ge(gains_turned, 1)
            copy(gain[:, :], bank[4][:, 0:N_GAIN]).then_inc(setup_act, 1)
            act.wait_ge(bias_made, 1)
            for c in range(2):
                last = copy(bias_out[:, 512 * c:512 * (c + 1)], bank[5 + c][0:2 * NH, :])
            last.then_inc(bias_copied, 1)
            for a in range(2, NQ):
                for half in range(2):
                    act.wait_ge(x_turned, 2 * a + half + 1)
                    copy(xT[:, 4 * half:4 * half + 4, P * a:P * (a + 1)],
                         bank[2 * (a % 2) + half][:, :].rearrange("p (k c) -> p k c", k=4)).then_inc(x_copied, 1)
            split_slab(0)
            split_slab(1)
            act.wait_ge(x_copied, 2 * NQ)
            act.wait_ge(setup_act, 1)
            for m in range(KT):
                normed_hi("mix_e", m)
                square("mix_e", m, xT[:, m, :])

            root("mix_e")
            for n in range(N_OUT0):
                split_slab(n + 2)
                if 0 < n <= len(EVEN) - 4:
                    projected(n - 1, EVEN[n - 1][0], n - 1)
            for n in range(N_OUT0 - 4, N_OUT0):
                projected(n, EVEN[n][0], n)
            heads(0, 2 * NH)
            out_projection(N_OUT0, "mlp0")
            mlp(N_MLP0, 0, "mlp0", "mix_o")

            p0 = len(EVEN)
            root("mix_o")
            split_slab(N_IN1 + 2)
            split_slab(N_IN1 + 3)
            projected(p0, "nar", N_IN1)
            uq4 = [uq_raw[:, k, :].rearrange("p (h c) -> p h c", c=96) for k in range(2)]
            wq4 = [wuq[0][:, k, :].rearrange("p (h c) -> p h c", c=P) for k in range(2)]
            kv3 = ukv_raw.rearrange("p (h c) -> p h c", c=P)
            act.wait_ge(low_loaded, 32)
            for k in range(2):
                copy(wq4[k][:, :, 0:96], uq4[k])
                copy(wq4[k][:, :, 96:112], uq4[k][:, :, 80:96])
                copy(wq4[k][:, :, 112:128], uq4[k][:, :, 64:80])
            copy(wuk[0].rearrange("p (h c) -> p h c", c=HD), kv3[:, :, 0:HD])
            copy(wuv[0].rearrange("p (h c) -> p h c", c=HD), kv3[:, :, HD:P]).then_inc(low_hi, 1)
            projected(p0 + 1, "qi0", N_IN1 + 1)
            split_slab(N_IN1 + 4)
            projected(p0 + 2, "qi1", N_IN1 + 2)
            for i in range(N_IDX):
                for blk in (1, 2, 3):
                    c0, w = SC[blk]
                    act.wait_ge(idx_ready, 3 * i + blk)
                    if i:
                        act.wait_ge(idx_added, 3 * (i - 1) + blk)
                    else:
                        act.wait_ge(low_lo, 1)
                    nc.scalar.activation(relu[:, c0:c0 + w], bank[blk - 1][:, 0:w], ACT.Relu,
                                         scale=float(D_IDX ** -0.5)).then_inc(relu_ready, 1)
            act.wait_ge(kr_rotated, 1)
            for slot in range(2):
                last = copy(kr[0][:, slot, :], kr32)
            last.then_inc(kr_hi, 1)
            for i in range(3, len(ODD)):
                n = N_IN1 + i
                split_slab(n + 2)
                if 3 < i <= 7:
                    projected(p0 + i - 1, ODD[i - 1][0], n - 1)
                if i == 7:
                    root("cq")
                if i == 9:
                    root("ckv")
            for i in range(7, len(ODD)):
                projected(p0 + i, ODD[i][0], N_IN1 + i)
            for t in range(4):
                act.wait_ge(dvt_ready, t + 1)
                copy(vd[0][:, :, P * t:P * (t + 1)],
                     bank[3 * (t % 2)][:, :].rearrange("p (a c) -> p a c", a=NQ)).then_inc(dv_hi, 1)
            heads(2 * NH, 4 * NH)
            out_projection(N_OUT1, "mlp1")
            mlp(N_MLP1, KT * GROUPS, "mlp1", "final")

            root("final")
            act.wait_ge(fin_ready, 1)
            for a in range(NQ):
                act.wait_ge(fin_turned, 2 * a + 2)
                if a >= 2:
                    act.wait_ge(out_stored[a % 2], 16)
                copy(otok[:, a % 2, 512:1024], bank[1 + (2 * a + 1) % 6][:, :], fin[:, 3, a:a + 1]).then_inc(fin_a, 1)

        @block.gpsimd
        def _(pool):
            def sub(dst, a, b):
                return nc.gpsimd.tensor_tensor(dst, a, b, ALU.subtract)

            def split(slot, n, width=P):
                pool.wait_ge(w_hi, n + 1)
                c = slice(0, KT * width)
                sub(wl[:, slot, c], raw[:, slot, c], wh[:, slot, c].bitcast(F32)).then_inc(w_lo, 1)

            def mlp(n0):
                with pool.Fori(0, GROUPS) as g:
                    for s in range(2 * KT):
                        split((n0 + s) % 2, 16 * g + (n0 + s))

            def prepare(j):
                slot, h = j % 2, j % NH
                if attention(j) == "A":
                    if j == 0:
                        pool.wait_ge(p_lo, 1)
                    if j >= 2:
                        pool.wait_ge(scores_ready, 3 * (j - 1))
                    nc.gpsimd.tensor_scalar(gf[:, slot, :], gb.bitcast(F32), hot[:, h:h + 1], None, ALU.mult)\
                        .then_inc(prep_ready, 1)
                elif attention(j) in "BC":
                    width = S
                    if attention(j) == "B":
                        width = 258
                        if h >= 2:
                            pool.wait_ge(prep_ready, prep_rank(j - 2) + 1)
                        nc.gpsimd.tensor_copy(strip_raw[:, slot, 0:2], sinks[:, h, :]).then_inc(sink_set, 1)
                    pool.wait_ge(strip_hi_ready, t5_rank(j) + 1)
                    sub(strip_l[:, slot, 0:width], strip_raw[:, slot, 0:width],
                        strip_h[:, slot, 0:width].bitcast(F32)).then_inc(prep_ready, 1)

            def heads(first, last):
                for s in head_steps(first, last):
                    if first <= s + 3 < last:
                        prepare(s + 3)
                    if latent(first, s + 3):
                        split_latent(s + 3)
                    if latent(first, s + 4):
                        rotate_latent(s + 4)

            def rotate_latent(j):
                h = j % NH
                if h:
                    pool.wait_ge(dq_lo, 2 * h)
                else:
                    pool.wait_ge(w_lo, N_OUT1 + 2)
                pool.wait_ge(dq_taken, 2 * h + 1)
                nc.gpsimd.tensor_tensor(tbuf[64:96, 0, :], tbuf[64:96, 0, :], sq[64:96, 0, :], ALU.add).then_inc(dq_t, 1)

            def split_latent(j):
                h, slot = j % NH, j % 2
                pool.wait_ge(dq_hi, 2 * h + 1)
                pool.wait_ge(dq_t, h + 1)
                sub(qd[1][0:96, slot, :], tbuf[0:96, 0, :], qd[0][0:96, slot, :].bitcast(F32)).then_inc(dq_lo, 1)
                pool.wait_ge(dq_hi, 2 * h + 2)
                sub(kd[1][0:HD, slot, :], tbuf[0:HD, 1, :], kd[0][0:HD, slot, :].bitcast(F32)).then_inc(dq_lo, 1)

            for n in range(N_OUT0 + 2):
                split(n % 2, n, NH if n == 0 else P)
            heads(0, 2 * NH)
            for n in range(N_OUT0 + 2, N_MLP0):
                split(n % 2, n)
            mlp(N_MLP0)
            for n in range(N_IN1, N_IN1 + 4):
                split(n % 2, n)
            uq4 = [uq_raw[:, k, :].rearrange("p (h c) -> p h c", c=96) for k in range(2)]
            kv3 = ukv_raw.rearrange("p (h c) -> p h c", c=P)
            pool.wait_ge(low_hi, 1)
            for k in range(2):
                hi, lo = (wuq[a][:, k, :].rearrange("p (h c) -> p h c", c=P) for a in range(2))
                for d, c in ((slice(0, 96), slice(0, 96)), (slice(96, 112), slice(80, 96)), (slice(112, 128), slice(64, 80))):
                    sub(lo[:, :, d], uq4[k][:, :, c], hi[:, :, d].bitcast(F32))
            for w, c in ((wuk, slice(0, HD)), (wuv, slice(HD, P))):
                hi, lo = (w[a].rearrange("p (h c) -> p h c", c=HD) for a in range(2))
                last = sub(lo, kv3[:, :, c], hi.bitcast(F32))
            last.then_inc(low_lo, 1)
            split(N_IN1 % 2, N_IN1 + 4)
            pool.wait_ge(idx_added, 3 * N_IDX)
            for blk in (1, 2, 3):
                c0 = SC[blk][0] + P * blk
                last = nc.gpsimd.affine_select(out=score[:, c0:c0 + P], in_=score[:, c0:c0 + P], compare_op=ALU.is_ge,
                                               fill=NEG, base=0, pattern=[[-1, P]], channel_multiplier=1)
            last.then_inc(causal_cut, 1)
            for n in range(N_IN1 + 5, N_OUT1 + 2):
                split(n % 2, n)
            heads(2 * NH, 4 * NH)
            for n in range(N_OUT1 + 2, N_MLP1):
                split(n % 2, n)
            mlp(N_MLP1)

        @block.vector
        def _(dve):
            v = nc.vector
            own = Steps(dve, step_v)

            def f(ap):
                return ap.bitcast(F32)

            def sub(dst, a, b):
                return v.tensor_tensor(dst, a, f(b), ALU.subtract)

            def token_factors(norm, sums):
                width = {"cq": Q_LORA, "ckv": KV_LORA}.get(norm, D)
                ms, b, y = fin[:, 0, :], fin[:, 1, :], fin[:, 2, :]
                i = NORMS.index(norm) + 1
                dve.wait_ge(sum_ready, i)
                own.link(v.tensor_scalar(ms, sums, 1.0 / width, EPS, ALU.mult, ALU.add))
                v.reciprocal(b, ms).then_inc(rec_ready, 1)
                dve.wait_ge(root_ready, i)
                own.link(v.scalar_tensor_tensor(b, y, -0.5, y, ALU.mult, ALU.mult))
                own.link(v.tensor_tensor(b, b, ms, ALU.mult))
                own.link(v.scalar_tensor_tensor(fin[:, 3, :], b, 1.5, y, ALU.add, ALU.mult))

            def rsqrt(norm, dst, factor=None):
                token_factors(norm, bank[0][:, 0:NQ])
                for a in range(NQ):
                    last = v.tensor_scalar(sq[:, 0, P * a:P * (a + 1)], ident, fin[:, 3, a:a + 1], None, ALU.mult)
                last.then_inc(diag_ready, 1)
                dve.wait_ge(spread_done, NORMS.index(norm) + 1)
                if factor is None:
                    last = v.tensor_copy(dst, bank[0][:, :])
                else:
                    last = v.tensor_tensor(dst, bank[0][:, :], factor, ALU.mult)
                last.then_inc(norm_ready, 1)
                dve.wait_ge(norm_ready, NORMS.index(norm) + 1)

            def take_slab(n, scale=1.0):
                dve.wait_ge(slab_done, n + 1)
                rank = n if n < N_OUT0 else len(EVEN) + n - N_IN1
                if rank >= 3:
                    dve.wait_ge(p_lo, rank - 1)
                v.scalar_tensor_tensor(tbuf[:, n % 2, :], pj(n)[:, :], scale, rstd[:, :], ALU.mult, ALU.mult)\
                    .then_inc(slab_taken, 1)

            def add_squares(norm, m):
                dve.wait_ge(sq_ready, SQ_BEFORE[norm] + m + 1)
                if m > 1:
                    dve.wait_ge(sq_added, ADD_BEFORE[norm] + m - 1)
                v.tensor_tensor(sqsum[:, :], sqsum[:, :], sq[:, m % 2, :], ALU.add).then_inc(sq_added, 1)

            def normed_lo(norm, m):
                T = XG_BEFORE[norm] + m
                dve.wait_ge(xg_hi, T + 1)
                v.scalar_tensor_tensor(xl[:, m, :], xT[:, m, :], gain[:, GAIN[norm] + m:GAIN[norm] + m + 1],
                                       f(xh[:, m, :]), ALU.mult, ALU.subtract).then_inc(xg_lo, 1)

            def projected(p, name, n):
                t = tbuf[:, n % 2, :]
                dve.wait_ge(p_hi, p + 1)
                if name == "fa":
                    own.link(sub(fl[32:32 + NH, :], rstd_q[0:NH, :], fl[0:NH, :]))
                    v.tensor_scalar(gb[64:64 + NH, :], f(fl[0:NH, :]), -1.0, None, ALU.mult)
                    last = v.tensor_scalar(gb[96:96 + NH, :], f(fl[32:32 + NH, :]), -1.0, None, ALU.mult)
                elif name == "vb":
                    b = bank[1][:, :].rearrange("p (a c) -> p a c", a=NQ)
                    for kv in range(2):
                        hi, lo = (vb[a][:, kv, :].rearrange("p (a c) -> p a c", a=NQ) for a in range(2))
                        for d in range(2):
                            c = slice(HD * d, HD * (d + 1))
                            last = sub(lo[:, :, c], b[:, :, HD * kv:HD * (kv + 1)], hi[:, :, c])
                elif name[0:2] == "va":
                    i = int(name[2])
                    c = slice(P * i, P * (i + 1))
                    last = sub(va[1][:, :, c], bank[1 + i % 2][:, :].rearrange("p (a c) -> p a c", a=NQ), va[0][:, :, c])
                elif name == "kb":
                    for kv in range(2):
                        rows = slice(HD * kv, HD * (kv + 1))
                        for d in range(2):
                            last = sub(kb[1][HD * d:HD * (d + 1), kv, :], t[rows, :], kb[0][rows, kv, :])
                elif name == "nar":
                    for r in range(0, P, 32):
                        last = sub(ki[1][r:r + 32, :], t[0:32, :], ki[0][0:32, :])
                elif name == "kv":
                    for d in range(2):
                        sub(kc[1][HD * d:HD * (d + 1), :], t[0:HD, :], kc[0][0:HD, :])
                    b = bank[3][:, :].rearrange("p (a c) -> p a c", a=NQ)
                    for d in range(2):
                        c = slice(HD * d, HD * (d + 1))
                        last = sub(vc[1][:, :, c], b[:, :, HD:P], vc[0][:, :, c])
                elif name[0:2] == "cq" or name == "ckv":
                    norm = "cq" if name[0:2] == "cq" else "ckv"
                    m = int(name[2]) if norm == "cq" else 0
                    hi, lo = (cq[0][:, m, :], cq[1][:, m, :]) if norm == "cq" else ckv
                    g = GAIN[norm] + m
                    if m:
                        add_squares("cq", 1)
                    last = v.scalar_tensor_tensor(lo, t, gain[:, g:g + 1], f(hi), ALU.mult, ALU.subtract)
                else:
                    i = int(name[2])
                    pair = {"ka": ka, "qa": qa, "qb": qb, "qc": qc, "qi": qi}[name[0:2]]
                    last = sub(pair[1][:, i, :], t, pair[0][:, i, :])
                last.then_inc(p_lo, 1)

            def forget_gate():
                t0, t1, s0, s1, q0 = tbuf[0:NH, 0, :], tbuf[0:NH, 1, :], sq[0:NH, 0, :], sq[0:NH, 1, :], rstd_q[0:NH, :]
                dve.wait_ge(slab_done, 1)
                own.link(v.tensor_tensor(t0, pj(0)[0:NH, :], rstd[0:NH, :], ALU.mult))
                v.tensor_scalar(t0, t0, bfor[:, :], None, ALU.add).then_inc(slab_taken, 1)
                dve.wait_ge(slab_taken, 1)
                v.scalar_tensor_tensor(s0, t0, -1.0, t0, ALU.mult, ALU.min).then_inc(fg_in, 1)
                dve.wait_ge(fg_out, 1)
                own.link(v.tensor_scalar(s0, s1, 1.0, None, ALU.add))
                own.link(v.scalar_tensor_tensor(t1, s0, -1.0, s1, ALU.add, ALU.subtract))
                v.tensor_scalar(q0, s0, -0.5, 1.5, ALU.mult, ALU.add).then_inc(fg_in, 1)
                dve.wait_ge(fg_out, 2)
                dve.wait_ge(fg_in, 2)
                v.memset(s0, 1.0)
                own.link(v.tensor_tensor(t1, t1, q0, ALU.mult))
                own.link(v.tensor_tensor(s1, s1, t1, ALU.subtract))
                own.link(v.scalar_tensor_tensor(t0, t0, 0.0, s1, ALU.min, ALU.subtract))
                v.tensor_tensor_scan(q0, s0, t0, 0.0, ALU.mult, ALU.add).then_inc(fg_in, 1)
                dve.wait_ge(fg_in, 3)

            def mlp_group(n0, H0, g, norm=None):
                for s in range(2 * KT):
                    n = 16 * g + (n0 + s)
                    dve.wait_ge(slab_done, n + 1)
                    ps = pj(n0 + s)[:, :]
                    if s < KT:
                        H = 8 * g + (H0 + s)
                        t, h = tbuf[:, s % 2, :], sq[:, s % 2, :]
                        v.tensor_tensor(t, ps, rstd[:, :], ALU.mult).then_inc(slab_taken, 1)
                        dve.wait_ge(slab_taken, n + 1)
                        if s >= 2:
                            dve.wait_ge(h_lo, H - 1)
                        v.scalar_tensor_tensor(h, t, 0.0, t, ALU.max, ALU.mult).then_inc(h32, 1)
                        dve.wait_ge(h_hi, H + 1)
                        sub(hid[1][:, s, :], h, hid[0][:, s, :]).then_inc(h_lo, 1)
                    else:
                        m = s - KT
                        v.tensor_tensor(xT[:, m, :], ps, xT[:, m, :], ALU.add).then_inc(slab_taken, 1)
                        if norm:
                            if norm != "final":
                                normed_lo(norm, m)
                            if m:
                                add_squares(norm, m)

            def mlp(n0, H0, norm, following):
                rsqrt(norm, rstd[:, :])
                with dve.Fori(0, GROUPS - 1) as g:
                    mlp_group(n0, H0, g)
                mlp_group(n0, H0, GROUPS - 1, following)

            def out_projection(n0, norm):
                for m in range(KT):
                    dve.wait_ge(slab_done, n0 + m + 1)
                    v.tensor_tensor(xT[:, m, :], pj(n0 + m)[:, :], xT[:, m, :], ALU.add).then_inc(slab_taken, 1)
                    if m:
                        add_squares(norm, m)
                for m in range(KT):
                    normed_lo(norm, m)

            def maxima(j):
                if j >= 2:
                    dve.wait_ge(exp_done, 3 * (j - 1))
                us = units(j)
                for i, (blk, b, col, w, _) in enumerate(us):
                    dve.wait_ge(scores_ready, 3 * j + b + 1)
                    m = v.reduce_max(negmax[:, j % 2, blk:blk + 1], bank[b][:, col:col + w], AX.X, negate=True)
                    if i + 1 == len(us) or us[i + 1][1] != b:
                        m.then_inc(max_ready, 1)

            def normalise(j):
                dve.wait_ge(exp_done, 3 * (j + 1))
                if j >= 2:
                    dve.wait_ge(probs_ready, 4 * (j - 1))
                v.reciprocal(rsum[:, j % 2, :], expsum[:, j % 2, :]).then_inc(rsum_ready, 1)
                dve.wait_ge(rsum_ready, j + 1)
                for blk, _, _, w, pc in units(j):
                    pr = probs[:, j % 2, pc:pc + w]
                    v.tensor_scalar(pr, pr, rsum[:, j % 2, blk:blk + 1], None, ALU.mult).then_inc(probs_ready, 1)

            def heads(first, last):
                for s in head_steps(first, last):
                    if first <= s:
                        for k, (b, w) in enumerate(pt_banks(s)):
                            dve.wait_ge(pt_hi, pt_before(s) + k + 1)
                            c = slice(PT_COL[b], PT_COL[b] + w)
                            sub(probT_l[:, c], bank[b][:, 0:w], probT_h[:, c]).then_inc(pt_lo, 1)
                    if first <= s + 2 < last:
                        maxima(s + 2)
                    if first <= s + 1 < last:
                        normalise(s + 1)
                    if latent(first, s + 4):
                        take_latent_query(s + 4)
                    if first <= s:
                        tile, r = out_tile(s)
                        dve.wait_ge(o_hi, s + 1)
                        sub(xl[r:r + HD, tile, :], bank[6][r:r + HD, :], xh[r:r + HD, tile, :]).then_inc(o_lo, 1)
                    if latent(first, s + 4):
                        take_latent_key(s + 4)
                    if first == 2 * NH and 0 <= s + 2 - first < ROUNDS - EARLY_ROUNDS:
                        top8()
                    if first == 2 * NH and s + 2 - first == ROUNDS - EARLY_ROUNDS:
                        v.tensor_scalar(mask_c[:, :], score[:, :], 0.5 * TAKEN, NEG, ALU.is_gt, ALU.mult)\
                            .then_inc(mask_ready, 1)

            def take_latent_query(j):
                h = j % NH
                scale = float((HD + ROPE) ** -0.5)
                if h:
                    dve.wait_ge(dq_lo, 2 * h - 1)
                dve.wait_ge(dq_ready, 2 * h + 1)
                v.scalar_tensor_tensor(tbuf[0:96, 0, :], bank[7][0:96, :], scale, rstd_q[0:96, :], ALU.mult, ALU.mult)
                v.scalar_tensor_tensor(sq[64:96, 0, :], bank[7][96:128, :], scale, rstd_q[96:128, :],
                                       ALU.mult, ALU.mult).then_inc(dq_taken, 1)

            def take_latent_key(j):
                h = j % NH
                if h:
                    dve.wait_ge(dq_lo, 2 * h)
                dve.wait_ge(dq_ready, 2 * h + 2)
                v.tensor_tensor(tbuf[0:HD, 1, :], bank[7][0:HD, :], rstd_k[0:HD, :], ALU.mult).then_inc(dq_taken, 1)

            def top8():
                for blk in (1, 2, 3):
                    c0, w = SC[blk]
                    last = v.max(best8[:, blk - 1, :], score[:, c0:c0 + w])
                own.link(last)
                for blk in (1, 2, 3):
                    c0, w = SC[blk]
                    last = v.match_replace(score[:, c0:c0 + w], best8[:, blk - 1, :], score[:, c0:c0 + w], TAKEN)
                own.link(last)

            def rotate(t, dst):
                a, b = sq[64:96, 0, :], sq[64:96, 1, :]
                v.tensor_tensor(a, t[64:96, :], rope[64:96, :], ALU.mult)
                own.link(v.tensor_tensor(b, t[96:128, :], rope[96:128, :], ALU.mult))
                return v.tensor_tensor(dst, a, b, ALU.add)

            v.memset(sinks[:, :, :], NEG)
            v.memset(table[BUCKETS:BUCKETS + 1, :], NEG)
            v.memset(ones[:, :], 1.0)
            v.memset(fl[0:64, :].bitcast(F32), 0.0)
            v.memset(fl[64:128, :].bitcast(F32), 1.0)
            v.memset(gb[0:64, :].bitcast(F32), 1.0)
            v.memset(gb[64:128, :].bitcast(F32), 0.0).then_inc(memsets_done, 1)
            dve.wait_ge(x_copied, 2 * NQ)
            dve.wait_ge(setup_act, 1)
            for m in range(KT):
                normed_lo("mix_e", m)
                if m:
                    add_squares("mix_e", m)

            rsqrt("mix_e", rstd[:, :])
            forget_gate()
            for n in range(1, len(EVEN) - 4):
                take_slab(n, HD ** -0.5 if EVEN[n][0][0] == "q" else 1.0)
                projected(n - 1, EVEN[n - 1][0], n - 1)
            projected(len(EVEN) - 5, "vb", len(EVEN) - 5)
            dve.wait_ge(slab_done, N_OUT0)
            for n in range(N_OUT0 - 4, N_OUT0):
                take_slab(n, HD ** -0.5)
                if n > N_OUT0 - 4:
                    projected(n - 1, EVEN[n - 1][0], n - 1)
            projected(N_OUT0 - 1, "qb3", N_OUT0 - 1)
            heads(0, 2 * NH)
            out_projection(N_OUT0, "mlp0")
            mlp(N_MLP0, 0, "mlp0", "mix_o")

            p0 = len(EVEN)
            rsqrt("mix_o", rstd[:, :])
            take_slab(N_IN1)
            dve.wait_ge(slab_taken, N_IN1 + 1)
            rotate(tbuf[:, N_IN1 % 2, :], kr32).then_inc(kr_rotated, 1)
            for i in (1, 2):
                take_slab(N_IN1 + i)
                projected(p0 + i - 1, ODD[i - 1][0], N_IN1 + i - 1)
            projected(p0 + 2, "qi1", N_IN1 + 2)
            dve.wait_ge(wi_turned, 1)
            v.tensor_copy(widx[:, :, :].rearrange("p a b -> p (a b)"), bank[3][:, 0:NQ * N_IDX]).then_inc(widx_ready, 1)
            dve.wait_ge(widx_ready, 1)
            dve.wait_ge(low_lo, 1)
            for i in range(N_IDX):
                for blk in (1, 2, 3):
                    c0, w = SC[blk]
                    dve.wait_ge(relu_ready, 3 * i + blk)
                    wcol = widx[:, blk, i:i + 1]
                    if i == 0:
                        e = v.tensor_scalar(score[:, c0:c0 + w], relu[:, c0:c0 + w], wcol, None, ALU.mult)
                    else:
                        dve.wait_ge(idx_added, 3 * (i - 1) + blk)
                        e = v.scalar_tensor_tensor(score[:, c0:c0 + w], relu[:, c0:c0 + w], wcol, score[:, c0:c0 + w],
                                                   ALU.mult, ALU.add)
                    e.then_inc(idx_added, 1)
            dve.wait_ge(kr_hi, 1)
            for slot in range(2):
                last = sub(kr[1][:, slot, :], kr32, kr[0][:, slot, :])
            last.then_inc(kr_ready, 1)
            dve.wait_ge(causal_cut, 1)

            for i in range(3, len(ODD)):
                n = N_IN1 + i
                if i < 7:
                    take_slab(n)
                if 3 < i <= 7:
                    projected(p0 + i - 1, ODD[i - 1][0], n - 1)
                if i == 7:
                    rsqrt("cq", rstd_q[:, :], rope[:, :])
                if i == 9:
                    rsqrt("ckv", rstd_k[:, :])
                for _ in range(min(2, EARLY_ROUNDS - 2 * (i - 3))):
                    top8()
            dve.wait_ge(slab_done, N_OUT1)
            for n in range(N_OUT1 - 4, N_OUT1):
                take_slab(n, HD ** -0.5)
                if n > N_OUT1 - 4:
                    projected(p0 + n - 1 - N_IN1, ODD[n - 1 - N_IN1][0], n - 1)
            projected(p0 + len(ODD) - 1, "qc3", N_OUT1 - 1)
            dve.wait_ge(p_lo, len(EVEN) + len(ODD))
            for t in range(5):
                if t < 4:
                    dve.wait_ge(dv_ready, t + 1)
                    v.tensor_tensor(tbuf[:, t % 2, :], bank[1 + t % 2][:, :], rstd_k[:, :], ALU.mult).then_inc(dv_taken, 1)
                if t:
                    c = slice(P * (t - 1), P * t)
                    dve.wait_ge(dv_hi, t)
                    sub(vd[1][:, :, c], bank[3 * ((t - 1) % 2)][:, :].rearrange("p (a c) -> p a c", a=NQ), vd[0][:, :, c])\
                        .then_inc(dv_lo, 1)
            heads(2 * NH, 4 * NH)
            out_projection(N_OUT1, "mlp1")
            mlp(N_MLP1, KT * GROUPS, "mlp1", "final")

            token_factors("final", bank[0][:, 0:NQ])
            v.tensor_copy(fin[:, 0, :], fin[:, 3, :]).then_inc(fin_ready, 1)
            for a in range(NQ):
                dve.wait_ge(fin_turned, 2 * a + 1)
                if a >= 2:
                    dve.wait_ge(out_stored[a % 2], 16)
                v.tensor_scalar(otok[:, a % 2, 0:512], bank[1 + (2 * a) % 6][:, :], fin[:, 3, a:a + 1], None, ALU.mult)\
                    .then_inc(fin_v, 1)


_INS = ["x", "norm_mix_e", "w_in_e", "b_forget", "sink_logits", "w_out_e", "norm_mix_o", "w_in_o", "norm_cq",
        "norm_ckv", "w_uq", "w_ukv", "w_out_o", "norm_mlp", "w_mlp1", "w_mlp2", "rel_bias", "norm_final"]


def kernel(**inputs):
    import concourse.bacc as bacc
    from concourse.bass_utils import run_bass_kernel_spmd

    nc = bacc.Bacc("TRN2", target_bir_lowering=False, num_devices=1)
    given = {name: np.ascontiguousarray(inputs[name]) for name in _INS}
    given.update(shape_constants())
    arrays, args = {}, []
    for name, a in given.items():
        arrays[f"in_{name}"] = a
        args.append(nc.dram_tensor(f"in_{name}", a.shape, mybir.dt.from_np(a.dtype), kind="ExternalInput").ap())
    out = nc.dram_tensor("out", (1, S, D), F32, kind="ExternalOutput").ap()
    trunk(nc, *args, out)
    result = run_bass_kernel_spmd(nc, [arrays], core_ids=[0])
    return result.results[0]["out"]
```

```python
from contextlib import ExitStack

import numpy as np

import concourse.bass as bass
from concourse import mybir

F32 = mybir.dt.float32
F32R = mybir.dt.float32r
BF16 = mybir.dt.bfloat16
ALU = mybir.AluOpType
ACT = mybir.ActivationFunctionType
AX = mybir.AxisListType

P = 128
D = 1024
KT = D // P
S = 512
NQ = S // P
DFF = 4 * D
GROUPS = DFF // D
EPS = 1e-6
NEG = -1e30
TAKEN = -3e38
HD = 64
NH = 8
W = 128
N_IDX, D_IDX = 8, 32
TOPK = min(256, S // 4)
ROUNDS = TOPK // 8
ROUNDS_AT = (0, 0, 0, 0, 2, 1, 2, 1, 1, 1, 1)
EARLY_ROUNDS = sum(ROUNDS_AT)
ROPE = 32
Q_LORA, KV_LORA = 256, 128
BUCKETS, MAX_EXACT, MAX_DIST = 32, 16, 128
EVEN_IN, ODD_IN = 2312, 1352
C_LEN, B_LEN = S + P - 1, 2 * W + P - 1


def shape_constants():
    def bucket(n):
        nf = np.float32(max(n, MAX_EXACT)) / np.float32(MAX_EXACT)
        large = MAX_EXACT + int(np.float32(np.log(nf)) / np.float32(np.log(MAX_DIST / MAX_EXACT))
                                * np.float32(BUCKETS - MAX_EXACT))
        return n if n < MAX_EXACT else min(large, BUCKETS - 1)

    onehot = np.zeros((BUCKETS + 1, 1024), np.float32)
    for i in range(C_LEN):
        dist = S - 1 - i
        onehot[bucket(dist) if dist >= 0 else BUCKETS, i] = 1
    for i in range(B_LEN):
        dist = 2 * W - 1 - i
        onehot[bucket(dist) if 0 <= dist < W else BUCKETS, C_LEN + i] = 1
    ident = np.eye(P, dtype=np.float32)
    hot = np.zeros((P, NH), np.float32)
    for q in range(4):
        hot[32 * q:32 * q + NH] = np.eye(NH)
    pos = np.arange(S, dtype=np.float32)
    inv = (np.float32(10000.0) ** (-np.arange(0, ROPE, 2, dtype=np.float32) / np.float32(ROPE))).astype(np.float32)
    ang = inv[:, None] * pos[None, :]
    cos, sin = np.cos(ang).astype(np.float32), np.sin(ang).astype(np.float32)
    rope = np.zeros((P, S), np.float32)
    rope[0:64] = 1
    rope[64:96] = np.concatenate([cos, cos])
    rope[96:128] = np.concatenate([-sin, sin])
    causal = np.where(np.arange(P)[None, :] <= np.arange(P)[:, None], 0, NEG).astype(np.float32)
    fixed = np.concatenate([ident, hot, ident[::-1], causal], axis=1)
    return {"c_onehot": onehot, "c_fixed": np.ascontiguousarray(fixed), "c_rope": rope}


N_CONST = 14
NORMS = ("mix_e", "mlp0", "mix_o", "cq", "ckv", "mlp1", "final")
NORM_TILES = (KT, KT, KT, 2, 1, KT, KT)
SQ_BEFORE = {k: sum(NORM_TILES[:i]) for i, k in enumerate(NORMS)}
ADD_BEFORE = {k: sum(NORM_TILES[:i]) - i for i, k in enumerate(NORMS)}
XG_BEFORE = {"mix_e": 0, "mlp0": KT, "mix_o": 2 * KT, "mlp1": 3 * KT, "final": 4 * KT}


def slab_plan():
    even = [("fa", 1536)] + [(f"ka{i}", 512 + P * i) for i in range(4)] + [(f"qa{i}", P * i) for i in range(4)] \
        + [(f"va{i}", 1024 + P * i) for i in range(4)] + [("kb", 2056), ("vb", 2184)] \
        + [(f"qb{i}", 1544 + P * i) for i in range(4)]
    odd = [("nar", 896), ("qi0", 640), ("qi1", 768), ("cq0", 936), ("cq1", 1064), ("ckv", 1192), ("kv", 512)] \
        + [(f"qc{i}", P * i) for i in range(4)]
    return even, odd


EVEN, ODD = slab_plan()
N_IN0 = 0
N_OUT0 = N_IN0 + len(EVEN)
N_MLP0 = N_OUT0 + KT
N_IN1 = N_MLP0 + 2 * KT * GROUPS
N_OUT1 = N_IN1 + len(ODD)
N_MLP1 = N_OUT1 + KT
N_END = N_MLP1 + 2 * KT * GROUPS
NAR = N_IN1

GAIN = {"mix_e": 0, "mlp0": 8, "mix_o": 16, "mlp1": 24, "final": 32, "cq": 40, "ckv": 42}
N_GAIN = 43


def trunk(nc, x, norm_mix_e, w_in_e, b_forget, sink_logits, w_out_e, norm_mix_o, w_in_o, norm_cq, norm_ckv,
          w_uq, w_ukv, w_out_o, norm_mlp, w_mlp1, w_mlp2, rel_bias, norm_final,
          c_onehot, c_fixed, c_rope, out):
    with ExitStack() as ctx:
        def sb(name, shape, dt=F32):
            return ctx.enter_context(nc.sbuf_tensor(name, shape, dt))

        def sem(name):
            return ctx.enter_context(nc.semaphore(name))

        bank = [ctx.enter_context(nc.psum_tensor(f"bank{i}", [P, 512], F32)) for i in range(8)]
        bias_rows = nc.dram_tensor("bias_rows", (2 * NH, 1024), F32, kind="Internal").ap()

        xT = sb("xT", [P, KT, S])
        xh = sb("xh", [P, KT, S], F32R)
        xl = sb("xl", [P, KT, S], F32R)
        raw = sb("raw", [P, 2, 1024])
        wh = sb("wh", [P, 2, 1024], F32R)
        wl = sb("wl", [P, 2, 1024], F32R)
        rstd = sb("rstd", [P, S])
        rstd_q = sb("rstd_q", [P, S])
        rstd_k = sb("rstd_k", [P, S])
        sqsum = sb("sqsum", [P, S])
        sq = sb("sq", [P, 2, S])
        tbuf = sb("tbuf", [P, 2, S])
        probs = sb("probs", [P, 2, 1280])
        probT_h = sb("probT_h", [P, 1280], F32R)
        probT_l = sb("probT_l", [P, 1280], F32R)
        strip_raw = sb("strip_raw", [P, 2, S])
        strip_h = sb("strip_h", [P, 2, S], F32R)
        strip_l = sb("strip_l", [P, 2, S], F32R)
        rope = sb("rope", [P, S])
        ident_b = sb("ident_b", [P, P], BF16)
        flip_r = sb("flip_r", [P, P], F32R)
        ones = sb("ones", [P, P])
        fixed = sb("fixed", [P, P + NH])
        ident = fixed[:, 0:P]
        hot = fixed[:, P:P + NH]
        gain = sb("gain", [P, N_GAIN])
        sinks = sb("sinks", [P, NH, 2])
        sink_in = sb("sink_in", [P, NH])
        bfor = sb("bfor", [NH, 1])
        negmax = sb("negmax", [P, 2, 4])
        expsum = sb("expsum", [P, 2, 4])
        rsum = sb("rsum", [P, 2, 4])
        widx = sb("widx", [P, NQ, N_IDX])
        best8 = sb("best8", [P, 3, 8])
        fin = sb("fin", [P, 4, NQ])
        causal = sb("causal", [P, P], BF16)
        score = sb("score", [P, 1152])
        mask_c = sb("mask_c", [P, 1152], BF16)
        USIZE = 19456
        ur = sb("ur", [P, USIZE], F32R)

        at = [0]

        def take(words):
            at[0] += words
            assert at[0] <= USIZE, at[0]
            return ur[:, at[0] - words:at[0]]

        def tiles(n, w=S):
            return take(n * w).rearrange("p (n w) -> p n w", n=n)

        qa = (tiles(4), tiles(4))
        ka = (tiles(4), tiles(4))
        va = (tiles(NQ), tiles(NQ))
        kb = (tiles(2), tiles(2))
        vb = (tiles(2), tiles(2))
        fl = take(S)
        gb = take(S)
        gf = tiles(2)
        qb = (xh[:, 4:8, :], xl[:, 4:8, :])
        at[0] = 0
        hid = (tiles(KT), tiles(KT))
        xn = (tiles(KT), tiles(KT))
        at[0] = 0
        qd = (tiles(2), tiles(2))
        kd = (tiles(2), tiles(2))
        vd = (tiles(NQ), tiles(NQ))
        wuq = (tiles(2, 1024), tiles(2, 1024))
        wuk = (take(512), take(512))
        wuv = (take(512), take(512))
        cq = (tiles(2), tiles(2))
        ckv = (take(S), take(S))
        kc = (take(S), take(S))
        vc = (tiles(NQ, P), tiles(NQ, P))
        qc = (xh[:, 0:4, :], xl[:, 0:4, :])
        qi = (qd[0], qd[1])
        ki = (kd[0][:, 0, :], kd[1][:, 0, :])
        kr = (kd[0][64:96, :, :], kd[1][64:96, :, :])

        relu = probs[:, 1, 0:1152]
        SC = {1: (0, 256), 2: (256, 384), 3: (640, 512)}
        praw = probs[:, :, :].rearrange("p a b -> p (a b)")
        uq_raw = praw[:, 0:1536].rearrange("p (k n) -> p k n", k=2)
        ukv_raw = praw[:, 1536:2560]
        x_tok = praw[:, 0:2048].rearrange("p (a n) -> p a n", a=2)
        otok = praw[:, 0:2048].rearrange("p (a n) -> p a n", a=2)
        qb_raw = [sq[:, 0, :], sq[:, 1, :], strip_raw[:, 0, :], strip_raw[:, 1, :]]
        qc_raw = [praw[:, S * i:S * (i + 1)] for i in range(4)]
        onehot = strip_raw[0:BUCKETS + 1, :, :].rearrange("p a b -> p (a b)")
        bias_out = strip_raw[0:2 * NH, :, :].rearrange("p a b -> p (a b)")
        g_rows = rstd_q[0:N_GAIN, 0:P]
        table = rstd_q[0:BUCKETS + 1, P:P + 2 * NH]
        w_scaled = rstd_q[0:N_IDX, :]
        kr32 = strip_raw[64:96, 1, :]

        raw_loaded = [sem("raw_loaded0"), sem("raw_loaded1")]
        consts_loaded = sem("consts_loaded")
        x_loaded = [sem("x_loaded0"), sem("x_loaded1")]
        x_turned = sem("x_turned")
        x_copied = sem("x_copied")
        gains_turned = sem("gains_turned")
        bias_made = sem("bias_made")
        setup_act = sem("setup_act")
        memsets_done = sem("memsets_done")
        bias_copied = sem("bias_copied")
        bias_stored = sem("bias_stored")
        w_hi = sem("w_hi")
        w_lo = sem("w_lo")
        slab_done = sem("slab_done")
        slab_taken = sem("slab_taken")
        p_hi = sem("p_hi")
        p_lo = sem("p_lo")
        vt_ready = sem("vt_ready")
        xg_hi = sem("xg_hi")
        xg_lo = sem("xg_lo")
        sq_ready = sem("sq_ready")
        sq_added = sem("sq_added")
        sum_ready = sem("sum_ready")
        rec_ready = sem("rec_ready")
        root_ready = sem("root_ready")
        diag_ready = sem("diag_ready")
        spread_done = sem("spread_done")
        norm_ready = sem("norm_ready")
        h32 = sem("h32")
        h_hi = sem("h_hi")
        h_lo = sem("h_lo")
        step_v = sem("step_v")
        step_a = sem("step_a")
        fg_in = sem("fg_in")
        fg_out = sem("fg_out")
        scores_ready = sem("scores_ready")
        max_ready = sem("max_ready")
        exp_done = sem("exp_done")
        rsum_ready = sem("rsum_ready")
        probs_ready = sem("probs_ready")
        pt_ready = sem("pt_ready")
        pt_hi = sem("pt_hi")
        pt_lo = sem("pt_lo")
        o_ready = sem("o_ready")
        o_hi = sem("o_hi")
        o_lo = sem("o_lo")
        strip_loaded = [sem("strip_loaded0"), sem("strip_loaded1")]
        sink_set = sem("sink_set")
        strip_hi_ready = sem("strip_hi_ready")
        prep_ready = sem("prep_ready")
        low_loaded = sem("low_loaded")
        low_hi = sem("low_hi")
        low_lo = sem("low_lo")
        wi_scaled = sem("wi_scaled")
        wi_turned = sem("wi_turned")
        widx_ready = sem("widx_ready")
        idx_ready = sem("idx_ready")
        relu_ready = sem("relu_ready")
        idx_added = sem("idx_added")
        causal_cut = sem("causal_cut")
        mask_ready = sem("mask_ready")
        dv_ready = sem("dv_ready")
        dv_hi = sem("dv_hi")
        dv_lo = sem("dv_lo")
        dq_ready = sem("dq_ready")
        dq_taken = sem("dq_taken")
        dq_t = sem("dq_t")
        dq_hi = sem("dq_hi")
        dq_lo = sem("dq_lo")
        fin_turned = sem("fin_turned")
        fin_v = sem("fin_v")
        fin_a = sem("fin_a")
        fin_ready = sem("fin_ready")
        kr_rotated = sem("kr_rotated")
        kr_hi = sem("kr_hi")
        kr_ready = sem("kr_ready")
        out_stored = [sem("out_stored0"), sem("out_stored1")]

        class Steps:

            def __init__(self, eng, s):
                self.eng, self.s, self.n = eng, s, 0

            def done(self, ins):
                ins.then_inc(self.s, 1)
                self.n += 1
                return self.n

            def wait(self, n=None):
                self.eng.wait_ge(self.s, self.n if n is None else n)

            def link(self, ins):
                self.done(ins)
                self.wait()

        def weights_of(n):
            def block(w, col, width=P, row=0, rows=D):
                return w[row:row + rows, col:col + width].rearrange("(k p) n -> p k n", p=P)
            if n < N_OUT0:
                name, col = EVEN[n]
                return block(w_in_e[0], col, NH if name == "fa" else P)
            if n < N_MLP0:
                return block(w_out_e[0], P * (n - N_OUT0))
            if N_IN1 <= n < N_OUT1:
                return block(w_in_o[0], ODD[n - N_IN1][1])
            return block(w_out_o[0], P * (n - N_OUT1))

        def raw_count(n):
            extra = 48 if n >= NAR and n % 2 == NAR % 2 else 0
            return 16 * (n // 2 + 1) + extra

        def pj(n):
            return bank[4 + n % 4]

        norms = []

        def units(j):
            if attention(j) == "B":
                return [(0, 0, 0, 130, 0), (1, 0, 130, 258, 130), (2, 1, 0, 258, 388), (3, 2, 0, 258, 646)]
            return [(0, 0, 0, 128, 0), (2, 0, 128, 384, 128), (1, 1, 0, 256, 512), (3, 2, 0, 512, 768)]

        def unit_of(j, blk):
            return [u for u in units(j) if u[0] == blk][0]

        def attention(j):
            return "ABDC"[j // NH]

        def pt_parts(j):
            if attention(j) == "B":
                return [(0, 3, 0, 0, 256), (1, 3, 256, 128, 256), (2, 4, 0, 256, 256), (3, 4, 256, 384, 128)]
            return [(0, 3, 0, 0, 512), (1, 4, 0, 128, 384), (3, 4, 384, 384, 128), (2, 5, 0, 256, 256)]

        def pt_banks(j):
            return [(3, 512), (4, 384)] if attention(j) == "B" else [(3, 512), (4, 512), (5, 256)]

        PT_COL = {3: 0, 4: 512, 5: 1024}

        def pt_before(j):
            return sum(len(pt_banks(i)) for i in range(j))

        def out_tile(j):
            h = j % NH
            return {"A": 0, "B": 4, "C": 0, "D": 4}[attention(j)] + h // 2, 64 * (h % 2)

        def strip_count(j):
            return sum(1 for i in range(j + 1) if attention(i) in "BC" and i % 2 == j % 2)

        def t5_rank(j):
            return sum(1 for i in range(j) if attention(i) in "BC")

        def prep_rank(j):
            return sum(1 for i in range(j) if attention(i) in "ABC")

        def out_bank(j):
            return bank[6] if j < 2 * NH else bank[7]

        def latent_banks(h):
            return (bank[3], bank[0]) if h < 2 else (bank[6], bank[6])

        def normed(norm):
            return xn if norm[0:3] == "mlp" else (xh, xl)

        def out_order(first):
            return list(range(KT)) if first == 0 else [4, 5, 6, 7, 0, 1, 2, 3]

        def head_steps(first, last):
            return range(first - (4 if attention(first) == "D" else 3), last)

        def latent(first, j):
            return first == 2 * NH <= j < 3 * NH

        def low_pieces():
            def columns(t, w):
                return t.rearrange("p (h c) -> p h c", c=w)
            pieces = []
            for k in range(2):
                src, dst = columns(uq_raw[:, k, :], 96), [columns(wuq[a][:, k, :], P) for a in range(2)]
                for d0, d1, c0 in ((0, 96, 0), (96, 112, 80), (112, 128, 64)):
                    pieces.append((src[:, :, c0:c0 + d1 - d0], [t[:, :, d0:d1] for t in dst]))
            for w, c in ((wuk, slice(0, HD)), (wuv, slice(HD, P))):
                pieces.append((columns(ukv_raw, P)[:, :, c], [columns(w[a], HD) for a in range(2)]))
            return pieces

        block = ctx.enter_context(nc.Block())

        @block.sync
        def _(sp):
            def load_slab(n, src=None):
                if n >= 2:
                    sp.wait_ge(w_hi, n - 1)
                    sp.wait_ge(w_lo, n - 1)
                if n == NAR:
                    w = w_in_o[0]
                    dst = raw[:, n % 2, :].rearrange("p (k n) -> p k n", k=KT)
                    for c0, c1, d0 in ((896, 960, 0), (1320, 1352, 64), (1336, 1352, 96), (1320, 1336, 112)):
                        sp.dma_start(dst[:, :, d0:d0 + c1 - c0],
                                     w[:, c0:c1].rearrange("(k p) n -> p k n", p=P)).then_inc(raw_loaded[n % 2], 16)
                    return
                src = weights_of(n)
                width = src.shape[2]
                dst = raw[:, n % 2, 0:KT * width].rearrange("p (k n) -> p k n", k=KT)
                sp.dma_start(dst, src).then_inc(raw_loaded[n % 2], 16)

            def load_mlp_group(layer, n0, g):
                base = n0 + 16 * g
                w1 = w_mlp1[layer].rearrange("(k p) n -> p k n", p=P)
                w2 = w_mlp2[layer].rearrange("(g k p) n -> p g k n", p=P, k=KT)
                for s in range(2 * KT):
                    sp.wait_ge(w_hi, base + (s - 1))
                    sp.wait_ge(w_lo, base + (s - 1))
                    slot = (n0 + s) % 2
                    dst = raw[:, slot, :].rearrange("p (k n) -> p k n", k=KT)
                    if s < KT:
                        src = w1[:, :, bass.ds(g * D + P * s, P)]
                    else:
                        src = w2[:, bass.ds(g, 1), :, P * (s - KT):P * (s - KT + 1)]
                        dst = raw[:, slot, :].rearrange("p (o k n) -> p o k n", k=KT, o=1)
                    sp.dma_start(dst, src).then_inc(raw_loaded[slot], 16)

            def load_mlp(layer, n0):
                with sp.Fori(0, GROUPS) as g:
                    load_mlp_group(layer, n0, g)

            def load_strip(j):
                slot = j % 2
                if attention(j - 2) in "BC":
                    sp.wait_ge(prep_ready, prep_rank(j - 2) + 1)
                if attention(j) == "B":
                    row, off, width, c0 = j % NH, C_LEN, 2 * W, 2
                else:
                    row, off, width, c0 = NH + j % NH, 0, S, 0
                src = bias_rows[row:row + 1, off:off + width + P - 1]
                src = bass.AP(src.tensor, src.offset, [[1, P], [1, width]])
                sp.dma_start(strip_raw[:, slot, c0:c0 + width], src).then_inc(strip_loaded[slot], 16)

            sp.dma_start(fixed[:, :], c_fixed[:, 0:P + NH]).then_inc(consts_loaded, 16)
            sp.dma_start(rstd_k[:, 0:2 * P], c_fixed[:, P + NH:3 * P + NH]).then_inc(consts_loaded, 16)
            for a in range(2):
                sp.dma_start(x_tok[:, a, :], x[0, P * a:P * (a + 1), :]).then_inc(x_loaded[a], 16)
            for key, src in (("mix_e", norm_mix_e[0]), ("mlp0", norm_mlp[0]), ("mix_o", norm_mix_o[0]),
                             ("mlp1", norm_mlp[1]), ("final", norm_final), ("cq", norm_cq[0]), ("ckv", norm_ckv[0])):
                rows = src.shape[0] // P
                sp.dma_start(g_rows[GAIN[key]:GAIN[key] + rows, :], src.rearrange("(t p) -> t p", p=P))\
                    .then_inc(consts_loaded, 16)
            load_slab(0)
            load_slab(1)
            sp.dma_start(table[0:BUCKETS, :], rel_bias).then_inc(consts_loaded, 16)
            sp.dma_start(onehot, c_onehot).then_inc(consts_loaded, 16)
            sp.dma_start(rope[:, :], c_rope).then_inc(consts_loaded, 16)
            sp.dma_start(bfor[:, :], b_forget.rearrange("a h -> h a")).then_inc(consts_loaded, 16)
            sp.dma_start(sink_in[:, :], sink_logits.to_broadcast([P, NH])).then_inc(consts_loaded, 16)
            for a in range(2, NQ):
                sp.wait_ge(x_turned, 2 * (a - 1))
                sp.dma_start(x_tok[:, a % 2, :], x[0, P * a:P * (a + 1), :]).then_inc(x_loaded[a % 2], 16)
            sp.wait_ge(bias_copied, 1)
            sp.dma_start(bias_rows, bias_out).then_inc(bias_stored, 16)
            for n in range(2, N_OUT0 + 4):
                load_slab(n)
            sp.wait_ge(bias_stored, 16)
            sp.wait_ge(p_lo, len(EVEN))
            for j in range(NH, 2 * NH):
                load_strip(j)
            sp.wait_ge(pt_ready, pt_before(2 * NH))
            sp.dma_start(uq_raw, w_uq[0].rearrange("(k p) n -> p k n", p=P)).then_inc(low_loaded, 16)
            sp.dma_start(ukv_raw, w_ukv[0]).then_inc(low_loaded, 16)
            for n in range(N_OUT0 + 4, N_MLP0):
                load_slab(n)
            load_mlp(0, N_MLP0)
            for n in range(N_IN1, N_OUT1 + 4):
                load_slab(n)
            sp.wait_ge(kr_ready, 1)
            for j in range(3 * NH, 4 * NH):
                load_strip(j)
            for n in range(N_OUT1 + 4, N_MLP1):
                load_slab(n)
            load_mlp(1, N_MLP1)
            for a in range(NQ):
                sp.wait_ge(fin_v, a + 1)
                sp.wait_ge(fin_a, a + 1)
                sp.dma_start(out[0, P * a:P * (a + 1), :], otok[:, a % 2, :]).then_inc(out_stored[a % 2], 16)
            for a in range(2):
                sp.wait_ge(out_stored[a], 32)

        @block.tensor
        def _(pe):
            mm = nc.tensor.matmul

            def product(dst, lhs, rhs, start=True, stop=True, check=True):
                mm(dst, lhs[0], rhs[0], start=start, stop=False, skip_group_check=not check)
                mm(dst, lhs[0], rhs[1], start=False, stop=False, skip_group_check=not check)
                return mm(dst, lhs[1], rhs[0], start=False, stop=stop, skip_group_check=not check)

            def slab(n, slot, dst, acts, tile_wait=None, width=P, norm_part=None, after=KT - 1):
                pe.wait_ge(w_hi, n + 1)
                pe.wait_ge(w_lo, n + 1)
                for k in range(KT):
                    if tile_wait:
                        tile_wait(k)
                    cols = slice(width * k, width * (k + 1))
                    last = product(dst, (wh[:, slot, cols], wl[:, slot, cols]), (acts[0][:, k, :], acts[1][:, k, :]),
                                   start=k == 0, stop=k == KT - 1)
                    if k == KT - 1:
                        last.then_inc(slab_done, 1)
                    if norm_part and k == after:
                        norm_part()

            def slab_tiles(n, ks, whole):
                pe.wait_ge(w_hi, n + 1)
                pe.wait_ge(w_lo, n + 1)
                for k in ks:
                    cols = slice(P * k, P * (k + 1))
                    last = product(pj(n)[:, :], (wh[:, n % 2, cols], wl[:, n % 2, cols]), (xh[:, k, :], xl[:, k, :]),
                                   start=k == whole[0], stop=k == whole[-1])
                if ks[-1] == whole[-1]:
                    last.then_inc(slab_done, 1)

            def sum_squares(norm):
                if norm == "ckv":
                    pe.wait_ge(norm_ready, NORMS.index(norm))
                    pe.wait_ge(sq_ready, SQ_BEFORE[norm] + 1)
                else:
                    pe.wait_ge(sq_added, ADD_BEFORE[norm] + NORM_TILES[NORMS.index(norm)] - 1)
                for a in range(NQ):
                    last = mm(bank[0][:, a:a + 1], sqsum[:, P * a:P * (a + 1)], ones[:, 0:1], start=True, stop=True)
                last.then_inc(sum_ready, 1)

            def spread(norm):
                pe.wait_ge(diag_ready, NORMS.index(norm) + 1)
                mm(bank[0][:, :], ones[:, :], sq[:, 0, :], start=True, stop=True).then_inc(spread_done, 1)

            def turn_values(n, b):
                pe.wait_ge(slab_taken, n + 1)
                for a in range(NQ):
                    last = nc.tensor.transpose(bank[b][:, P * a:P * (a + 1)], tbuf[:, n % 2, P * a:P * (a + 1)],
                                               ident[:, :])
                last.then_inc(vt_ready, 1)

            def mlp_group(n0, H0, norm, g):
                base = n0 + 16 * g
                for s in range(2 * KT):
                    n = base + s
                    pe.wait_ge(slab_taken, n - 3)
                    if s < KT:
                        wait = (lambda k: pe.wait_ge(xg_lo, XG_BEFORE[norm] + k + 1)) if s == 0 else None
                        part = {0: lambda: sum_squares(norm), 1: lambda: spread(norm)}.get(s) if isinstance(g, int) else None
                        slab(n, (n0 + s) % 2, pj(n0 + s)[:, :], xn, wait, norm_part=part, after=4 - s)
                    else:
                        wait = (lambda k: pe.wait_ge(h_lo, 8 * g + (H0 + k + 1))) if s == KT else None
                        slab(n, (n0 + s) % 2, pj(n0 + s)[:, :], hid, wait)

            def mlp(n0, H0, norm):
                mlp_group(n0, H0, norm, 0)
                with pe.Fori(1, GROUPS) as g:
                    mlp_group(n0, H0, norm, g)

            def scores(j):
                kind, h, slot = attention(j), j % NH, j % 2
                r = 64 * (h % 2)
                if kind in "ABC":
                    pe.wait_ge(prep_ready, prep_rank(j) + 1)
                if kind == "D":
                    pe.wait_ge(dq_lo, 2 * (h + 1))
                if j == NH:
                    pe.wait_ge(p_lo, len(EVEN))
                if j == 3 * NH:
                    pe.wait_ge(mask_ready, 1)
                if j == 2 * NH:
                    pe.wait_ge(dv_lo, 4)
                    pe.wait_ge(dq_taken, 4)
                for i, (blk, b, col, width, _) in enumerate(units(j)):
                    if i == 0 or units(j)[i - 1][1] != b:
                        if j not in (0, 2 * NH):
                            pe.wait_ge(exp_done, 3 * (j - 1) + b + 1)
                    qs = slice(P * blk, P * (blk + 1))
                    last_in_bank = i + 1 == len(units(j)) or units(j)[i + 1][1] != b
                    if kind == "B":
                        t = h // 2
                        kv = h // 4
                        dst = bank[b][:, col:col + width]
                        c0 = 0 if width == 258 else 128
                        if c0 == 0:
                            mm(dst, flip_r[:, :], strip_h[:, slot, 0:258], start=True, stop=False)
                            mm(dst, flip_r[:, :], strip_l[:, slot, 0:258], start=False, stop=False)
                        else:
                            mm(dst[:, 0:2], flip_r[:, :], strip_h[:, slot, 0:2], start=True, stop=False)
                            mm(dst[:, 0:2], flip_r[:, :], strip_l[:, slot, 0:2], start=False, stop=True)
                            mm(dst[:, 2:130], flip_r[:, :], strip_h[:, slot, 130:258], start=True, stop=False)
                            mm(dst[:, 2:130], flip_r[:, :], strip_l[:, slot, 130:258], start=False, stop=False)
                        k0 = max(blk - 1, 0) * P
                        ks = slice(k0, k0 + width - 2)
                        last = product(dst[:, 2:width], (qb[0][r:r + 64, t, qs], qb[1][r:r + 64, t, qs]),
                                       (kb[0][r:r + 64, kv, ks], kb[1][r:r + 64, kv, ks]), start=False)
                    else:
                        dst = bank[b][:, col:col + width]
                        if kind == "A":
                            t = h // 2
                            mm(dst, fl[:, qs], gf[:, slot, 0:width], start=True, stop=False)
                            product(dst, (qa[0][r:r + 64, t, qs], qa[1][r:r + 64, t, qs]),
                                    (ka[0][r:r + 64, t, 0:width], ka[1][r:r + 64, t, 0:width]), start=False, stop=False)
                            last = mm(dst[:, P * blk:P * (blk + 1)], ident_b[:, :], causal[:, :], start=False, stop=True)
                        elif kind == "D":
                            product(dst, (qd[0][0:96, slot, qs], qd[1][0:96, slot, qs]),
                                    (kd[0][0:96, slot, 0:width], kd[1][0:96, slot, 0:width]), start=True, stop=False)
                            last = mm(dst[:, P * blk:P * (blk + 1)], ident_b[:, :], causal[:, :], start=False, stop=True)
                        else:
                            t = h // 2
                            off = S - width
                            mm(dst, flip_r[:, :], strip_h[:, slot, off:S], start=True, stop=False)
                            mm(dst, flip_r[:, :], strip_l[:, slot, off:S], start=False, stop=False)
                            if blk:
                                c0, w = SC[blk]
                                mm(dst, ident_b[:, :], mask_c[:, c0:c0 + w], start=False, stop=False)
                            last = product(dst, (qc[0][r:r + 64, t, qs], qc[1][r:r + 64, t, qs]),
                                           (kc[0][r:r + 64, 0:width], kc[1][r:r + 64, 0:width]), start=False)
                    if last_in_bank:
                        last.then_inc(scores_ready, 1)

            def turn_probs(j):
                slot = j % 2
                if j == 0:
                    pe.wait_ge(slab_taken, N_OUT0)
                if j == 2 * NH:
                    pe.wait_ge(slab_taken, N_OUT1)
                pe.wait_ge(probs_ready, 4 * (j + 1))
                done = None
                parts = pt_parts(j)
                for i, (kt, b, col, q0, nq) in enumerate(parts):
                    if (i == 0 or parts[i - 1][1] != b):
                        before = [x for x in range(j) if x // (2 * NH) == j // (2 * NH) and any(bb == b for bb, _ in pt_banks(x))]
                        if before:
                            x = before[-1]
                            k = [bb for bb, _ in pt_banks(x)].index(b)
                            pe.wait_ge(pt_lo, pt_before(x) + k + 1)
                    for q in range(q0, q0 + nq, P):
                        blk = q // P
                        _, _, _, width, pcol = unit_of(j, blk)
                        if attention(j) == "B":
                            c = pcol + (2 if kt == blk - 1 or blk == 0 else 130)
                        else:
                            c = pcol + P * kt
                        done = nc.tensor.transpose(bank[b][:, col + q - q0:col + q - q0 + P],
                                                   probs[:, slot, c:c + P], ident[:, :])
                    if i + 1 == len(parts) or parts[i + 1][1] != b:
                        done.then_inc(pt_ready, 1)

            def values(j):
                kind, h = attention(j), j % NH
                if j not in (0, 2 * NH):
                    pe.wait_ge(o_lo, j)
                for i, (kt, b, col, q0, nq) in enumerate(pt_parts(j)):
                    k = [bb for bb, _ in pt_banks(j)].index(b)
                    pe.wait_ge(pt_lo, pt_before(j) + k + 1)
                    pc = PT_COL[b] + col
                    t = h // 2
                    v = {"A": lambda a: va[a][:, kt, P * t:P * (t + 1)],
                         "B": lambda a: vb[a][:, h // 4, P * kt:P * (kt + 1)],
                         "D": lambda a: vd[a][:, kt, P * t:P * (t + 1)],
                         "C": lambda a: vc[a][:, kt, :]}[kind]
                    last = product(out_bank(j)[:, q0:q0 + nq], (v(0), v(1)),
                                   (probT_h[:, pc:pc + nq], probT_l[:, pc:pc + nq]),
                                   start=i == 0, stop=i == 3, check=kind != "B")
                last.then_inc(o_ready, 1)

            def latent_query(h):
                if h == 0:
                    pe.wait_ge(p_lo, len(EVEN) + 7)
                    pe.wait_ge(low_lo, KT)
                else:
                    pe.wait_ge(dq_taken, 2 * h)
                if h == 2:
                    pe.wait_ge(slab_taken, N_OUT1)
                for k in range(2):
                    last = product(latent_banks(h)[0][:, :],
                                   (wuq[0][:, k, P * h:P * (h + 1)], wuq[1][:, k, P * h:P * (h + 1)]),
                                   (cq[0][:, k, :], cq[1][:, k, :]), start=k == 0, stop=k == 1)
                last.then_inc(dq_ready, 1)

            def latent_key(h):
                if h == 0:
                    pe.wait_ge(norm_ready, NORMS.index("ckv") + 1)
                if h >= 2:
                    pe.wait_ge(dq_taken, 2 * h + 1)
                product(latent_banks(h)[1][0:64, :], (wuk[0][:, HD * h:HD * (h + 1)], wuk[1][:, HD * h:HD * (h + 1)]),
                        ckv).then_inc(dq_ready, 1)

            def heads(first, last, steps):
                for s in steps:
                    if first <= s + 2 < last:
                        scores(s + 2)
                    if latent(first, s + 4):
                        latent_query((s + 4) % NH)
                    if first <= s:
                        values(s)
                    if first <= s + 1 < last:
                        turn_probs(s + 1)
                    if latent(first, s + 4):
                        latent_key((s + 4) % NH)

            def out_projection(n0, first, last):
                order = out_order(first)
                pe.wait_ge(o_lo, last - 2)
                slab_tiles(n0, order[:-1], order)
                values(last - 1)
                pe.wait_ge(pt_lo, pt_before(last))
                early = 3 if pj(n0 + 1) is not out_bank(last - 1) else 0
                if early:
                    slab_tiles(n0 + 1, order[:early], order)
                pe.wait_ge(o_lo, last)
                slab_tiles(n0, order[-1:], order)
                slab_tiles(n0 + 1, order[early:], order)
                for n in range(n0 + 2, n0 + KT):
                    if n >= n0 + 4:
                        pe.wait_ge(slab_taken, n - 3)
                    slab_tiles(n, order, order)

            steps0, steps1 = head_steps(0, 2 * NH), head_steps(2 * NH, 4 * NH)
            pe.wait_ge(consts_loaded, 16 * N_CONST)
            pe.wait_ge(memsets_done, 1)
            for a in range(NQ):
                pe.wait_ge(x_loaded[a % 2], 16 * (a // 2 + 1))
                for half in range(2):
                    if a >= 2:
                        pe.wait_ge(x_copied, 2 * (a - 2) + half + 1)
                    b = 2 * (a % 2) + half
                    for k in range(4):
                        c = P * (4 * half + k)
                        last = nc.tensor.transpose(bank[b][:, P * k:P * (k + 1)], x_tok[:, a % 2, c:c + P], ident[:, :])
                    last.then_inc(x_turned, 1)
                if a == 1:
                    nc.tensor.transpose(bank[4][:, 0:N_GAIN], g_rows, ident[0:N_GAIN, 0:N_GAIN]).then_inc(gains_turned, 1)
                    for c in range(2):
                        last = mm(bank[5 + c][0:2 * NH, :], table, onehot[:, 512 * c:512 * (c + 1)], start=True, stop=True)
                    last.then_inc(bias_made, 1)

            for n in range(N_OUT0):
                name = EVEN[n][0]
                if n == 0:
                    pe.wait_ge(bias_copied, 1)
                if n >= 4:
                    pe.wait_ge(slab_taken, n - 3)
                if n == N_OUT0 - 1:
                    pe.wait_ge(p_lo, len(EVEN) - 4)
                    heads(0, 2 * NH, steps0[:2])
                width = NH if name == "fa" else P
                dst = pj(n)[0:NH, :] if name == "fa" else pj(n)[:, :]
                part = {0: lambda: sum_squares("mix_e"), 1: lambda: spread("mix_e")}.get(n)
                slab(n, n % 2, dst, (xh, xl), (lambda k: pe.wait_ge(xg_lo, k + 1)) if n == 0 else None, width,
                     part, KT - 1 if n == 0 else 3)
                prev = EVEN[n - 1][0] if n else ""
                if prev in ("va0", "va1", "va2", "va3", "vb"):
                    v = [e[0] for e in EVEN if e[0][0] == "v"].index(prev)
                    if v >= 2:
                        pe.wait_ge(p_lo, n - 2)
                    turn_values(n - 1, 1 + v % 2)
            heads(0, 2 * NH, steps0[2:-1])
            out_projection(N_OUT0, 0, 16)
            mlp(N_MLP0, 0, "mlp0")

            def input_slab(i, norm_part=None, after=KT - 1):
                n = N_IN1 + i
                pe.wait_ge(slab_taken, n - 3)
                slab(n, n % 2, pj(n)[:, :], (xh, xl), (lambda k: pe.wait_ge(xg_lo, 2 * KT + k + 1)) if i == 0 else None,
                     norm_part=norm_part, after=after)

            input_slab(0, lambda: sum_squares("mix_o"), 4)
            input_slab(1, lambda: spread("mix_o"), 3)
            input_slab(2)
            input_slab(3)
            pe.wait_ge(wi_scaled, 1)
            for a in range(NQ):
                last = nc.tensor.transpose(bank[3][:, 8 * a:8 * a + 8], w_scaled[:, P * a:P * (a + 1)],
                                           ident[0:8, 0:8])
            last.then_inc(wi_turned, 1)
            pe.wait_ge(p_lo, len(EVEN) + 3)
            for i in range(N_IDX):
                r = 32 * (i % 4)
                for blk in (1, 2, 3):
                    if i:
                        pe.wait_ge(relu_ready, 3 * (i - 1) + blk)
                    w = SC[blk][1]
                    qs = slice(P * blk, P * (blk + 1))
                    product(bank[blk - 1][:, 0:w], (qi[0][r:r + 32, i // 4, qs], qi[1][r:r + 32, i // 4, qs]),
                            (ki[0][r:r + 32, 0:w], ki[1][r:r + 32, 0:w])).then_inc(idx_ready, 1)
            def latent_values(a):
                if a == 0:
                    pe.wait_ge(p_lo, len(EVEN) + 6)
                    pe.wait_ge(low_lo, KT)
                if a >= 2:
                    pe.wait_ge(dv_lo, a - 1)
                ts = slice(P * a, P * (a + 1))
                product(bank[1 + a % 2][:, :], (ckv[0][:, ts], ckv[1][:, ts]), wuv).then_inc(dv_ready, 1)

            input_slab(4)
            pe.wait_ge(relu_ready, 3 * N_IDX)
            input_slab(5, lambda: sum_squares("cq"))
            input_slab(6, lambda: spread("cq"), 5)
            input_slab(7, lambda: sum_squares("ckv"), 5)
            pe.wait_ge(widx_ready, 1)
            turn_values(N_IN1 + 6, 3)
            input_slab(8, lambda: spread("ckv"), 5)
            latent_values(0)
            latent_values(1)
            input_slab(9, lambda: heads(2 * NH, 4 * NH, steps1[:1]), 3)
            latent_values(2)
            latent_values(3)
            input_slab(10, lambda: heads(2 * NH, 4 * NH, steps1[1:2]), 3)
            heads(2 * NH, 4 * NH, steps1[2:-1])
            out_projection(N_OUT1, 16, 32)
            mlp(N_MLP1, KT * GROUPS, "mlp1")

            pe.wait_ge(slab_taken, N_END)
            sum_squares("final")
            pe.wait_ge(xg_hi, XG_BEFORE["final"] + KT)
            for a in range(NQ):
                for half in range(2):
                    i = 2 * a + half
                    if i >= 6:
                        pe.wait_ge((fin_v, fin_a)[half], (i - 6) // 2 + 1)
                    for k in range(4):
                        last = nc.tensor.transpose(bank[1 + i % 6][:, P * k:P * (k + 1)],
                                                   xT[:, 4 * half + k, P * a:P * (a + 1)], ident[:, :])
                    last.then_inc(fin_turned, 1)

        @block.scalar
        def _(act):
            def copy(dst, src, scale=1.0):
                return nc.scalar.activation(dst, src, ACT.Copy, scale=scale)

            def split(slot, loaded, free, width=P):
                act.wait_ge(raw_loaded[slot], loaded)
                if free is not None:
                    act.wait_ge(slab_done, free)
                copy(wh[:, slot, 0:KT * width], raw[:, slot, 0:KT * width]).then_inc(w_hi, 1)

            def split_slab(n):
                if n < N_END:
                    split(n % 2, raw_count(n), n - 1 if n >= 2 else None, NH if n == 0 else P)

            def square(norm, m, src, wait=None):
                if wait is not None:
                    act.wait_ge(*wait)
                if m == 0:
                    if NORMS.index(norm):
                        act.wait_ge(sum_ready, NORMS.index(norm))
                    dst = sqsum[:, :]
                else:
                    dst = sq[:, m % 2, :]
                    if m >= 3:
                        act.wait_ge(sq_added, ADD_BEFORE[norm] + m - 2)
                nc.scalar.activation(dst, src, ACT.Square).then_inc(sq_ready, 1)

            def root(norm):
                act.wait_ge(rec_ready, NORMS.index(norm) + 1)
                nc.scalar.activation(fin[:, 2, :], fin[:, 1, :], ACT.Sqrt).then_inc(root_ready, 1)

            def normed_hi(norm, m):
                copy(normed(norm)[0][:, m, :], xT[:, m, :], gain[:, GAIN[norm] + m:GAIN[norm] + m + 1]).then_inc(xg_hi, 1)

            def projected(p, name, n):
                t = tbuf[:, n % 2, :]
                if name[0] == "v":
                    v = [e[0] for e in EVEN if e[0][0] == "v"].index(name)
                    act.wait_ge(vt_ready, v + 1)
                    b = bank[1 + v % 2][:, :].rearrange("p (a c) -> p a c", a=NQ)
                    if name == "vb":
                        for kv in range(2):
                            dst = vb[0][:, kv, :].rearrange("p (a c) -> p a c", a=NQ)
                            for d in range(2):
                                last = copy(dst[:, :, HD * d:HD * (d + 1)], b[:, :, HD * kv:HD * (kv + 1)])
                    else:
                        i = int(name[2])
                        last = copy(va[0][:, :, P * i:P * (i + 1)], b)
                    last.then_inc(p_hi, 1)
                    return
                act.wait_ge(slab_taken, n + 1)
                if name == "fa":
                    forget_gate(p)
                elif name == "kb":
                    for kv in range(2):
                        for d in range(2):
                            last = copy(kb[0][HD * d:HD * (d + 1), kv, :], t[HD * kv:HD * (kv + 1), :])
                    last.then_inc(p_hi, 1)
                elif name == "nar":
                    copy(w_scaled, t[32:32 + N_IDX, :], float(N_IDX ** -0.5)).then_inc(wi_scaled, 1)
                    for r in range(0, P, 32):
                        last = copy(ki[0][r:r + 32, :], t[0:32, :])
                    last.then_inc(p_hi, 1)
                elif name == "kv":
                    for d in range(2):
                        copy(kc[0][HD * d:HD * (d + 1), :], t[0:HD, :])
                    act.wait_ge(vt_ready, 6)
                    b = bank[3][:, :].rearrange("p (a c) -> p a c", a=NQ)
                    for d in range(2):
                        last = copy(vc[0][:, :, HD * d:HD * (d + 1)], b[:, :, HD:P])
                    last.then_inc(p_hi, 1)
                elif name[0:2] == "cq" or name == "ckv":
                    norm = name[0:2] if name[0:2] == "cq" else name
                    m = int(name[2]) if norm == "cq" else 0
                    square(norm, m, t)
                    g = GAIN[norm] + m
                    copy(cq[0][:, m, :] if norm == "cq" else ckv[0], t, gain[:, g:g + 1]).then_inc(p_hi, 1)
                else:
                    i = int(name[2])
                    dst = {"ka": ka, "qa": qa, "qb": qb, "qc": qc, "qi": qi}[name[0:2]][0][:, i, :]
                    src = {"qb": qb_raw, "qc": qc_raw}.get(name[0:2])
                    copy(dst, src[i] if src else t).then_inc(p_hi, 1)

            def forget_gate(p):
                t0, s0, s1 = tbuf[0:NH, 0, :], sq[0:NH, 0, :], sq[0:NH, 1, :]
                act.wait_ge(fg_in, 1)
                nc.scalar.activation(s1, s0, ACT.Exp).then_inc(fg_out, 1)
                act.wait_ge(fg_in, 2)
                nc.scalar.activation(s1, s0, ACT.Ln).then_inc(fg_out, 1)
                act.wait_ge(fg_in, 3)
                copy(fl[0:NH, :], rstd_q[0:NH, :]).then_inc(p_hi, 1)

            def hidden(n, slot, H):
                act.wait_ge(h32, H + 1)
                copy(hid[0][:, slot, :], sq[:, slot % 2, :]).then_inc(h_hi, 1)

            def mlp_group(n0, H0, g, norm=None, low=False):
                for s in range(2 * KT):
                    n = 16 * g + (n0 + s)
                    if not isinstance(g, int) or n + 2 < N_END:
                        split((n0 + s) % 2, raw_count(n + 2) if isinstance(g, int) else 128 * g + raw_count(n0 + s + 2),
                              n + 1)
                    if s < KT:
                        hidden(n, s, 8 * g + (H0 + s))
                    elif norm:
                        m = s - KT
                        square(norm, m, xT[:, m, :], (slab_taken, n + 1))
                        if norm == "final":
                            copy(xT[:, m, :], xT[:, m, :], gain[:, GAIN[norm] + m:GAIN[norm] + m + 1]).then_inc(xg_hi, 1)
                        else:
                            normed_hi(norm, m)
                        if low:
                            if m == 0:
                                act.wait_ge(low_loaded, 32)
                            src, dst = low_pieces()[m]
                            copy(dst[0], src).then_inc(low_hi, 1)

            def mlp(n0, H0, norm, following, low=False):
                root(norm)
                with act.Fori(0, GROUPS - 1) as g:
                    mlp_group(n0, H0, g)
                mlp_group(n0, H0, GROUPS - 1, following, low)

            def strip(j):
                slot = j % 2
                width = 258 if attention(j) == "B" else S
                act.wait_ge(strip_loaded[slot], 16 * strip_count(j))
                if attention(j) == "B":
                    act.wait_ge(sink_set, j % NH + 1)
                if attention(j - 2) in "BC":
                    act.wait_ge(scores_ready, 3 * (j - 1))
                copy(strip_h[:, slot, 0:width], strip_raw[:, slot, 0:width]).then_inc(strip_hi_ready, 1)

            def heads(first, last, steps):
                for s in steps:
                    if first <= s + 3 < last and attention(s + 3) in "BC":
                        strip(s + 3)
                    if first <= s:
                        for k, (b, w) in enumerate(pt_banks(s)):
                            act.wait_ge(pt_ready, pt_before(s) + k + 1)
                            if k == 0 and s:
                                act.wait_ge(o_ready, s)
                            copy(probT_h[:, PT_COL[b]:PT_COL[b] + w], bank[b][:, 0:w]).then_inc(pt_hi, 1)
                    if latent(first, s + 3):
                        h, slot = (s + 3) % NH, (s + 3) % 2
                        act.wait_ge(dq_t, h + 1)
                        copy(qd[0][0:96, slot, :], tbuf[0:96, 0, :]).then_inc(dq_hi, 1)
                        act.wait_ge(dq_taken, 2 * h + 2)
                        copy(kd[0][0:HD, slot, :], tbuf[0:HD, 1, :]).then_inc(dq_hi, 1)
                    if first <= s + 2 < last:
                        j = s + 2
                        slot = j % 2
                        if j >= 2:
                            act.wait_ge(pt_ready, pt_before(j - 1))
                        us = units(j)
                        for i, (blk, b, col, w, pc) in enumerate(us):
                            act.wait_ge(max_ready, 3 * j + b + 1)
                            e = nc.scalar.activation(probs[:, slot, pc:pc + w], bank[b][:, col:col + w], ACT.Exp,
                                                     bias=negmax[:, slot, blk:blk + 1],
                                                     accum_out=expsum[:, slot, blk:blk + 1])
                            if i + 1 == len(us) or us[i + 1][1] != b:
                                e.then_inc(exp_done, 1)
                    if first <= s:
                        tile, r = out_tile(s)
                        act.wait_ge(o_ready, s + 1)
                        copy(xh[r:r + HD, tile, :], out_bank(s)[r:r + HD, :]).then_inc(o_hi, 1)

            def out_projection(n0, norm):
                for m in range(KT):
                    n = n0 + m
                    act.wait_ge(slab_done, n + 1)
                    split_slab(n + 2)
                    square(norm, m, xT[:, m, :], (slab_taken, n + 1))
                    normed_hi(norm, m)

            act.wait_ge(consts_loaded, 16 * N_CONST)
            act.wait_ge(memsets_done, 1)
            copy(sinks[:, :, 0], sink_in[:, :])
            copy(ident_b[:, :], ident)
            copy(flip_r[:, :], rstd_k[:, 0:P])
            copy(causal[:, :], rstd_k[:, P:2 * P])
            for a in range(2):
                for half in range(2):
                    act.wait_ge(x_turned, 2 * a + half + 1)
                    copy(xT[:, 4 * half:4 * half + 4, P * a:P * (a + 1)],
                         bank[2 * (a % 2) + half][:, :].rearrange("p (k c) -> p k c", k=4)).then_inc(x_copied, 1)
            act.wait_ge(gains_turned, 1)
            copy(gain[:, :], bank[4][:, 0:N_GAIN]).then_inc(setup_act, 1)
            act.wait_ge(bias_made, 1)
            for c in range(2):
                last = copy(bias_out[:, 512 * c:512 * (c + 1)], bank[5 + c][0:2 * NH, :])
            last.then_inc(bias_copied, 1)
            for a in range(2, NQ):
                for half in range(2):
                    act.wait_ge(x_turned, 2 * a + half + 1)
                    copy(xT[:, 4 * half:4 * half + 4, P * a:P * (a + 1)],
                         bank[2 * (a % 2) + half][:, :].rearrange("p (k c) -> p k c", k=4)).then_inc(x_copied, 1)
            split_slab(0)
            split_slab(1)
            act.wait_ge(x_copied, 2 * NQ)
            act.wait_ge(setup_act, 1)
            for m in range(KT):
                normed_hi("mix_e", m)
                square("mix_e", m, xT[:, m, :])

            root("mix_e")
            steps = head_steps(0, 2 * NH)
            for n in range(N_OUT0):
                if n == N_OUT0 - 1:
                    heads(0, 2 * NH, steps[:2])
                split_slab(n + 2)
                if 0 < n <= len(EVEN) - 4:
                    projected(n - 1, EVEN[n - 1][0], n - 1)
            heads(0, 2 * NH, steps[2:3])
            for n in range(N_OUT0 - 4, N_OUT0):
                projected(n, EVEN[n][0], n)
            heads(0, 2 * NH, steps[3:])
            out_projection(N_OUT0, "mlp0")
            mlp(N_MLP0, 0, "mlp0", "mix_o", low=True)

            p0 = len(EVEN)
            root("mix_o")
            split_slab(N_IN1 + 2)
            split_slab(N_IN1 + 3)
            projected(p0, "nar", N_IN1)
            projected(p0 + 1, "qi0", N_IN1 + 1)
            split_slab(N_IN1 + 4)
            projected(p0 + 2, "qi1", N_IN1 + 2)
            split_slab(N_IN1 + 5)
            projected(p0 + 3, "cq0", N_IN1 + 3)
            for i in range(N_IDX):
                for blk in (1, 2, 3):
                    c0, w = SC[blk]
                    act.wait_ge(idx_ready, 3 * i + blk)
                    if i:
                        act.wait_ge(idx_added, 3 * (i - 1) + blk)
                    else:
                        act.wait_ge(low_lo, KT)
                    nc.scalar.activation(relu[:, c0:c0 + w], bank[blk - 1][:, 0:w], ACT.Relu,
                                         scale=float(D_IDX ** -0.5)).then_inc(relu_ready, 1)
            act.wait_ge(kr_rotated, 1)
            for slot in range(2):
                last = copy(kr[0][:, slot, :], kr32)
            last.then_inc(kr_hi, 1)

            def latent_values_hi(a):
                act.wait_ge(diag_ready, NORMS.index("ckv") + 1)
                act.wait_ge(dv_ready, a + 1)
                copy(vd[0][:, a, :], bank[1 + a % 2][:, :], fin[:, 3, a:a + 1]).then_inc(dv_hi, 1)

            steps = head_steps(2 * NH, 4 * NH)
            for i in range(4, len(ODD)):
                n = N_IN1 + i
                if i == 5:
                    projected(p0 + 4, "cq1", n - 1)
                if i == 6:
                    projected(p0 + 5, "ckv", n - 1)
                    root("cq")
                if i == 8:
                    projected(p0 + 6, "kv", N_IN1 + 6)
                    root("ckv")
                if i == 9:
                    latent_values_hi(0)
                    latent_values_hi(1)
                if i == 10:
                    heads(2 * NH, 4 * NH, steps[:2])
                    latent_values_hi(2)
                    latent_values_hi(3)
                split_slab(n + 2)
            for i in range(7, len(ODD)):
                act.wait_ge(slab_done, N_OUT1)
                projected(p0 + i, ODD[i][0], N_IN1 + i)
            heads(2 * NH, 4 * NH, steps[2:])
            out_projection(N_OUT1, "mlp1")
            mlp(N_MLP1, KT * GROUPS, "mlp1", "final")

            root("final")
            act.wait_ge(fin_ready, 1)
            for a in range(NQ):
                act.wait_ge(fin_turned, 2 * a + 2)
                if a >= 2:
                    act.wait_ge(out_stored[a % 2], 16)
                copy(otok[:, a % 2, 512:1024], bank[1 + (2 * a + 1) % 6][:, :], fin[:, 3, a:a + 1]).then_inc(fin_a, 1)

        @block.gpsimd
        def _(pool):
            def sub(dst, a, b):
                return nc.gpsimd.tensor_tensor(dst, a, b, ALU.subtract)

            def split(slot, n, width=P):
                pool.wait_ge(w_hi, n + 1)
                c = slice(0, KT * width)
                sub(wl[:, slot, c], raw[:, slot, c], wh[:, slot, c].bitcast(F32)).then_inc(w_lo, 1)

            def mlp(n0, groups):
                with pool.Fori(0, groups) as g:
                    for s in range(2 * KT):
                        split((n0 + s) % 2, 16 * g + (n0 + s))

            def low(m):
                src, dst = low_pieces()[m]
                pool.wait_ge(low_hi, m + 1)
                sub(dst[1], src, dst[0].bitcast(F32)).then_inc(low_lo, 1)

            def prepare(j):
                slot, h = j % 2, j % NH
                if attention(j) == "A":
                    if j == 0:
                        pool.wait_ge(p_lo, 1)
                    if j >= 2:
                        pool.wait_ge(scores_ready, 3 * (j - 1))
                    nc.gpsimd.tensor_scalar(gf[:, slot, :], gb.bitcast(F32), hot[:, h:h + 1], None, ALU.mult)\
                        .then_inc(prep_ready, 1)
                elif attention(j) in "BC":
                    width = S
                    if attention(j) == "B":
                        width = 258
                        if h >= 2:
                            pool.wait_ge(prep_ready, prep_rank(j - 2) + 1)
                        nc.gpsimd.tensor_copy(strip_raw[:, slot, 0:2], sinks[:, h, :]).then_inc(sink_set, 1)
                    pool.wait_ge(strip_hi_ready, t5_rank(j) + 1)
                    sub(strip_l[:, slot, 0:width], strip_raw[:, slot, 0:width],
                        strip_h[:, slot, 0:width].bitcast(F32)).then_inc(prep_ready, 1)

            def heads(first, last, steps):
                for s in steps:
                    if first <= s + 3 < last and s + 3 >= 2:
                        prepare(s + 3)
                    if latent(first, s + 3):
                        split_latent(s + 3)
                    if latent(first, s + 4):
                        rotate_latent(s + 4)

            def rotate_latent(j):
                h = j % NH
                if h:
                    pool.wait_ge(dq_lo, 2 * h)
                else:
                    pool.wait_ge(w_lo, N_OUT1)
                pool.wait_ge(dq_taken, 2 * h + 1)
                nc.gpsimd.tensor_tensor(tbuf[64:96, 0, :], tbuf[64:96, 0, :], sq[64:96, 0, :], ALU.add).then_inc(dq_t, 1)

            def split_latent(j):
                h, slot = j % NH, j % 2
                pool.wait_ge(dq_hi, 2 * h + 1)
                pool.wait_ge(dq_t, h + 1)
                sub(qd[1][0:96, slot, :], tbuf[0:96, 0, :], qd[0][0:96, slot, :].bitcast(F32)).then_inc(dq_lo, 1)
                pool.wait_ge(dq_hi, 2 * h + 2)
                sub(kd[1][0:HD, slot, :], tbuf[0:HD, 1, :], kd[0][0:HD, slot, :].bitcast(F32)).then_inc(dq_lo, 1)

            for n in range(N_OUT0 + 2):
                if n in (N_OUT0 - 4, N_OUT0 - 3):
                    prepare(n - (N_OUT0 - 4))
                split(n % 2, n, NH if n == 0 else P)
            heads(0, 2 * NH, head_steps(0, 2 * NH))
            for n in range(N_OUT0 + 2, N_MLP0):
                split(n % 2, n)
            mlp(N_MLP0, GROUPS - 1)
            for n in range(N_IN1 - 2 * KT, N_IN1 + 6):
                split(n % 2, n)
                m = n - (N_IN1 - KT) - 2
                if 0 <= m < KT:
                    low(m)
            pool.wait_ge(idx_added, 3 * N_IDX)
            for blk in (1, 2, 3):
                c0 = SC[blk][0] + P * blk
                last = nc.gpsimd.affine_select(out=score[:, c0:c0 + P], in_=score[:, c0:c0 + P], compare_op=ALU.is_ge,
                                               fill=NEG, base=0, pattern=[[-1, P]], channel_multiplier=1)
            last.then_inc(causal_cut, 1)
            steps = head_steps(2 * NH, 4 * NH)
            for n in range(N_IN1 + 6, N_OUT1 + 2):
                split(n % 2, n)
                if n == N_OUT1 - 1:
                    heads(2 * NH, 4 * NH, steps[:1])
                    pool.wait_ge(dq_t, 1)
                if n == N_OUT1:
                    heads(2 * NH, 4 * NH, steps[1:2])
                    pool.wait_ge(dq_t, 2)
            heads(2 * NH, 4 * NH, steps[2:])
            for n in range(N_OUT1 + 2, N_MLP1):
                split(n % 2, n)
            mlp(N_MLP1, GROUPS)

        @block.vector
        def _(dve):
            v = nc.vector
            own = Steps(dve, step_v)

            def f(ap):
                return ap.bitcast(F32)

            def sub(dst, a, b):
                return v.tensor_tensor(dst, a, f(b), ALU.subtract)

            def token_factors(norm, sums):
                width = {"cq": Q_LORA, "ckv": KV_LORA}.get(norm, D)
                ms, b, y = fin[:, 0, :], fin[:, 1, :], fin[:, 2, :]
                i = NORMS.index(norm) + 1
                dve.wait_ge(sum_ready, i)
                own.link(v.tensor_scalar(ms, sums, 1.0 / width, EPS, ALU.mult, ALU.add))
                v.reciprocal(b, ms).then_inc(rec_ready, 1)
                dve.wait_ge(root_ready, i)
                own.link(v.scalar_tensor_tensor(b, y, -0.5, y, ALU.mult, ALU.mult))
                own.link(v.tensor_tensor(b, b, ms, ALU.mult))
                own.link(v.scalar_tensor_tensor(fin[:, 3, :], b, 1.5, y, ALU.add, ALU.mult))

            def spread_factors(norm):
                token_factors(norm, bank[0][:, 0:NQ])
                for a in range(NQ):
                    last = v.tensor_scalar(sq[:, 0, P * a:P * (a + 1)], ident, fin[:, 3, a:a + 1], None, ALU.mult)
                last.then_inc(diag_ready, 1)

            def take_factors(norm, dst, factor=None):
                dve.wait_ge(spread_done, NORMS.index(norm) + 1)
                if factor is None:
                    last = v.tensor_copy(dst, bank[0][:, :])
                else:
                    last = v.tensor_tensor(dst, bank[0][:, :], factor, ALU.mult)
                last.then_inc(norm_ready, 1)
                dve.wait_ge(norm_ready, NORMS.index(norm) + 1)

            def rsqrt(norm, dst):
                spread_factors(norm)
                take_factors(norm, dst)

            def take_slab(n, scale=1.0, dst=None):
                dve.wait_ge(slab_done, n + 1)
                rank = n if n < N_OUT0 else len(EVEN) + n - N_IN1
                if rank >= 3 and dst is None:
                    dve.wait_ge(p_lo, rank - 1)
                v.scalar_tensor_tensor(tbuf[:, n % 2, :] if dst is None else dst, pj(n)[:, :], scale, rstd[:, :], ALU.mult, ALU.mult)\
                    .then_inc(slab_taken, 1)

            def add_squares(norm, m):
                dve.wait_ge(sq_ready, SQ_BEFORE[norm] + m + 1)
                if m > 1:
                    dve.wait_ge(sq_added, ADD_BEFORE[norm] + m - 1)
                v.tensor_tensor(sqsum[:, :], sqsum[:, :], sq[:, m % 2, :], ALU.add).then_inc(sq_added, 1)

            def normed_lo(norm, m):
                T = XG_BEFORE[norm] + m
                dve.wait_ge(xg_hi, T + 1)
                hi, lo = (t[:, m, :] for t in normed(norm))
                v.scalar_tensor_tensor(lo, xT[:, m, :], gain[:, GAIN[norm] + m:GAIN[norm] + m + 1],
                                       f(hi), ALU.mult, ALU.subtract).then_inc(xg_lo, 1)

            def projected(p, name, n):
                t = tbuf[:, n % 2, :]
                dve.wait_ge(p_hi, p + 1)
                if name == "fa":
                    own.link(sub(fl[32:32 + NH, :], rstd_q[0:NH, :], fl[0:NH, :]))
                    v.tensor_scalar(gb[64:64 + NH, :], f(fl[0:NH, :]), -1.0, None, ALU.mult)
                    last = v.tensor_scalar(gb[96:96 + NH, :], f(fl[32:32 + NH, :]), -1.0, None, ALU.mult)
                elif name == "vb":
                    b = bank[1][:, :].rearrange("p (a c) -> p a c", a=NQ)
                    for kv in range(2):
                        hi, lo = (vb[a][:, kv, :].rearrange("p (a c) -> p a c", a=NQ) for a in range(2))
                        for d in range(2):
                            c = slice(HD * d, HD * (d + 1))
                            last = sub(lo[:, :, c], b[:, :, HD * kv:HD * (kv + 1)], hi[:, :, c])
                elif name[0:2] == "va":
                    i = int(name[2])
                    c = slice(P * i, P * (i + 1))
                    last = sub(va[1][:, :, c], bank[1 + i % 2][:, :].rearrange("p (a c) -> p a c", a=NQ), va[0][:, :, c])
                elif name == "kb":
                    for kv in range(2):
                        rows = slice(HD * kv, HD * (kv + 1))
                        for d in range(2):
                            last = sub(kb[1][HD * d:HD * (d + 1), kv, :], t[rows, :], kb[0][rows, kv, :])
                elif name == "nar":
                    for r in range(0, P, 32):
                        last = sub(ki[1][r:r + 32, :], t[0:32, :], ki[0][0:32, :])
                elif name == "kv":
                    for d in range(2):
                        sub(kc[1][HD * d:HD * (d + 1), :], t[0:HD, :], kc[0][0:HD, :])
                    b = bank[3][:, :].rearrange("p (a c) -> p a c", a=NQ)
                    for d in range(2):
                        c = slice(HD * d, HD * (d + 1))
                        last = sub(vc[1][:, :, c], b[:, :, HD:P], vc[0][:, :, c])
                elif name[0:2] == "cq" or name == "ckv":
                    norm = "cq" if name[0:2] == "cq" else "ckv"
                    m = int(name[2]) if norm == "cq" else 0
                    hi, lo = (cq[0][:, m, :], cq[1][:, m, :]) if norm == "cq" else ckv
                    g = GAIN[norm] + m
                    if m:
                        add_squares("cq", 1)
                    last = v.scalar_tensor_tensor(lo, t, gain[:, g:g + 1], f(hi), ALU.mult, ALU.subtract)
                else:
                    i = int(name[2])
                    pair = {"ka": ka, "qa": qa, "qb": qb, "qc": qc, "qi": qi}[name[0:2]]
                    src = {"qb": qb_raw, "qc": qc_raw}.get(name[0:2])
                    last = sub(pair[1][:, i, :], src[i] if src else t, pair[0][:, i, :])
                last.then_inc(p_lo, 1)

            def forget_gate():
                t0, t1, s0, s1, q0 = tbuf[0:NH, 0, :], tbuf[0:NH, 1, :], sq[0:NH, 0, :], sq[0:NH, 1, :], rstd_q[0:NH, :]
                dve.wait_ge(slab_done, 1)
                own.link(v.tensor_tensor(t0, pj(0)[0:NH, :], rstd[0:NH, :], ALU.mult))
                v.tensor_scalar(t0, t0, bfor[:, :], None, ALU.add).then_inc(slab_taken, 1)
                dve.wait_ge(slab_taken, 1)
                v.scalar_tensor_tensor(s0, t0, -1.0, t0, ALU.mult, ALU.min).then_inc(fg_in, 1)
                dve.wait_ge(fg_out, 1)
                own.link(v.tensor_scalar(s0, s1, 1.0, None, ALU.add))
                own.link(v.scalar_tensor_tensor(t1, s0, -1.0, s1, ALU.add, ALU.subtract))
                v.tensor_scalar(q0, s0, -0.5, 1.5, ALU.mult, ALU.add).then_inc(fg_in, 1)
                dve.wait_ge(fg_out, 2)
                dve.wait_ge(fg_in, 2)
                v.memset(s0, 1.0)
                own.link(v.tensor_tensor(t1, t1, q0, ALU.mult))
                own.link(v.tensor_tensor(s1, s1, t1, ALU.subtract))
                own.link(v.scalar_tensor_tensor(t0, t0, 0.0, s1, ALU.min, ALU.subtract))
                v.tensor_tensor_scan(q0, s0, t0, 0.0, ALU.mult, ALU.add).then_inc(fg_in, 1)
                dve.wait_ge(fg_in, 3)

            def mlp_group(n0, H0, g, norm=None):
                for s in range(2 * KT):
                    n = 16 * g + (n0 + s)
                    dve.wait_ge(slab_done, n + 1)
                    ps = pj(n0 + s)[:, :]
                    if s < KT:
                        H = 8 * g + (H0 + s)
                        t, h = tbuf[:, s % 2, :], sq[:, s % 2, :]
                        v.tensor_tensor(t, ps, rstd[:, :], ALU.mult).then_inc(slab_taken, 1)
                        dve.wait_ge(slab_taken, n + 1)
                        if s >= 2:
                            dve.wait_ge(h_lo, H - 1)
                        v.scalar_tensor_tensor(h, t, 0.0, t, ALU.max, ALU.mult).then_inc(h32, 1)
                        dve.wait_ge(h_hi, H + 1)
                        sub(hid[1][:, s, :], h, hid[0][:, s, :]).then_inc(h_lo, 1)
                    else:
                        m = s - KT
                        v.tensor_tensor(xT[:, m, :], ps, xT[:, m, :], ALU.add).then_inc(slab_taken, 1)
                        if norm:
                            if norm != "final":
                                normed_lo(norm, m)
                            if m:
                                add_squares(norm, m)

            def mlp(n0, H0, norm, following):
                rsqrt(norm, rstd[:, :])
                with dve.Fori(0, GROUPS - 1) as g:
                    mlp_group(n0, H0, g)
                mlp_group(n0, H0, GROUPS - 1, following)

            def out_projection(n0, norm):
                for m in range(KT):
                    dve.wait_ge(slab_done, n0 + m + 1)
                    v.tensor_tensor(xT[:, m, :], pj(n0 + m)[:, :], xT[:, m, :], ALU.add).then_inc(slab_taken, 1)
                    if m:
                        add_squares(norm, m)
                    normed_lo(norm, m)

            def maxima(j):
                if j >= 2:
                    dve.wait_ge(exp_done, 3 * (j - 1))
                us = units(j)
                for i, (blk, b, col, w, _) in enumerate(us):
                    dve.wait_ge(scores_ready, 3 * j + b + 1)
                    m = v.reduce_max(negmax[:, j % 2, blk:blk + 1], bank[b][:, col:col + w], AX.X, negate=True)
                    if i + 1 == len(us) or us[i + 1][1] != b:
                        m.then_inc(max_ready, 1)

            def normalise(j):
                dve.wait_ge(exp_done, 3 * (j + 1))
                if j >= 2:
                    dve.wait_ge(probs_ready, 4 * (j - 1))
                v.reciprocal(rsum[:, j % 2, :], expsum[:, j % 2, :]).then_inc(rsum_ready, 1)
                dve.wait_ge(rsum_ready, j + 1)
                for blk, _, _, w, pc in units(j):
                    pr = probs[:, j % 2, pc:pc + w]
                    v.tensor_scalar(pr, pr, rsum[:, j % 2, blk:blk + 1], None, ALU.mult).then_inc(probs_ready, 1)

            def outputs_lo(j):
                tile, r = out_tile(j)
                dve.wait_ge(o_hi, j + 1)
                sub(xl[r:r + HD, tile, :], out_bank(j)[r:r + HD, :], xh[r:r + HD, tile, :]).then_inc(o_lo, 1)

            def heads(first, last, steps):
                for s in steps:
                    if first <= s:
                        for k, (b, w) in enumerate(pt_banks(s)):
                            dve.wait_ge(pt_hi, pt_before(s) + k + 1)
                            c = slice(PT_COL[b], PT_COL[b] + w)
                            sub(probT_l[:, c], bank[b][:, 0:w], probT_h[:, c]).then_inc(pt_lo, 1)
                    if first <= s + 2 < last:
                        maxima(s + 2)
                    if first <= s + 1 < last:
                        normalise(s + 1)
                    if latent(first, s + 4):
                        take_latent_query(s + 4)
                    if first <= s:
                        outputs_lo(s)
                    if latent(first, s + 4):
                        take_latent_key(s + 4)
                    if first == 2 * NH and 0 <= s + 2 - first < ROUNDS - EARLY_ROUNDS:
                        top8()
                    if first == 2 * NH and s + 2 - first == ROUNDS - EARLY_ROUNDS:
                        v.tensor_scalar(mask_c[:, :], score[:, :], 0.5 * TAKEN, NEG, ALU.is_gt, ALU.mult)\
                            .then_inc(mask_ready, 1)

            def take_latent_query(j):
                h = j % NH
                scale = float((HD + ROPE) ** -0.5)
                if h:
                    dve.wait_ge(dq_lo, 2 * h - 1)
                dve.wait_ge(dq_ready, 2 * h + 1)
                v.scalar_tensor_tensor(tbuf[0:96, 0, :], latent_banks(h)[0][0:96, :], scale, rstd_q[0:96, :], ALU.mult, ALU.mult)
                v.scalar_tensor_tensor(sq[64:96, 0, :], latent_banks(h)[0][96:128, :], scale, rstd_q[96:128, :],
                                       ALU.mult, ALU.mult).then_inc(dq_taken, 1)

            def take_latent_key(j):
                h = j % NH
                if h:
                    dve.wait_ge(dq_lo, 2 * h)
                dve.wait_ge(dq_ready, 2 * h + 2)
                v.tensor_tensor(tbuf[0:HD, 1, :], latent_banks(h)[1][0:HD, :], rstd_k[0:HD, :], ALU.mult).then_inc(dq_taken, 1)

            def top8():
                for blk in (1, 2, 3):
                    c0, w = SC[blk]
                    last = v.max(best8[:, blk - 1, :], score[:, c0:c0 + w])
                own.link(last)
                for blk in (1, 2, 3):
                    c0, w = SC[blk]
                    last = v.match_replace(score[:, c0:c0 + w], best8[:, blk - 1, :], score[:, c0:c0 + w], TAKEN)
                own.link(last)

            def rotate(t, dst):
                a, b = sq[64:96, 0, :], sq[64:96, 1, :]
                v.tensor_tensor(a, t[64:96, :], rope[64:96, :], ALU.mult)
                own.link(v.tensor_tensor(b, t[96:128, :], rope[96:128, :], ALU.mult))
                return v.tensor_tensor(dst, a, b, ALU.add)

            v.memset(sinks[:, :, :], NEG)
            v.memset(table[BUCKETS:BUCKETS + 1, :], NEG)
            v.memset(ones[:, :], 1.0)
            v.memset(fl[0:64, :].bitcast(F32), 0.0)
            v.memset(fl[64:128, :].bitcast(F32), 1.0)
            v.memset(gb[0:64, :].bitcast(F32), 1.0)
            v.memset(gb[64:128, :].bitcast(F32), 0.0).then_inc(memsets_done, 1)
            dve.wait_ge(x_copied, 2 * NQ)
            dve.wait_ge(setup_act, 1)
            for m in range(KT):
                normed_lo("mix_e", m)
                if m:
                    add_squares("mix_e", m)

            rsqrt("mix_e", rstd[:, :])
            forget_gate()
            for n in range(1, len(EVEN) - 4):
                take_slab(n, HD ** -0.5 if EVEN[n][0][0] == "q" else 1.0)
                projected(n - 1, EVEN[n - 1][0], n - 1)
            projected(len(EVEN) - 5, "vb", len(EVEN) - 5)
            steps = head_steps(0, 2 * NH)
            dve.wait_ge(spread_done, 1)
            dve.wait_ge(bias_stored, 16)
            for i in range(4):
                if i == 3:
                    heads(0, 2 * NH, steps[:2])
                take_slab(N_OUT0 - 4 + i, HD ** -0.5, qb_raw[i])
            heads(0, 2 * NH, steps[2:3])
            for n in range(N_OUT0 - 4, N_OUT0):
                projected(n, EVEN[n][0], n)
            heads(0, 2 * NH, steps[3:])
            out_projection(N_OUT0, "mlp0")
            mlp(N_MLP0, 0, "mlp0", "mix_o")

            p0 = len(EVEN)
            rsqrt("mix_o", rstd[:, :])
            take_slab(N_IN1)
            dve.wait_ge(slab_taken, N_IN1 + 1)
            rotate(tbuf[:, N_IN1 % 2, :], kr32).then_inc(kr_rotated, 1)
            for i in (1, 2):
                take_slab(N_IN1 + i)
                projected(p0 + i - 1, ODD[i - 1][0], N_IN1 + i - 1)
            take_slab(N_IN1 + 3)
            projected(p0 + 2, "qi1", N_IN1 + 2)
            dve.wait_ge(wi_turned, 1)
            v.tensor_copy(widx[:, :, :].rearrange("p a b -> p (a b)"), bank[3][:, 0:NQ * N_IDX]).then_inc(widx_ready, 1)
            dve.wait_ge(widx_ready, 1)
            dve.wait_ge(low_lo, KT)
            projected(p0 + 3, "cq0", N_IN1 + 3)
            for i in range(N_IDX):
                for blk in (1, 2, 3):
                    c0, w = SC[blk]
                    dve.wait_ge(relu_ready, 3 * i + blk)
                    wcol = widx[:, blk, i:i + 1]
                    if i == 0:
                        e = v.tensor_scalar(score[:, c0:c0 + w], relu[:, c0:c0 + w], wcol, None, ALU.mult)
                    else:
                        dve.wait_ge(idx_added, 3 * (i - 1) + blk)
                        e = v.scalar_tensor_tensor(score[:, c0:c0 + w], relu[:, c0:c0 + w], wcol, score[:, c0:c0 + w],
                                                   ALU.mult, ALU.add)
                    e.then_inc(idx_added, 1)
            dve.wait_ge(kr_hi, 1)
            for slot in range(2):
                last = sub(kr[1][:, slot, :], kr32, kr[0][:, slot, :])
            last.then_inc(kr_ready, 1)
            dve.wait_ge(causal_cut, 1)

            def latent_values_lo(a):
                dve.wait_ge(dv_hi, a + 1)
                v.scalar_tensor_tensor(vd[1][:, a, :], bank[1 + a % 2][:, :], fin[:, 3, a:a + 1], f(vd[0][:, a, :]),
                                       ALU.mult, ALU.subtract).then_inc(dv_lo, 1)

            steps = head_steps(2 * NH, 4 * NH)
            for i in range(4, len(ODD)):
                n = N_IN1 + i
                if i >= 9:
                    heads(2 * NH, 4 * NH, steps[i - 9:i - 8])
                if i < 7:
                    take_slab(n)
                else:
                    take_slab(n, HD ** -0.5, qc_raw[i - 7])
                if i == 4:
                    projected(p0 + 4, "cq1", n)
                if i == 5:
                    projected(p0 + 5, "ckv", n)
                    spread_factors("cq")
                if i == 6:
                    take_factors("cq", rstd_q[:, :], rope[:, :])
                if i == 7:
                    projected(p0 + 6, "kv", n - 1)
                    spread_factors("ckv")
                if i == 8:
                    take_factors("ckv", rstd_k[:, :])
                    latent_values_lo(0)
                    latent_values_lo(1)
                if i == 9:
                    latent_values_lo(2)
                    latent_values_lo(3)
                for _ in range(ROUNDS_AT[i]):
                    top8()
            for i in range(7, len(ODD)):
                projected(p0 + i, ODD[i][0], N_IN1 + i)
            heads(2 * NH, 4 * NH, steps[2:])
            out_projection(N_OUT1, "mlp1")
            mlp(N_MLP1, KT * GROUPS, "mlp1", "final")

            token_factors("final", bank[0][:, 0:NQ])
            v.tensor_copy(fin[:, 0, :], fin[:, 3, :]).then_inc(fin_ready, 1)
            for a in range(NQ):
                dve.wait_ge(fin_turned, 2 * a + 1)
                if a >= 2:
                    dve.wait_ge(out_stored[a % 2], 16)
                v.tensor_scalar(otok[:, a % 2, 0:512], bank[1 + (2 * a) % 6][:, :], fin[:, 3, a:a + 1], None, ALU.mult)\
                    .then_inc(fin_v, 1)


_INS = ["x", "norm_mix_e", "w_in_e", "b_forget", "sink_logits", "w_out_e", "norm_mix_o", "w_in_o", "norm_cq",
        "norm_ckv", "w_uq", "w_ukv", "w_out_o", "norm_mlp", "w_mlp1", "w_mlp2", "rel_bias", "norm_final"]


def kernel(**inputs):
    import concourse.bacc as bacc
    from concourse.bass_utils import run_bass_kernel_spmd

    nc = bacc.Bacc("TRN2", target_bir_lowering=False, num_devices=1)
    given = {name: np.ascontiguousarray(inputs[name]) for name in _INS}
    given.update(shape_constants())
    arrays, args = {}, []
    for name, a in given.items():
        arrays[f"in_{name}"] = a
        args.append(nc.dram_tensor(f"in_{name}", a.shape, mybir.dt.from_np(a.dtype), kind="ExternalInput").ap())
    out = nc.dram_tensor("out", (1, S, D), F32, kind="ExternalOutput").ap()
    trunk(nc, *args, out)
    result = run_bass_kernel_spmd(nc, [arrays], core_ids=[0])
    return result.results[0]["out"]
```

```python
from contextlib import ExitStack

import numpy as np

import concourse.bass as bass
from concourse import mybir

F32 = mybir.dt.float32
F32R = mybir.dt.float32r
BF16 = mybir.dt.bfloat16
ALU = mybir.AluOpType
ACT = mybir.ActivationFunctionType
AX = mybir.AxisListType

P = 128
D = 1024
KT = D // P
S = 512
NQ = S // P
DFF = 4 * D
GROUPS = DFF // D
EPS = 1e-6
NEG = -1e30
TAKEN = -3e38
HD = 64
NH = 8
W = 128
N_IDX, D_IDX = 8, 32
TOPK = min(256, S // 4)
ROUNDS = TOPK // 8
ROUNDS_AT = (0, 0, 0, 0, 0, 1, 2, 1, 2, 1, 1)
EARLY_ROUNDS = sum(ROUNDS_AT)
ROPE = 32
Q_LORA, KV_LORA = 256, 128
BUCKETS, MAX_EXACT, MAX_DIST = 32, 16, 128
EVEN_IN, ODD_IN = 2312, 1352
C_LEN, B_LEN = S + P - 1, 2 * W + P - 1


def shape_constants():
    def bucket(n):
        nf = np.float32(max(n, MAX_EXACT)) / np.float32(MAX_EXACT)
        large = MAX_EXACT + int(np.float32(np.log(nf)) / np.float32(np.log(MAX_DIST / MAX_EXACT))
                                * np.float32(BUCKETS - MAX_EXACT))
        return n if n < MAX_EXACT else min(large, BUCKETS - 1)

    onehot = np.zeros((BUCKETS + 1, 1024), np.float32)
    for i in range(C_LEN):
        dist = S - 1 - i
        onehot[bucket(dist) if dist >= 0 else BUCKETS, i] = 1
    for i in range(B_LEN):
        dist = 2 * W - 1 - i
        onehot[bucket(dist) if 0 <= dist < W else BUCKETS, C_LEN + i] = 1
    ident = np.eye(P, dtype=np.float32)
    hot = np.zeros((P, NH), np.float32)
    for q in range(4):
        hot[32 * q:32 * q + NH] = np.eye(NH)
    pos = np.arange(S, dtype=np.float32)
    inv = (np.float32(10000.0) ** (-np.arange(0, ROPE, 2, dtype=np.float32) / np.float32(ROPE))).astype(np.float32)
    ang = inv[:, None] * pos[None, :]
    cos, sin = np.cos(ang).astype(np.float32), np.sin(ang).astype(np.float32)
    rope = np.zeros((P, S), np.float32)
    rope[0:64] = 1
    rope[64:96] = np.concatenate([cos, cos])
    rope[96:128] = np.concatenate([-sin, sin])
    causal = np.where(np.arange(P)[None, :] <= np.arange(P)[:, None], 0, NEG).astype(np.float32)
    fixed = np.concatenate([ident, hot, ident[::-1], causal], axis=1)
    return {"c_onehot": onehot, "c_fixed": np.ascontiguousarray(fixed), "c_rope": rope}


N_SETUP = 6
NORMS = ("mix_e", "mlp0", "mix_o", "cq", "ckv", "mlp1", "final")
NORM_TILES = (KT, KT, KT, 2, 1, KT, KT)
SQ_BEFORE = {k: sum(NORM_TILES[:i]) for i, k in enumerate(NORMS)}
ADD_BEFORE = {k: sum(NORM_TILES[:i]) - i for i, k in enumerate(NORMS)}
XG_BEFORE = {"mix_e": 0, "mlp0": KT, "mix_o": 2 * KT, "mlp1": 3 * KT, "final": 4 * KT}


def slab_plan():
    even = [("fa", 1536)] + [(f"ka{i}", 512 + P * i) for i in range(4)] + [(f"qa{i}", P * i) for i in range(4)] \
        + [(f"va{i}", 1024 + P * i) for i in range(4)] + [("kb", 2056), ("vb", 2184)] \
        + [(f"qb{i}", 1544 + P * i) for i in range(4)]
    odd = [("nar", 896), ("qi0", 640), ("qi1", 768), ("cq0", 936), ("cq1", 1064), ("ckv", 1192), ("kv", 512)] \
        + [(f"qc{i}", P * i) for i in range(4)]
    return even, odd


EVEN, ODD = slab_plan()
N_IN0 = 0
N_OUT0 = N_IN0 + len(EVEN)
SPLIT0 = len(EVEN) - 4
N_MLP0 = N_OUT0 + KT
N_IN1 = N_MLP0 + 2 * KT * GROUPS
N_OUT1 = N_IN1 + len(ODD)
N_MLP1 = N_OUT1 + KT
N_END = N_MLP1 + 2 * KT * GROUPS
NAR = N_IN1

GAIN = {"mix_e": 0, "mlp0": 8, "mix_o": 16, "mlp1": 24, "final": 32, "cq": 40, "ckv": 42}
N_GAIN = 43


def trunk(nc, x, norm_mix_e, w_in_e, b_forget, sink_logits, w_out_e, norm_mix_o, w_in_o, norm_cq, norm_ckv,
          w_uq, w_ukv, w_out_o, norm_mlp, w_mlp1, w_mlp2, rel_bias, norm_final,
          c_onehot, c_fixed, c_rope, out):
    with ExitStack() as ctx:
        def sb(name, shape, dt=F32):
            return ctx.enter_context(nc.sbuf_tensor(name, shape, dt))

        def sem(name):
            return ctx.enter_context(nc.semaphore(name))

        bank = [ctx.enter_context(nc.psum_tensor(f"bank{i}", [P, 512], F32)) for i in range(8)]
        bias_rows = nc.dram_tensor("bias_rows", (2 * NH, 1024), F32, kind="Internal").ap()

        xT = sb("xT", [P, KT, S])
        xh = sb("xh", [P, KT, S], F32R)
        xl = sb("xl", [P, KT, S], F32R)
        raw = sb("raw", [P, 2, 1024])
        wh = sb("wh", [P, 2, 1024], F32R)
        wl = sb("wl", [P, 2, 1024], F32R)
        rstd = sb("rstd", [P, S])
        rstd_q = sb("rstd_q", [P, S])
        rstd_k = sb("rstd_k", [P, S])
        sqsum = sb("sqsum", [P, S])
        sq = sb("sq", [P, 2, S])
        tbuf = sb("tbuf", [P, 2, S])
        probs = sb("probs", [P, 2, 1280])
        probT_h = sb("probT_h", [P, 1280], F32R)
        probT_l = sb("probT_l", [P, 1280], F32R)
        strip_raw = sb("strip_raw", [P, 2, S])
        strip_h = sb("strip_h", [P, 2, S], F32R)
        strip_l = sb("strip_l", [P, 2, S], F32R)
        rope = sb("rope", [P, S])
        ident_b = sb("ident_b", [P, P], BF16)
        flip_r = sb("flip_r", [P, P], F32R)
        ones = sb("ones", [P, P])
        fixed = sb("fixed", [P, P + NH])
        ident = fixed[:, 0:P]
        hot = fixed[:, P:P + NH]
        gain = sb("gain", [P, N_GAIN])
        sinks = sb("sinks", [P, NH, 2])
        sink_in = sb("sink_in", [P, NH])
        bfor = sb("bfor", [NH, 1])
        negmax = sb("negmax", [P, 2, 4])
        expsum = sb("expsum", [P, 2, 4])
        rsum = sb("rsum", [P, 2, 4])
        widx = sb("widx", [P, NQ, N_IDX])
        best8 = sb("best8", [P, 3, 8])
        fin = sb("fin", [P, 4, NQ])
        causal = sb("causal", [P, P], BF16)
        spare = sb("spare", [P, 1])
        score = sb("score", [P, 1152])
        mask_c = sb("mask_c", [P, 1152], BF16)
        USIZE = 19456
        ur = sb("ur", [P, USIZE], F32R)

        at = [0]

        def take(words):
            at[0] += words
            assert at[0] <= USIZE, at[0]
            return ur[:, at[0] - words:at[0]]

        def tiles(n, w=S):
            return take(n * w).rearrange("p (n w) -> p n w", n=n)

        qa = (tiles(4), tiles(4))
        ka = (tiles(4), tiles(4))
        va = (tiles(NQ), tiles(NQ))
        kb = (tiles(2), tiles(2))
        vb = (tiles(2), tiles(2))
        fl = take(S)
        gb = take(S)
        gf = tiles(2)
        qb = (xh[:, 4:8, :], xl[:, 4:8, :])
        at[0] = 0
        hid = (tiles(KT), tiles(KT))
        xn = (tiles(KT), tiles(KT))
        at[0] = 0
        qd = (tiles(2), tiles(2))
        kd = (tiles(2), tiles(2))
        vd = (tiles(NQ), tiles(NQ))
        wuq = (tiles(2, 1024), tiles(2, 1024))
        wuk = (take(512), take(512))
        wuv = (take(512), take(512))
        cq = (tiles(2), tiles(2))
        ckv = (take(S), take(S))
        kc = (take(S), take(S))
        vc = (tiles(NQ, P), tiles(NQ, P))
        qc = (xh[:, 0:4, :], xl[:, 0:4, :])
        qi = (qd[0], qd[1])
        ki = (kd[0][:, 0, :], kd[1][:, 0, :])
        kr = (kd[0][64:96, :, :], kd[1][64:96, :, :])

        relu = probs[:, 1, 0:1152]
        SC = {1: (0, 256), 2: (256, 384), 3: (640, 512)}
        praw = probs[:, :, :].rearrange("p a b -> p (a b)")
        uq_raw = praw[:, 0:1536].rearrange("p (k n) -> p k n", k=2)
        ukv_raw = praw[:, 1536:2560]
        tbuf_flat = tbuf[:, :, :].rearrange("p a b -> p (a b)")
        x_tok = [(praw[:, 0:512], praw[:, 512:1024]), (praw[:, 1024:1536], praw[:, 1536:2048]),
                 (tbuf_flat[:, 0:512], tbuf_flat[:, 512:1024]), (sqsum[:, :], rstd[:, :])]
        otok = praw[:, 0:2048].rearrange("p (a n) -> p a n", a=2)
        qb_raw = [sq[:, 0, :], sq[:, 1, :], strip_raw[:, 0, :], strip_raw[:, 1, :]]
        qc_raw = [rope[:, :], strip_raw[:, 0, :], strip_raw[:, 1, :], rstd[:, :]]
        late = {0: (qb[0], qb[1], qb_raw), 2 * NH: (qc[0], qc[1], qc_raw)}
        o_raw = rope
        diag = [sqsum, sq[:, 1, :]]
        onehot = strip_raw[0:BUCKETS + 1, :, :].rearrange("p a b -> p (a b)")
        bias_out = strip_raw[0:2 * NH, :, :].rearrange("p a b -> p (a b)")
        g_rows = rstd_q[0:N_GAIN, 0:P]
        table = rstd_k[0:BUCKETS + 1, 2 * P:2 * P + 2 * NH]
        w_scaled = rstd_q[0:N_IDX, :]
        kr32 = strip_raw[64:96, 1, :]

        raw_loaded = [sem("raw_loaded0"), sem("raw_loaded1")]
        fixed_loaded = sem("fixed_loaded")
        gains_loaded = sem("gains_loaded")
        setup_loaded = sem("setup_loaded")
        x_loaded = [sem(f"x_loaded{a}") for a in range(NQ)]
        x_turned = sem("x_turned")
        x_copied_a = sem("x_copied_a")
        x_copied_v = sem("x_copied_v")
        gains_turned = sem("gains_turned")
        bias_made = sem("bias_made")
        setup_act = sem("setup_act")
        memsets_done = sem("memsets_done")
        bias_copied = sem("bias_copied")
        bias_stored = sem("bias_stored")
        w_hi = sem("w_hi")
        w_lo = sem("w_lo")
        slab_done = sem("slab_done")
        slab_taken = sem("slab_taken")
        p_hi = sem("p_hi")
        p_lo = sem("p_lo")
        vt_ready = sem("vt_ready")
        xg_hi = sem("xg_hi")
        xg_lo = sem("xg_lo")
        sq_ready = sem("sq_ready")
        sq_added = sem("sq_added")
        sum_ready = sem("sum_ready")
        rec_ready = sem("rec_ready")
        root_ready = sem("root_ready")
        diag_ready = sem("diag_ready")
        spread_done = sem("spread_done")
        norm_ready = sem("norm_ready")
        h32 = sem("h32")
        h_hi = sem("h_hi")
        h_lo = sem("h_lo")
        step_v = sem("step_v")
        fg_in = sem("fg_in")
        fg_out = sem("fg_out")
        scores_ready = sem("scores_ready")
        max_ready = sem("max_ready")
        exp_done = sem("exp_done")
        rsum_ready = sem("rsum_ready")
        diag_made = sem("diag_made")
        late_hi = sem("late_hi")
        late_lo = sem("late_lo")
        probs_ready = sem("probs_ready")
        pt_ready = sem("pt_ready")
        pt_hi = sem("pt_hi")
        pt_lo = sem("pt_lo")
        o_ready = sem("o_ready")
        o_hi = sem("o_hi")
        o_lo = sem("o_lo")
        o_pair_lo = sem("o_pair_lo")
        strip_loaded = [sem("strip_loaded0"), sem("strip_loaded1")]
        sink_set = sem("sink_set")
        strip_hi_ready = sem("strip_hi_ready")
        prep_ready = sem("prep_ready")
        low_loaded = sem("low_loaded")
        low_hi = sem("low_hi")
        low_lo = sem("low_lo")
        wi_scaled = sem("wi_scaled")
        wi_turned = sem("wi_turned")
        widx_ready = sem("widx_ready")
        idx_ready = sem("idx_ready")
        relu_ready = sem("relu_ready")
        idx_added = sem("idx_added")
        causal_cut = sem("causal_cut")
        mask_ready = sem("mask_ready")
        dv_ready = sem("dv_ready")
        dv_hi = sem("dv_hi")
        dv_lo = sem("dv_lo")
        dq_ready = sem("dq_ready")
        dq_taken = sem("dq_taken")
        dq_t = sem("dq_t")
        dq_hi = sem("dq_hi")
        dq_lo = sem("dq_lo")
        fin_turned = sem("fin_turned")
        fin_v = sem("fin_v")
        fin_a = sem("fin_a")
        fin_ready = sem("fin_ready")
        kr_rotated = sem("kr_rotated")
        kr_hi = sem("kr_hi")
        kr_ready = sem("kr_ready")
        out_stored = [sem("out_stored0"), sem("out_stored1")]

        class Steps:

            def __init__(self, eng, s):
                self.eng, self.s, self.n = eng, s, 0

            def done(self, ins):
                ins.then_inc(self.s, 1)
                self.n += 1
                return self.n

            def wait(self, n=None):
                self.eng.wait_ge(self.s, self.n if n is None else n)

            def link(self, ins):
                self.done(ins)
                self.wait()

        def weights_of(n):
            def block(w, col, width=P, row=0, rows=D):
                return w[row:row + rows, col:col + width].rearrange("(k p) n -> p k n", p=P)
            if n < N_OUT0:
                name, col = EVEN[n]
                return block(w_in_e[0], col, NH if name == "fa" else P)
            if n < N_MLP0:
                return block(w_out_e[0], P * (n - N_OUT0))
            if N_IN1 <= n < N_OUT1:
                return block(w_in_o[0], ODD[n - N_IN1][1])
            return block(w_out_o[0], P * (n - N_OUT1))

        def raw_count(n):
            extra = 48 if n >= NAR and n % 2 == NAR % 2 else 0
            return 16 * (n // 2 + 1) + extra

        def pj(n):
            return bank[4 + n % 4]

        def units(j):
            if attention(j) == "B":
                return [(0, 0, 0, 130, 0), (1, 0, 130, 258, 130), (2, 1, 0, 258, 388), (3, 2, 0, 258, 646)]
            return [(0, 0, 0, 128, 0), (2, 0, 128, 384, 128), (1, 1, 0, 256, 512), (3, 2, 0, 512, 768)]

        def unit_of(j, blk):
            return [u for u in units(j) if u[0] == blk][0]

        def attention(j):
            return "ABDC"[j // NH]

        def pt_parts(j):
            if attention(j) == "B":
                return [(0, 3, 0, 0, 256), (1, 3, 256, 128, 256), (2, 4, 0, 256, 256), (3, 4, 256, 384, 128)]
            return [(0, 3, 0, 0, 512), (1, 4, 0, 128, 384), (3, 4, 384, 384, 128), (2, 5, 0, 256, 256)]

        def pt_banks(j):
            return [(3, 512), (4, 384)] if attention(j) == "B" else [(3, 512), (4, 512), (5, 256)]

        PT_COL = {3: 0, 4: 512, 5: 1024}

        def pt_before(j):
            return sum(len(pt_banks(i)) for i in range(j))

        def out_tile(j):
            h = j % NH
            return {"A": 0, "B": 4, "C": 0, "D": 4}[attention(j)] + h // 2, 64 * (h % 2)

        def strip_count(j):
            return sum(1 for i in range(j + 1) if attention(i) in "BC" and i % 2 == j % 2)

        def normed_before(j):
            return 4 * direct_before(j)

        def direct_before(j):
            return sum(1 for i in range(j) if attention(i) != "D")

        def t5_rank(j):
            return sum(1 for i in range(j) if attention(i) in "BC")

        def prep_rank(j):
            return sum(1 for i in range(j) if attention(i) in "ABC")

        def out_bank(j):
            return bank[6] if j < 2 * NH else bank[7]

        def latent_banks(h):
            return (bank[3], bank[0]) if h < 2 else (bank[6], bank[6])

        def normed(norm):
            return xn if norm[0:3] == "mlp" else (xh, xl)

        def out_order(first):
            return list(range(KT)) if first == 0 else [4, 5, 6, 7, 0, 1, 2, 3]

        def head_steps(first, last):
            return range(first - (4 if attention(first) == "D" else 3), last)

        def latent(first, j):
            return first == 2 * NH <= j < 3 * NH

        def low_pieces():
            def columns(t, w):
                return t.rearrange("p (h c) -> p h c", c=w)
            pieces = []
            for k in range(2):
                src, dst = columns(uq_raw[:, k, :], 96), [columns(wuq[a][:, k, :], P) for a in range(2)]
                for d0, d1, c0 in ((0, 96, 0), (96, 112, 80), (112, 128, 64)):
                    pieces.append((src[:, :, c0:c0 + d1 - d0], [t[:, :, d0:d1] for t in dst]))
            for w, c in ((wuk, slice(0, HD)), (wuv, slice(HD, P))):
                pieces.append((columns(ukv_raw, P)[:, :, c], [columns(w[a], HD) for a in range(2)]))
            return pieces

        block = ctx.enter_context(nc.Block())

        @block.sync
        def _(sp):
            def load_slab(n, src=None):
                if n >= 2:
                    sp.wait_ge(w_hi, n - 1)
                    sp.wait_ge(w_lo, n - 1)
                if n == NAR:
                    w = w_in_o[0]
                    dst = raw[:, n % 2, :].rearrange("p (k n) -> p k n", k=KT)
                    for c0, c1, d0 in ((896, 960, 0), (1320, 1352, 64), (1336, 1352, 96), (1320, 1336, 112)):
                        sp.dma_start(dst[:, :, d0:d0 + c1 - c0],
                                     w[:, c0:c1].rearrange("(k p) n -> p k n", p=P)).then_inc(raw_loaded[n % 2], 16)
                    return
                src = weights_of(n)
                width = src.shape[2]
                dst = raw[:, n % 2, 0:KT * width].rearrange("p (k n) -> p k n", k=KT)
                sp.dma_start(dst, src).then_inc(raw_loaded[n % 2], 16)

            def load_mlp_group(layer, n0, g):
                base = n0 + 16 * g
                w1 = w_mlp1[layer].rearrange("(k p) n -> p k n", p=P)
                w2 = w_mlp2[layer].rearrange("(g k p) n -> p g k n", p=P, k=KT)
                for s in range(2 * KT):
                    sp.wait_ge(w_hi, base + (s - 1))
                    sp.wait_ge(w_lo, base + (s - 1))
                    slot = (n0 + s) % 2
                    dst = raw[:, slot, :].rearrange("p (k n) -> p k n", k=KT)
                    if s < KT:
                        src = w1[:, :, bass.ds(g * D + P * s, P)]
                    else:
                        src = w2[:, bass.ds(g, 1), :, P * (s - KT):P * (s - KT + 1)]
                        dst = raw[:, slot, :].rearrange("p (o k n) -> p o k n", k=KT, o=1)
                    sp.dma_start(dst, src).then_inc(raw_loaded[slot], 16)

            def load_mlp(layer, n0):
                with sp.Fori(0, GROUPS) as g:
                    load_mlp_group(layer, n0, g)

            def load_strip(j):
                slot = j % 2
                if attention(j - 2) in "BC":
                    sp.wait_ge(prep_ready, prep_rank(j - 2) + 1)
                if attention(j) == "B":
                    row, off, width, c0 = j % NH, C_LEN, 2 * W, 2
                else:
                    row, off, width, c0 = NH + j % NH, 0, S, 0
                src = bias_rows[row:row + 1, off:off + width + P - 1]
                src = bass.AP(src.tensor, src.offset, [[1, P], [1, width]])
                sp.dma_start(strip_raw[:, slot, c0:c0 + width], src).then_inc(strip_loaded[slot], 16)

            for a in range(3):
                sp.dma_start((praw[:, 0:1024], praw[:, 1024:2048], tbuf_flat)[a], x[0, P * a:P * (a + 1), :])\
                    .then_inc(x_loaded[a], 16)
            for half in range(2):
                sp.dma_start(x_tok[3][half], x[0, 3 * P:4 * P, 512 * half:512 * (half + 1)]).then_inc(x_loaded[3], 16)
            for key, src in (("mix_e", norm_mix_e[0]), ("mlp0", norm_mlp[0]), ("mix_o", norm_mix_o[0]),
                             ("mlp1", norm_mlp[1]), ("final", norm_final), ("cq", norm_cq[0]), ("ckv", norm_ckv[0])):
                rows = src.shape[0] // P
                sp.dma_start(g_rows[GAIN[key]:GAIN[key] + rows, :], src.rearrange("(t p) -> t p", p=P))\
                    .then_inc(gains_loaded, 16)
            load_slab(0)
            load_slab(1)
            for dst, src in ((rstd_k[:, 0:2 * P], c_fixed[:, P + NH:3 * P + NH]), (table[0:BUCKETS, :], rel_bias),
                             (onehot, c_onehot), (rope[:, :], c_rope), (bfor[:, :], b_forget.rearrange("a h -> h a")),
                             (sink_in[:, :], sink_logits.to_broadcast([P, NH]))):
                sp.dma_start(dst, src).then_inc(setup_loaded, 16)
            for n in range(2, 8):
                load_slab(n)
            sp.wait_ge(bias_copied, 1)
            sp.dma_start(bias_rows, bias_out).then_inc(bias_stored, 16)
            for n in range(8, N_OUT0 + 4):
                load_slab(n)
            sp.wait_ge(bias_stored, 16)
            sp.wait_ge(late_lo, 4)
            for j in range(NH, 2 * NH):
                load_strip(j)
            sp.wait_ge(pt_ready, pt_before(2 * NH))
            sp.dma_start(uq_raw, w_uq[0].rearrange("(k p) n -> p k n", p=P)).then_inc(low_loaded, 16)
            sp.dma_start(ukv_raw, w_ukv[0]).then_inc(low_loaded, 16)
            for n in range(N_OUT0 + 4, N_MLP0):
                load_slab(n)
            load_mlp(0, N_MLP0)
            for n in range(N_IN1, N_OUT1 + 4):
                load_slab(n)
            sp.wait_ge(late_lo, 8)
            for j in range(3 * NH, 4 * NH):
                load_strip(j)
            for n in range(N_OUT1 + 4, N_MLP1):
                load_slab(n)
            load_mlp(1, N_MLP1)
            for a in range(NQ):
                sp.wait_ge(fin_v, a + 1)
                sp.wait_ge(fin_a, a + 1)
                sp.dma_start(out[0, P * a:P * (a + 1), :], otok[:, a % 2, :]).then_inc(out_stored[a % 2], 16)
            for a in range(2):
                sp.wait_ge(out_stored[a], 32)

        @block.tensor
        def _(pe):
            mm = nc.tensor.matmul

            def product(dst, lhs, rhs, start=True, stop=True, check=True):
                mm(dst, lhs[0], rhs[0], start=start, stop=False, skip_group_check=not check)
                mm(dst, lhs[0], rhs[1], start=False, stop=False, skip_group_check=not check)
                return mm(dst, lhs[1], rhs[0], start=False, stop=stop, skip_group_check=not check)

            def slab(n, slot, dst, acts, tile_wait=None, width=P, norm_part=None, after=KT - 1):
                pe.wait_ge(w_hi, n + 1)
                pe.wait_ge(w_lo, n + 1)
                for k in range(KT):
                    if tile_wait:
                        tile_wait(k)
                    cols = slice(width * k, width * (k + 1))
                    last = product(dst, (wh[:, slot, cols], wl[:, slot, cols]), (acts[0][:, k, :], acts[1][:, k, :]),
                                   start=k == 0, stop=k == KT - 1)
                    if k == KT - 1:
                        last.then_inc(slab_done, 1)
                    if norm_part and k == after:
                        norm_part()

            def slab_tiles(n, ks, whole):
                pe.wait_ge(w_hi, n + 1)
                pe.wait_ge(w_lo, n + 1)
                for k in ks:
                    cols = slice(P * k, P * (k + 1))
                    last = product(pj(n)[:, :], (wh[:, n % 2, cols], wl[:, n % 2, cols]), (xh[:, k, :], xl[:, k, :]),
                                   start=k == whole[0], stop=k == whole[-1])
                if ks[-1] == whole[-1]:
                    last.then_inc(slab_done, 1)

            def sum_squares(norm):
                if norm == "ckv":
                    pe.wait_ge(norm_ready, NORMS.index(norm))
                    pe.wait_ge(sq_ready, SQ_BEFORE[norm] + 1)
                else:
                    pe.wait_ge(sq_added, ADD_BEFORE[norm] + NORM_TILES[NORMS.index(norm)] - 1)
                for a in range(NQ):
                    last = mm(bank[0][:, a:a + 1], sqsum[:, P * a:P * (a + 1)], ones[:, 0:1], start=True, stop=True)
                last.then_inc(sum_ready, 1)

            def spread(norm):
                pe.wait_ge(diag_ready, NORMS.index(norm) + 1)
                mm(bank[0][:, :], ones[:, :], sq[:, 0, :], start=True, stop=True).then_inc(spread_done, 1)

            def turn_values(n, b):
                pe.wait_ge(slab_taken, n + 1)
                for a in range(NQ):
                    last = nc.tensor.transpose(bank[b][:, P * a:P * (a + 1)], tbuf[:, n % 2, P * a:P * (a + 1)],
                                               ident[:, :])
                last.then_inc(vt_ready, 1)

            def mlp_group(n0, H0, norm, g):
                base = n0 + 16 * g
                for s in range(2 * KT):
                    n = base + s
                    pe.wait_ge(slab_taken, n - 3)
                    if s < KT:
                        wait = (lambda k: pe.wait_ge(xg_lo, XG_BEFORE[norm] + k + 1)) if s == 0 else None
                        part = {0: lambda: sum_squares(norm), 1: lambda: spread(norm)}.get(s) if isinstance(g, int) else None
                        slab(n, (n0 + s) % 2, pj(n0 + s)[:, :], xn, wait, norm_part=part, after=4 - s)
                    else:
                        wait = (lambda k: pe.wait_ge(h_lo, 8 * g + (H0 + k + 1))) if s == KT else None
                        slab(n, (n0 + s) % 2, pj(n0 + s)[:, :], hid, wait)

            def mlp(n0, H0, norm):
                mlp_group(n0, H0, norm, 0)
                with pe.Fori(1, GROUPS) as g:
                    mlp_group(n0, H0, norm, g)

            def scores(j):
                kind, h, slot = attention(j), j % NH, j % 2
                r = 64 * (h % 2)
                if kind in "ABC":
                    pe.wait_ge(prep_ready, prep_rank(j) + 1)
                if kind == "D":
                    pe.wait_ge(dq_lo, 2 * (h + 1))
                if j == NH:
                    pe.wait_ge(late_lo, 4)
                if j == 3 * NH:
                    pe.wait_ge(mask_ready, 1)
                    pe.wait_ge(late_lo, 8)
                if j == 2 * NH:
                    pe.wait_ge(dv_lo, 4)
                    pe.wait_ge(dq_taken, 4)
                for i, (blk, b, col, width, _) in enumerate(units(j)):
                    if i == 0 or units(j)[i - 1][1] != b:
                        if j not in (0, 2 * NH):
                            pe.wait_ge(exp_done, 3 * (j - 1) + b + 1)
                    qs = slice(P * blk, P * (blk + 1))
                    last_in_bank = i + 1 == len(units(j)) or units(j)[i + 1][1] != b
                    if kind == "B":
                        t = h // 2
                        kv = h // 4
                        dst = bank[b][:, col:col + width]
                        c0 = 0 if width == 258 else 128
                        if c0 == 0:
                            mm(dst, flip_r[:, :], strip_h[:, slot, 0:258], start=True, stop=False)
                            mm(dst, flip_r[:, :], strip_l[:, slot, 0:258], start=False, stop=False)
                        else:
                            mm(dst[:, 0:2], flip_r[:, :], strip_h[:, slot, 0:2], start=True, stop=False)
                            mm(dst[:, 0:2], flip_r[:, :], strip_l[:, slot, 0:2], start=False, stop=True)
                            mm(dst[:, 2:130], flip_r[:, :], strip_h[:, slot, 130:258], start=True, stop=False)
                            mm(dst[:, 2:130], flip_r[:, :], strip_l[:, slot, 130:258], start=False, stop=False)
                        k0 = max(blk - 1, 0) * P
                        ks = slice(k0, k0 + width - 2)
                        last = product(dst[:, 2:width], (qb[0][r:r + 64, t, qs], qb[1][r:r + 64, t, qs]),
                                       (kb[0][r:r + 64, kv, ks], kb[1][r:r + 64, kv, ks]), start=False)
                    else:
                        dst = bank[b][:, col:col + width]
                        if kind == "A":
                            t = h // 2
                            mm(dst, fl[:, qs], gf[:, slot, 0:width], start=True, stop=False)
                            product(dst, (qa[0][r:r + 64, t, qs], qa[1][r:r + 64, t, qs]),
                                    (ka[0][r:r + 64, t, 0:width], ka[1][r:r + 64, t, 0:width]), start=False, stop=False)
                            last = mm(dst[:, P * blk:P * (blk + 1)], ident_b[:, :], causal[:, :], start=False, stop=True)
                        elif kind == "D":
                            product(dst, (qd[0][0:96, slot, qs], qd[1][0:96, slot, qs]),
                                    (kd[0][0:96, slot, 0:width], kd[1][0:96, slot, 0:width]), start=True, stop=False)
                            last = mm(dst[:, P * blk:P * (blk + 1)], ident_b[:, :], causal[:, :], start=False, stop=True)
                        else:
                            t = h // 2
                            off = S - width
                            mm(dst, flip_r[:, :], strip_h[:, slot, off:S], start=True, stop=False)
                            mm(dst, flip_r[:, :], strip_l[:, slot, off:S], start=False, stop=False)
                            if blk:
                                c0, w = SC[blk]
                                mm(dst, ident_b[:, :], mask_c[:, c0:c0 + w], start=False, stop=False)
                            last = product(dst, (qc[0][r:r + 64, t, qs], qc[1][r:r + 64, t, qs]),
                                           (kc[0][r:r + 64, 0:width], kc[1][r:r + 64, 0:width]), start=False)
                    if last_in_bank:
                        last.then_inc(scores_ready, 1)

            def turn_probs(j):
                slot = j % 2
                if j == 0:
                    pe.wait_ge(slab_taken, N_OUT0)
                if j == 2 * NH:
                    pe.wait_ge(slab_taken, N_OUT1)
                if attention(j) == "D":
                    pe.wait_ge(diag_made, 4 * (j % NH + 1))
                else:
                    pe.wait_ge(probs_ready, normed_before(j + 1))
                parts = pt_parts(j)
                for i, (kt, b, col, q0, nq) in enumerate(parts):
                    if (i == 0 or parts[i - 1][1] != b):
                        before = [x for x in range(j) if x // (2 * NH) == j // (2 * NH) and any(bb == b for bb, _ in pt_banks(x))]
                        if before:
                            x = before[-1]
                            k = [bb for bb, _ in pt_banks(x)].index(b)
                            pe.wait_ge(pt_lo, pt_before(x) + k + 1)
                    for q in range(q0, q0 + nq, P):
                        blk = q // P
                        _, _, _, width, pcol = unit_of(j, blk)
                        if attention(j) == "B":
                            c = pcol + (2 if kt == blk - 1 or blk == 0 else 130)
                        else:
                            c = pcol + P * kt
                        dst = bank[b][:, col + q - q0:col + q - q0 + P]
                        if attention(j) == "D":
                            done = mm(dst, probs[:, slot, c:c + P], diag[slot][:, q:q + P], start=True, stop=True)
                        else:
                            done = nc.tensor.transpose(dst, probs[:, slot, c:c + P], ident[:, :])
                    if i + 1 == len(parts) or parts[i + 1][1] != b:
                        done.then_inc(pt_ready, 1)

            def values(j):
                kind, h = attention(j), j % NH
                if j not in (0, 2 * NH):
                    if attention(j - 1) != "D":
                        pe.wait_ge(o_lo, direct_before(j))
                    pe.wait_ge(o_hi, j)
                for i, (kt, b, col, q0, nq) in enumerate(pt_parts(j)):
                    k = [bb for bb, _ in pt_banks(j)].index(b)
                    pe.wait_ge(pt_lo, pt_before(j) + k + 1)
                    pc = PT_COL[b] + col
                    t = h // 2
                    v = {"A": lambda a: va[a][:, kt, P * t:P * (t + 1)],
                         "B": lambda a: vb[a][:, h // 4, P * kt:P * (kt + 1)],
                         "D": lambda a: vd[a][:, kt, P * t:P * (t + 1)],
                         "C": lambda a: vc[a][:, kt, :]}[kind]
                    last = product(out_bank(j)[:, q0:q0 + nq], (v(0), v(1)),
                                   (probT_h[:, pc:pc + nq], probT_l[:, pc:pc + nq]),
                                   start=i == 0, stop=i == 3, check=kind != "B")
                last.then_inc(o_ready, 1)

            def latent_query(h):
                if h == 0:
                    pe.wait_ge(p_lo, SPLIT0 + 7)
                    pe.wait_ge(low_lo, KT)
                else:
                    pe.wait_ge(dq_taken, 2 * h)
                if h == 2:
                    pe.wait_ge(slab_taken, N_OUT1)
                for k in range(2):
                    last = product(latent_banks(h)[0][:, :],
                                   (wuq[0][:, k, P * h:P * (h + 1)], wuq[1][:, k, P * h:P * (h + 1)]),
                                   (cq[0][:, k, :], cq[1][:, k, :]), start=k == 0, stop=k == 1)
                last.then_inc(dq_ready, 1)

            def latent_key(h):
                if h == 0:
                    pe.wait_ge(norm_ready, NORMS.index("ckv") + 1)
                if h >= 2:
                    pe.wait_ge(dq_taken, 2 * h + 1)
                product(latent_banks(h)[1][0:64, :], (wuk[0][:, HD * h:HD * (h + 1)], wuk[1][:, HD * h:HD * (h + 1)]),
                        ckv).then_inc(dq_ready, 1)

            def heads(first, last, steps):
                for s in steps:
                    if first <= s + 2 < last:
                        scores(s + 2)
                    if latent(first, s + 4):
                        latent_query((s + 4) % NH)
                    if first <= s:
                        values(s)
                    if first <= s + 1 < last:
                        turn_probs(s + 1)
                    if latent(first, s + 4):
                        latent_key((s + 4) % NH)

            def out_projection(n0, first, last):
                order = out_order(first)
                pe.wait_ge(o_lo, direct_before(last - 2))
                if first:
                    pe.wait_ge(o_pair_lo, NH // 2)
                slab_tiles(n0, order[:-1], order)
                values(last - 1)
                pe.wait_ge(pt_lo, pt_before(last))
                early = 3 if pj(n0 + 1) is not out_bank(last - 1) else 0
                if early:
                    slab_tiles(n0 + 1, order[:early], order)
                pe.wait_ge(o_lo, direct_before(last))
                slab_tiles(n0, order[-1:], order)
                slab_tiles(n0 + 1, order[early:], order)
                for n in range(n0 + 2, n0 + KT):
                    if n >= n0 + 4:
                        pe.wait_ge(slab_taken, n - 3)
                    slab_tiles(n, order, order)

            steps0, steps1 = head_steps(0, 2 * NH), head_steps(2 * NH, 4 * NH)
            pe.wait_ge(fixed_loaded, 16)
            for a in range(NQ):
                pe.wait_ge(x_loaded[a], 32 if a == 3 else 16)
                for half in range(2):
                    for k in range(4):
                        last = nc.tensor.transpose(bank[2 * a + half][:, P * k:P * (k + 1)],
                                                   x_tok[a][half][:, P * k:P * (k + 1)], ident[:, :])
                    last.then_inc(x_turned, 1)
                if a == 2:
                    pe.wait_ge(gains_loaded, 16 * 7)
                    pe.wait_ge(x_copied_a, 1)
                    nc.tensor.transpose(bank[0][:, 0:N_GAIN], g_rows, ident[0:N_GAIN, 0:N_GAIN]).then_inc(gains_turned, 1)

            def bias_products():
                pe.wait_ge(setup_loaded, 16 * N_SETUP)
                for c in range(2):
                    last = mm(bank[1 + c][0:2 * NH, :], table, onehot[:, 512 * c:512 * (c + 1)], start=True, stop=True)
                last.then_inc(bias_made, 1)

            for n in range(N_OUT0):
                name = EVEN[n][0]
                if n >= 4:
                    pe.wait_ge(slab_taken, n - 3)
                if n == N_OUT0 - 1:
                    pe.wait_ge(p_lo, SPLIT0)
                    heads(0, 2 * NH, steps0[:2])
                width = NH if name == "fa" else P
                dst = pj(n)[0:NH, :] if name == "fa" else pj(n)[:, :]
                if n == 1:
                    pe.wait_ge(memsets_done, 1)
                if n == 4:
                    bias_products()
                if EVEN[n][0] == "va1":
                    pe.wait_ge(bias_copied, 1)
                part = {1: lambda: sum_squares("mix_e"), 2: lambda: spread("mix_e")}.get(n)
                slab(n, n % 2, dst, (xh, xl), (lambda k: pe.wait_ge(xg_lo, k + 1)) if n == 0 else None, width,
                     part, KT - 1 if n == 1 else 5)
                prev = EVEN[n - 1][0] if n else ""
                if prev in ("va0", "va1", "va2", "va3", "vb"):
                    v = [e[0] for e in EVEN if e[0][0] == "v"].index(prev)
                    if v >= 2:
                        pe.wait_ge(p_lo, n - 2)
                    turn_values(n - 1, 1 + v % 2)
            heads(0, 2 * NH, steps0[2:-1])
            out_projection(N_OUT0, 0, 16)
            mlp(N_MLP0, 0, "mlp0")

            def input_slab(i, norm_part=None, after=KT - 1):
                n = N_IN1 + i
                pe.wait_ge(slab_taken, n - 3)
                slab(n, n % 2, pj(n)[:, :], (xh, xl), (lambda k: pe.wait_ge(xg_lo, 2 * KT + k + 1)) if i == 0 else None,
                     norm_part=norm_part, after=after)

            input_slab(0, lambda: sum_squares("mix_o"), 4)
            input_slab(1, lambda: spread("mix_o"), 3)
            input_slab(2)
            input_slab(3)
            pe.wait_ge(wi_scaled, 1)
            for a in range(NQ):
                last = nc.tensor.transpose(bank[3][:, 8 * a:8 * a + 8], w_scaled[:, P * a:P * (a + 1)],
                                           ident[0:8, 0:8])
            last.then_inc(wi_turned, 1)
            pe.wait_ge(p_lo, SPLIT0 + 3)
            for i in range(N_IDX):
                r = 32 * (i % 4)
                for blk in (1, 2, 3):
                    if i:
                        pe.wait_ge(relu_ready, 3 * (i - 1) + blk)
                    w = SC[blk][1]
                    qs = slice(P * blk, P * (blk + 1))
                    product(bank[blk - 1][:, 0:w], (qi[0][r:r + 32, i // 4, qs], qi[1][r:r + 32, i // 4, qs]),
                            (ki[0][r:r + 32, 0:w], ki[1][r:r + 32, 0:w])).then_inc(idx_ready, 1)
                n = N_IN1 + 4 + i // 4
                if i % 4 == 0:
                    pe.wait_ge(slab_taken, n - 3)
                slab_tiles(n, [2 * (i % 4), 2 * (i % 4) + 1], range(KT))
            def latent_values(a):
                if a == 0:
                    pe.wait_ge(p_lo, SPLIT0 + 6)
                    pe.wait_ge(low_lo, KT)
                if a >= 2:
                    pe.wait_ge(dv_lo, a - 1)
                ts = slice(P * a, P * (a + 1))
                product(bank[1 + a % 2][:, :], (ckv[0][:, ts], ckv[1][:, ts]), wuv).then_inc(dv_ready, 1)

            pe.wait_ge(relu_ready, 3 * N_IDX)
            input_slab(6, lambda: sum_squares("cq"), 2)
            input_slab(7, lambda: spread("cq"), 2)
            pe.wait_ge(norm_ready, NORMS.index("cq") + 1)
            sum_squares("ckv")
            pe.wait_ge(widx_ready, 1)
            turn_values(N_IN1 + 6, 3)
            input_slab(8, lambda: spread("ckv"))
            latent_values(0)
            latent_values(1)
            input_slab(9, lambda: heads(2 * NH, 4 * NH, steps1[:1]), 3)
            latent_values(2)
            latent_values(3)
            input_slab(10, lambda: heads(2 * NH, 4 * NH, steps1[1:2]), 3)
            heads(2 * NH, 4 * NH, steps1[2:-1])
            out_projection(N_OUT1, 16, 32)
            mlp(N_MLP1, KT * GROUPS, "mlp1")

            pe.wait_ge(slab_taken, N_END)
            sum_squares("final")
            pe.wait_ge(xg_hi, XG_BEFORE["final"] + KT)
            for a in range(NQ):
                for half in range(2):
                    i = 2 * a + half
                    if i >= 6:
                        pe.wait_ge((fin_v, fin_a)[half], (i - 6) // 2 + 1)
                    for k in range(4):
                        last = nc.tensor.transpose(bank[1 + i % 6][:, P * k:P * (k + 1)],
                                                   xT[:, 4 * half + k, P * a:P * (a + 1)], ident[:, :])
                    last.then_inc(fin_turned, 1)

        @block.scalar
        def _(act):
            def copy(dst, src, scale=1.0):
                return nc.scalar.activation(dst, src, ACT.Copy, scale=scale)

            def split(slot, loaded, free, width=P):
                act.wait_ge(raw_loaded[slot], loaded)
                if free is not None:
                    act.wait_ge(slab_done, free)
                copy(wh[:, slot, 0:KT * width], raw[:, slot, 0:KT * width]).then_inc(w_hi, 1)

            def split_slab(n):
                if n < N_END:
                    split(n % 2, raw_count(n), n - 1 if n >= 2 else None, NH if n == 0 else P)

            def square(norm, m, src, wait=None):
                if wait is not None:
                    act.wait_ge(*wait)
                if m == 0:
                    if NORMS.index(norm):
                        act.wait_ge(sum_ready, NORMS.index(norm))
                    dst = sqsum[:, :]
                else:
                    dst = sq[:, m % 2, :]
                    if m >= 3:
                        act.wait_ge(sq_added, ADD_BEFORE[norm] + m - 2)
                nc.scalar.activation(dst, src, ACT.Square).then_inc(sq_ready, 1)

            def root(norm):
                act.wait_ge(rec_ready, NORMS.index(norm) + 1)
                nc.scalar.activation(fin[:, 2, :], fin[:, 1, :], ACT.Sqrt).then_inc(root_ready, 1)

            def normed_hi(norm, m):
                copy(normed(norm)[0][:, m, :], xT[:, m, :], gain[:, GAIN[norm] + m:GAIN[norm] + m + 1]).then_inc(xg_hi, 1)

            def projected(p, name, n):
                t = tbuf[:, n % 2, :]
                if name[0] == "v":
                    v = [e[0] for e in EVEN if e[0][0] == "v"].index(name)
                    act.wait_ge(vt_ready, v + 1)
                    b = bank[1 + v % 2][:, :].rearrange("p (a c) -> p a c", a=NQ)
                    if name == "vb":
                        for kv in range(2):
                            dst = vb[0][:, kv, :].rearrange("p (a c) -> p a c", a=NQ)
                            for d in range(2):
                                last = copy(dst[:, :, HD * d:HD * (d + 1)], b[:, :, HD * kv:HD * (kv + 1)])
                    else:
                        i = int(name[2])
                        last = copy(va[0][:, :, P * i:P * (i + 1)], b)
                    last.then_inc(p_hi, 1)
                    return
                act.wait_ge(slab_taken, n + 1)
                if name == "fa":
                    forget_gate(p)
                elif name == "kb":
                    for kv in range(2):
                        for d in range(2):
                            last = copy(kb[0][HD * d:HD * (d + 1), kv, :], t[HD * kv:HD * (kv + 1), :])
                    last.then_inc(p_hi, 1)
                elif name == "nar":
                    copy(w_scaled, t[32:32 + N_IDX, :], float(N_IDX ** -0.5)).then_inc(wi_scaled, 1)
                    for r in range(0, P, 32):
                        last = copy(ki[0][r:r + 32, :], t[0:32, :])
                    last.then_inc(p_hi, 1)
                elif name == "kv":
                    for d in range(2):
                        copy(kc[0][HD * d:HD * (d + 1), :], t[0:HD, :])
                    act.wait_ge(vt_ready, 6)
                    b = bank[3][:, :].rearrange("p (a c) -> p a c", a=NQ)
                    for d in range(2):
                        last = copy(vc[0][:, :, HD * d:HD * (d + 1)], b[:, :, HD:P])
                    last.then_inc(p_hi, 1)
                elif name[0:2] == "cq" or name == "ckv":
                    norm = name[0:2] if name[0:2] == "cq" else name
                    m = int(name[2]) if norm == "cq" else 0
                    square(norm, m, t)
                    g = GAIN[norm] + m
                    copy(cq[0][:, m, :] if norm == "cq" else ckv[0], t, gain[:, g:g + 1]).then_inc(p_hi, 1)
                else:
                    i = int(name[2])
                    dst = {"ka": ka, "qa": qa, "qi": qi}[name[0:2]][0][:, i, :]
                    copy(dst, t).then_inc(p_hi, 1)

            def forget_gate(p):
                t0, s0, s1 = tbuf[0:NH, 0, :], sq[0:NH, 0, :], sq[0:NH, 1, :]
                act.wait_ge(fg_in, 1)
                nc.scalar.activation(s1, s0, ACT.Exp).then_inc(fg_out, 1)
                act.wait_ge(fg_in, 2)
                nc.scalar.activation(s1, s0, ACT.Ln).then_inc(fg_out, 1)
                split_slab(5)
                act.wait_ge(fg_in, 3)
                copy(fl[0:NH, :], rstd_q[0:NH, :]).then_inc(p_hi, 1)

            def hidden(n, slot, H):
                act.wait_ge(h32, H + 1)
                copy(hid[0][:, slot, :], sq[:, slot % 2, :]).then_inc(h_hi, 1)

            def mlp_group(n0, H0, g, norm=None, low=False):
                for s in range(2 * KT):
                    n = 16 * g + (n0 + s)
                    if not isinstance(g, int) or n + 2 < N_END:
                        split((n0 + s) % 2, raw_count(n + 2) if isinstance(g, int) else 128 * g + raw_count(n0 + s + 2),
                              n + 1)
                    if s < KT:
                        hidden(n, s, 8 * g + (H0 + s))
                    elif norm:
                        m = s - KT
                        square(norm, m, xT[:, m, :], (slab_taken, n + 1))
                        if norm == "final":
                            copy(xT[:, m, :], xT[:, m, :], gain[:, GAIN[norm] + m:GAIN[norm] + m + 1]).then_inc(xg_hi, 1)
                        else:
                            normed_hi(norm, m)
                        if low:
                            if m == 0:
                                act.wait_ge(low_loaded, 32)
                            src, dst = low_pieces()[m]
                            copy(dst[0], src).then_inc(low_hi, 1)

            def mlp(n0, H0, norm, following, low=False):
                root(norm)
                with act.Fori(0, GROUPS - 1) as g:
                    mlp_group(n0, H0, g)
                mlp_group(n0, H0, GROUPS - 1, following, low)

            def strip(j):
                slot = j % 2
                width = 258 if attention(j) == "B" else S
                act.wait_ge(strip_loaded[slot], 16 * strip_count(j))
                if attention(j) == "B":
                    act.wait_ge(sink_set, j % NH + 1)
                if attention(j - 2) in "BC":
                    act.wait_ge(scores_ready, 3 * (j - 1))
                copy(strip_h[:, slot, 0:width], strip_raw[:, slot, 0:width]).then_inc(strip_hi_ready, 1)

            def load_exp():
                nc.scalar.activation(spare[:, :], ones[:, 0:1], ACT.Exp)

            def factors_of_sums(j):
                h, slot = j % NH, j % 2
                if h >= 2:
                    act.wait_ge(pt_ready, pt_before(j - 1))
                act.wait_ge(rsum_ready, j + 1)
                for blk, _, _, _, _ in units(j):
                    copy(diag[slot][:, P * blk:P * (blk + 1)], ident, rsum[:, slot, blk:blk + 1]).then_inc(diag_made, 1)

            def heads(first, last, steps):
                for s in steps:
                    if first <= s + 3 < last and attention(s + 3) in "BC":
                        strip(s + 3)
                    if latent(first, s + 1):
                        factors_of_sums(s + 1)
                    if first <= s:
                        for k, (b, w) in enumerate(pt_banks(s)):
                            act.wait_ge(pt_ready, pt_before(s) + k + 1)
                            if k == 0 and s:
                                act.wait_ge(o_ready, s)
                            copy(probT_h[:, PT_COL[b]:PT_COL[b] + w], bank[b][:, 0:w]).then_inc(pt_hi, 1)
                    if latent(first, s + 3):
                        h, slot = (s + 3) % NH, (s + 3) % 2
                        act.wait_ge(dq_taken, 2 * h + 2)
                        copy(kd[0][0:HD, slot, :], tbuf[0:HD, 1, :]).then_inc(dq_hi, 1)
                    if 0 <= s - first < 4:
                        i = s - first
                        act.wait_ge(slab_taken, N_OUT1 if first else N_OUT0)
                        hi, _, src = late[first]
                        copy(hi[:, i, :], src[i]).then_inc(late_hi, 1)
                    if first <= s + 2 < last:
                        j = s + 2
                        slot = j % 2
                        if j >= 2:
                            act.wait_ge(pt_ready, pt_before(j - 1))
                        us = units(j)
                        for i, (blk, b, col, w, pc) in enumerate(us):
                            act.wait_ge(max_ready, 3 * j + b + 1)
                            e = nc.scalar.activation(probs[:, slot, pc:pc + w], bank[b][:, col:col + w], ACT.Exp,
                                                     bias=negmax[:, slot, blk:blk + 1],
                                                     accum_out=expsum[:, slot, blk:blk + 1])
                            if i + 1 == len(us) or us[i + 1][1] != b:
                                e.then_inc(exp_done, 1)
                    if first <= s:
                        tile, r = out_tile(s)
                        act.wait_ge(o_ready, s + 1)
                        if attention(s) == "D":
                            if s == first:
                                act.wait_ge(late_lo, 5)
                            elif s % 2 == 0:
                                act.wait_ge(o_pair_lo, (s - first) // 2)
                            copy(o_raw[r:r + HD, :], out_bank(s)[r:r + HD, :])
                        copy(xh[r:r + HD, tile, :], out_bank(s)[r:r + HD, :]).then_inc(o_hi, 1)
                    if latent(first, s + 4):
                        h, slot = (s + 4) % NH, (s + 4) % 2
                        act.wait_ge(dq_t, h + 1)
                        copy(qd[0][0:96, slot, :], tbuf[0:96, 0, :]).then_inc(dq_hi, 1)

            def out_projection(n0, norm):
                for m in range(KT):
                    n = n0 + m
                    act.wait_ge(slab_done, n + 1)
                    split_slab(n + 2)
                    square(norm, m, xT[:, m, :], (slab_taken, n + 1))
                    normed_hi(norm, m)

            act.dma_start(fixed[:, :], c_fixed[:, 0:P + NH]).then_inc(fixed_loaded, 16)
            def x_part(a):
                act.wait_ge(x_turned, 2 * a + 1)
                copy(xT[:, 0:4, P * a:P * (a + 1)],
                     bank[2 * a][:, :].rearrange("p (k c) -> p k c", k=4)).then_inc(x_copied_a, 1)

            for a in range(3):
                x_part(a)
            split_slab(0)
            split_slab(1)
            x_part(3)
            act.wait_ge(gains_turned, 1)
            copy(gain[:, :], bank[0][:, 0:N_GAIN]).then_inc(setup_act, 1)
            act.wait_ge(x_copied_a, NQ)
            act.wait_ge(setup_act, 1)
            for m in range(KT):
                if m == 4:
                    act.wait_ge(x_copied_v, NQ)
                normed_hi("mix_e", m)
            for m in range(KT):
                square("mix_e", m, xT[:, m, :])
                if m == 3:
                    split_slab(2)
            act.wait_ge(setup_loaded, 16 * N_SETUP)
            act.wait_ge(memsets_done, 1)
            copy(sinks[:, :, 0], sink_in[:, :])
            copy(ident_b[:, :], ident)
            copy(flip_r[:, :], rstd_k[:, 0:P])
            copy(causal[:, :], rstd_k[:, P:2 * P])

            root("mix_e")
            split_slab(3)
            split_slab(4)
            projected(0, "fa", 0)
            load_exp()
            projected(1, EVEN[1][0], 1)
            projected(2, EVEN[2][0], 2)
            act.wait_ge(bias_made, 1)
            for c in range(2):
                last = copy(bias_out[:, 512 * c:512 * (c + 1)], bank[1 + c][0:2 * NH, :])
            last.then_inc(bias_copied, 1)
            steps = head_steps(0, 2 * NH)
            for n in range(4, N_OUT0):
                if n == N_OUT0 - 1:
                    heads(0, 2 * NH, steps[:2])
                split_slab(n + 2)
                if n <= len(EVEN) - 4:
                    projected(n - 1, EVEN[n - 1][0], n - 1)
            heads(0, 2 * NH, steps[2:3])
            heads(0, 2 * NH, steps[3:])
            out_projection(N_OUT0, "mlp0")
            mlp(N_MLP0, 0, "mlp0", "mix_o", low=True)

            p0 = SPLIT0
            root("mix_o")
            split_slab(N_IN1 + 2)
            split_slab(N_IN1 + 3)
            projected(p0, "nar", N_IN1)
            projected(p0 + 1, "qi0", N_IN1 + 1)
            split_slab(N_IN1 + 4)
            projected(p0 + 2, "qi1", N_IN1 + 2)
            split_slab(N_IN1 + 5)
            projected(p0 + 3, "cq0", N_IN1 + 3)
            for i in range(N_IDX):
                for blk in (1, 2, 3):
                    c0, w = SC[blk]
                    act.wait_ge(idx_ready, 3 * i + blk)
                    if i:
                        act.wait_ge(idx_added, 3 * (i - 1) + blk)
                    else:
                        act.wait_ge(low_lo, KT)
                    nc.scalar.activation(relu[:, c0:c0 + w], bank[blk - 1][:, 0:w], ACT.Relu,
                                         scale=float(D_IDX ** -0.5)).then_inc(relu_ready, 1)
                if i == 5:
                    split_slab(N_IN1 + 6)
                    projected(p0 + 4, "cq1", N_IN1 + 4)
            act.wait_ge(kr_rotated, 1)
            for slot in range(2):
                last = copy(kr[0][:, slot, :], kr32)
            last.then_inc(kr_hi, 1)

            def latent_values_hi(a):
                act.wait_ge(diag_ready, NORMS.index("ckv") + 1)
                act.wait_ge(dv_ready, a + 1)
                copy(vd[0][:, a, :], bank[1 + a % 2][:, :], fin[:, 3, a:a + 1]).then_inc(dv_hi, 1)

            steps = head_steps(2 * NH, 4 * NH)
            for i in range(5, len(ODD)):
                n = N_IN1 + i
                if i == 6:
                    projected(p0 + 5, "ckv", n - 1)
                    root("cq")
                if i == 8:
                    root("ckv")
                    projected(p0 + 6, "kv", N_IN1 + 6)
                if i == 9:
                    load_exp()
                    latent_values_hi(0)
                    latent_values_hi(1)
                    heads(2 * NH, 4 * NH, steps[:1])
                if i == 10:
                    latent_values_hi(2)
                    latent_values_hi(3)
                    heads(2 * NH, 4 * NH, steps[1:2])
                split_slab(n + 2)
            heads(2 * NH, 4 * NH, steps[2:])
            out_projection(N_OUT1, "mlp1")
            mlp(N_MLP1, KT * GROUPS, "mlp1", "final")

            root("final")
            act.wait_ge(fin_ready, 1)
            for a in range(NQ):
                act.wait_ge(fin_turned, 2 * a + 2)
                if a >= 2:
                    act.wait_ge(out_stored[a % 2], 16)
                copy(otok[:, a % 2, 512:1024], bank[1 + (2 * a + 1) % 6][:, :], fin[:, 3, a:a + 1]).then_inc(fin_a, 1)

        @block.gpsimd
        def _(pool):
            def sub(dst, a, b):
                return nc.gpsimd.tensor_tensor(dst, a, b, ALU.subtract)

            def split(slot, n, width=P):
                pool.wait_ge(w_hi, n + 1)
                c = slice(0, KT * width)
                sub(wl[:, slot, c], raw[:, slot, c], wh[:, slot, c].bitcast(F32)).then_inc(w_lo, 1)

            def mlp(n0, groups):
                with pool.Fori(0, groups) as g:
                    for s in range(2 * KT):
                        split((n0 + s) % 2, 16 * g + (n0 + s))

            def low(m):
                src, dst = low_pieces()[m]
                pool.wait_ge(low_hi, m + 1)
                sub(dst[1], src, dst[0].bitcast(F32)).then_inc(low_lo, 1)

            def prepare(j):
                slot, h = j % 2, j % NH
                if attention(j) == "A":
                    if j == 0:
                        pool.wait_ge(p_lo, 1)
                    if j >= 2:
                        pool.wait_ge(scores_ready, 3 * (j - 1))
                    nc.gpsimd.tensor_scalar(gf[:, slot, :], gb.bitcast(F32), hot[:, h:h + 1], None, ALU.mult)\
                        .then_inc(prep_ready, 1)
                elif attention(j) in "BC":
                    width = S
                    if attention(j) == "B":
                        width = 258
                        if h >= 2:
                            pool.wait_ge(prep_ready, prep_rank(j - 2) + 1)
                        else:
                            pool.wait_ge(late_lo, 4)
                        nc.gpsimd.tensor_copy(strip_raw[:, slot, 0:2], sinks[:, h, :]).then_inc(sink_set, 1)
                    pool.wait_ge(strip_hi_ready, t5_rank(j) + 1)
                    sub(strip_l[:, slot, 0:width], strip_raw[:, slot, 0:width],
                        strip_h[:, slot, 0:width].bitcast(F32)).then_inc(prep_ready, 1)

            def heads(first, last, steps):
                for s in steps:
                    if first <= s + 3 < last and s + 3 >= 2:
                        prepare(s + 3)
                    if 0 <= s - first < 4:
                        i = s - first
                        hi, lo, src = late[first]
                        pool.wait_ge(late_hi, i + (5 if first else 1))
                        sub(lo[:, i, :], src[i], hi[:, i, :].bitcast(F32)).then_inc(late_lo, 1)
                    if latent(first, s + 3):
                        split_key(s + 3)
                    if latent(first, s + 4):
                        rotate_query(s + 4)
                        split_query(s + 4)
                    if latent(first, s) and s % 2:
                        tile, _ = out_tile(s)
                        pool.wait_ge(o_hi, s + 1)
                        sub(xl[:, tile, :], o_raw[:, :], xh[:, tile, :].bitcast(F32)).then_inc(o_pair_lo, 1)

            def rotate_query(j):
                h = j % NH
                if h:
                    pool.wait_ge(dq_lo, 2 * h)
                else:
                    pool.wait_ge(w_lo, N_OUT1)
                pool.wait_ge(dq_taken, 2 * h + 1)
                nc.gpsimd.tensor_tensor(tbuf[64:96, 0, :], tbuf[64:96, 0, :], sq[64:96, 0, :], ALU.add).then_inc(dq_t, 1)

            def split_query(j):
                h, slot = j % NH, j % 2
                pool.wait_ge(dq_hi, 2 * h + 1)
                pool.wait_ge(dq_t, h + 1)
                sub(qd[1][0:96, slot, :], tbuf[0:96, 0, :], qd[0][0:96, slot, :].bitcast(F32)).then_inc(dq_lo, 1)

            def split_key(j):
                h, slot = j % NH, j % 2
                pool.wait_ge(dq_hi, 2 * h + 2)
                sub(kd[1][0:HD, slot, :], tbuf[0:HD, 1, :], kd[0][0:HD, slot, :].bitcast(F32)).then_inc(dq_lo, 1)

            for n in range(N_OUT0 + 2):
                if n in (N_OUT0 - 4, N_OUT0 - 3):
                    prepare(n - (N_OUT0 - 4))
                split(n % 2, n, NH if n == 0 else P)
            heads(0, 2 * NH, head_steps(0, 2 * NH))
            for n in range(N_OUT0 + 2, N_MLP0):
                split(n % 2, n)
            mlp(N_MLP0, GROUPS - 1)
            for n in range(N_IN1 - 2 * KT, N_IN1 + 7):
                split(n % 2, n)
                m = n - (N_IN1 - KT) - 2
                if 0 <= m < KT:
                    low(m)
            pool.wait_ge(idx_added, 3 * N_IDX)
            for blk in (1, 2, 3):
                c0 = SC[blk][0] + P * blk
                last = nc.gpsimd.affine_select(out=score[:, c0:c0 + P], in_=score[:, c0:c0 + P], compare_op=ALU.is_ge,
                                               fill=NEG, base=0, pattern=[[-1, P]], channel_multiplier=1)
            last.then_inc(causal_cut, 1)
            steps = head_steps(2 * NH, 4 * NH)
            for n in range(N_IN1 + 7, N_OUT1 + 2):
                split(n % 2, n)
                if n == N_OUT1 - 1:
                    heads(2 * NH, 4 * NH, steps[:1])
                if n == N_OUT1:
                    heads(2 * NH, 4 * NH, steps[1:2])
            heads(2 * NH, 4 * NH, steps[2:])
            for n in range(N_OUT1 + 2, N_MLP1):
                split(n % 2, n)
            mlp(N_MLP1, GROUPS)

        @block.vector
        def _(dve):
            v = nc.vector
            own = Steps(dve, step_v)

            def f(ap):
                return ap.bitcast(F32)

            def sub(dst, a, b):
                return v.tensor_tensor(dst, a, f(b), ALU.subtract)

            def token_factors(norm, sums):
                width = {"cq": Q_LORA, "ckv": KV_LORA}.get(norm, D)
                ms, b, y = fin[:, 0, :], fin[:, 1, :], fin[:, 2, :]
                i = NORMS.index(norm) + 1
                dve.wait_ge(sum_ready, i)
                own.link(v.tensor_scalar(ms, sums, 1.0 / width, EPS, ALU.mult, ALU.add))
                v.reciprocal(b, ms).then_inc(rec_ready, 1)
                dve.wait_ge(root_ready, i)
                own.link(v.scalar_tensor_tensor(b, y, -0.5, y, ALU.mult, ALU.mult))
                own.link(v.tensor_tensor(b, b, ms, ALU.mult))
                own.link(v.scalar_tensor_tensor(fin[:, 3, :], b, 1.5, y, ALU.add, ALU.mult))

            def spread_factors(norm):
                token_factors(norm, bank[0][:, 0:NQ])
                for a in range(NQ):
                    last = v.tensor_scalar(sq[:, 0, P * a:P * (a + 1)], ident, fin[:, 3, a:a + 1], None, ALU.mult)
                last.then_inc(diag_ready, 1)

            def take_factors(norm, dst, factor=None):
                dve.wait_ge(spread_done, NORMS.index(norm) + 1)
                if factor is None:
                    last = v.tensor_copy(dst, bank[0][:, :])
                else:
                    last = v.tensor_tensor(dst, bank[0][:, :], factor, ALU.mult)
                last.then_inc(norm_ready, 1)
                dve.wait_ge(norm_ready, NORMS.index(norm) + 1)

            def rsqrt(norm, dst):
                spread_factors(norm)
                take_factors(norm, dst)

            def take_slab(n, scale=1.0, dst=None):
                dve.wait_ge(slab_done, n + 1)
                rank = n if n < N_OUT0 else SPLIT0 + n - N_IN1
                if rank >= 3 and dst is None:
                    dve.wait_ge(p_lo, rank - 1)
                v.scalar_tensor_tensor(tbuf[:, n % 2, :] if dst is None else dst, pj(n)[:, :], scale, rstd[:, :], ALU.mult, ALU.mult)\
                    .then_inc(slab_taken, 1)

            def add_squares(norm, m):
                dve.wait_ge(sq_ready, SQ_BEFORE[norm] + m + 1)
                if m > 1:
                    dve.wait_ge(sq_added, ADD_BEFORE[norm] + m - 1)
                v.tensor_tensor(sqsum[:, :], sqsum[:, :], sq[:, m % 2, :], ALU.add).then_inc(sq_added, 1)

            def normed_lo(norm, m):
                T = XG_BEFORE[norm] + m
                dve.wait_ge(xg_hi, T + 1)
                hi, lo = (t[:, m, :] for t in normed(norm))
                v.scalar_tensor_tensor(lo, xT[:, m, :], gain[:, GAIN[norm] + m:GAIN[norm] + m + 1],
                                       f(hi), ALU.mult, ALU.subtract).then_inc(xg_lo, 1)

            def projected(p, name, n):
                t = tbuf[:, n % 2, :]
                dve.wait_ge(p_hi, p + 1)
                if name == "fa":
                    own.link(sub(fl[32:32 + NH, :], rstd_q[0:NH, :], fl[0:NH, :]))
                    v.tensor_scalar(gb[64:64 + NH, :], f(fl[0:NH, :]), -1.0, None, ALU.mult)
                    last = v.tensor_scalar(gb[96:96 + NH, :], f(fl[32:32 + NH, :]), -1.0, None, ALU.mult)
                elif name == "vb":
                    b = bank[1][:, :].rearrange("p (a c) -> p a c", a=NQ)
                    for kv in range(2):
                        hi, lo = (vb[a][:, kv, :].rearrange("p (a c) -> p a c", a=NQ) for a in range(2))
                        for d in range(2):
                            c = slice(HD * d, HD * (d + 1))
                            last = sub(lo[:, :, c], b[:, :, HD * kv:HD * (kv + 1)], hi[:, :, c])
                elif name[0:2] == "va":
                    i = int(name[2])
                    c = slice(P * i, P * (i + 1))
                    last = sub(va[1][:, :, c], bank[1 + i % 2][:, :].rearrange("p (a c) -> p a c", a=NQ), va[0][:, :, c])
                elif name == "kb":
                    for kv in range(2):
                        rows = slice(HD * kv, HD * (kv + 1))
                        for d in range(2):
                            last = sub(kb[1][HD * d:HD * (d + 1), kv, :], t[rows, :], kb[0][rows, kv, :])
                elif name == "nar":
                    for r in range(0, P, 32):
                        last = sub(ki[1][r:r + 32, :], t[0:32, :], ki[0][0:32, :])
                elif name == "kv":
                    for d in range(2):
                        sub(kc[1][HD * d:HD * (d + 1), :], t[0:HD, :], kc[0][0:HD, :])
                    b = bank[3][:, :].rearrange("p (a c) -> p a c", a=NQ)
                    for d in range(2):
                        c = slice(HD * d, HD * (d + 1))
                        last = sub(vc[1][:, :, c], b[:, :, HD:P], vc[0][:, :, c])
                elif name[0:2] == "cq" or name == "ckv":
                    norm = "cq" if name[0:2] == "cq" else "ckv"
                    m = int(name[2]) if norm == "cq" else 0
                    hi, lo = (cq[0][:, m, :], cq[1][:, m, :]) if norm == "cq" else ckv
                    g = GAIN[norm] + m
                    if m:
                        add_squares("cq", 1)
                    last = v.scalar_tensor_tensor(lo, t, gain[:, g:g + 1], f(hi), ALU.mult, ALU.subtract)
                else:
                    i = int(name[2])
                    pair = {"ka": ka, "qa": qa, "qi": qi}[name[0:2]]
                    last = sub(pair[1][:, i, :], t, pair[0][:, i, :])
                last.then_inc(p_lo, 1)

            def forget_gate():
                t0, t1, s0, s1, q0 = tbuf[0:NH, 0, :], tbuf[0:NH, 1, :], sq[0:NH, 0, :], sq[0:NH, 1, :], rstd_q[0:NH, :]
                dve.wait_ge(slab_done, 1)
                dve.wait_ge(setup_loaded, 16 * N_SETUP)
                own.link(v.tensor_tensor(t0, pj(0)[0:NH, :], rstd[0:NH, :], ALU.mult))
                v.tensor_scalar(t0, t0, bfor[:, :], None, ALU.add).then_inc(slab_taken, 1)
                dve.wait_ge(slab_taken, 1)
                v.scalar_tensor_tensor(s0, t0, -1.0, t0, ALU.mult, ALU.min).then_inc(fg_in, 1)
                dve.wait_ge(fg_out, 1)
                own.link(v.tensor_scalar(s0, s1, 1.0, None, ALU.add))
                own.link(v.scalar_tensor_tensor(t1, s0, -1.0, s1, ALU.add, ALU.subtract))
                v.tensor_scalar(q0, s0, -0.5, 1.5, ALU.mult, ALU.add).then_inc(fg_in, 1)
                dve.wait_ge(fg_out, 2)
                dve.wait_ge(fg_in, 2)
                v.memset(s0, 1.0)
                own.link(v.tensor_tensor(t1, t1, q0, ALU.mult))
                own.link(v.tensor_tensor(s1, s1, t1, ALU.subtract))
                own.link(v.scalar_tensor_tensor(t0, t0, 0.0, s1, ALU.min, ALU.subtract))
                v.tensor_tensor_scan(q0, s0, t0, 0.0, ALU.mult, ALU.add).then_inc(fg_in, 1)
                dve.wait_ge(fg_in, 3)

            def mlp_group(n0, H0, g, norm=None):
                for s in range(2 * KT):
                    n = 16 * g + (n0 + s)
                    dve.wait_ge(slab_done, n + 1)
                    ps = pj(n0 + s)[:, :]
                    if s < KT:
                        H = 8 * g + (H0 + s)
                        t, h = tbuf[:, s % 2, :], sq[:, s % 2, :]
                        v.tensor_tensor(t, ps, rstd[:, :], ALU.mult).then_inc(slab_taken, 1)
                        dve.wait_ge(slab_taken, n + 1)
                        if s >= 2:
                            dve.wait_ge(h_lo, H - 1)
                        v.scalar_tensor_tensor(h, t, 0.0, t, ALU.max, ALU.mult).then_inc(h32, 1)
                        dve.wait_ge(h_hi, H + 1)
                        sub(hid[1][:, s, :], h, hid[0][:, s, :]).then_inc(h_lo, 1)
                    else:
                        m = s - KT
                        v.tensor_tensor(xT[:, m, :], ps, xT[:, m, :], ALU.add).then_inc(slab_taken, 1)
                        if norm:
                            if norm != "final":
                                normed_lo(norm, m)
                            if m:
                                add_squares(norm, m)

            def mlp(n0, H0, norm, following):
                rsqrt(norm, rstd[:, :])
                with dve.Fori(0, GROUPS - 1) as g:
                    mlp_group(n0, H0, g)
                mlp_group(n0, H0, GROUPS - 1, following)

            def out_projection(n0, norm):
                for m in range(KT):
                    dve.wait_ge(slab_done, n0 + m + 1)
                    v.tensor_tensor(xT[:, m, :], pj(n0 + m)[:, :], xT[:, m, :], ALU.add).then_inc(slab_taken, 1)
                    if m:
                        add_squares(norm, m)
                    normed_lo(norm, m)

            def maxima(j):
                if j >= 2:
                    dve.wait_ge(exp_done, 3 * (j - 1))
                us = units(j)
                for i, (blk, b, col, w, _) in enumerate(us):
                    dve.wait_ge(scores_ready, 3 * j + b + 1)
                    m = v.reduce_max(negmax[:, j % 2, blk:blk + 1], bank[b][:, col:col + w], AX.X, negate=True)
                    if i + 1 == len(us) or us[i + 1][1] != b:
                        m.then_inc(max_ready, 1)

            def sums(j):
                dve.wait_ge(exp_done, 3 * (j + 1))
                if j >= 2:
                    if attention(j - 2) == "D":
                        dve.wait_ge(diag_made, 4 * ((j - 2) % NH + 1))
                    else:
                        dve.wait_ge(probs_ready, normed_before(j - 1))
                v.reciprocal(rsum[:, j % 2, :], expsum[:, j % 2, :]).then_inc(rsum_ready, 1)

            def normalise(j):
                sums(j)
                dve.wait_ge(rsum_ready, j + 1)
                for blk, _, _, w, pc in units(j):
                    pr = probs[:, j % 2, pc:pc + w]
                    v.tensor_scalar(pr, pr, rsum[:, j % 2, blk:blk + 1], None, ALU.mult).then_inc(probs_ready, 1)

            def outputs_lo(j):
                tile, r = out_tile(j)
                dve.wait_ge(o_hi, j + 1)
                sub(xl[r:r + HD, tile, :], out_bank(j)[r:r + HD, :], xh[r:r + HD, tile, :]).then_inc(o_lo, 1)

            def heads(first, last, steps):
                for s in steps:
                    if first <= s:
                        for k, (b, w) in enumerate(pt_banks(s)):
                            dve.wait_ge(pt_hi, pt_before(s) + k + 1)
                            c = slice(PT_COL[b], PT_COL[b] + w)
                            sub(probT_l[:, c], bank[b][:, 0:w], probT_h[:, c]).then_inc(pt_lo, 1)
                    if first <= s + 2 < last:
                        maxima(s + 2)
                    if first <= s + 1 < last and attention(s + 1) != "D":
                        normalise(s + 1)
                    if latent(first, s + 4):
                        take_latent_query(s + 4)
                    if latent(first, s + 2):
                        sums(s + 2)
                    if first == 2 * NH and 0 <= s + 2 - first < ROUNDS - EARLY_ROUNDS:
                        top8()
                    if first <= s and attention(s) != "D":
                        outputs_lo(s)
                    if latent(first, s + 4):
                        take_latent_key(s + 4)
                    if first == 2 * NH and s + 2 - first == ROUNDS - EARLY_ROUNDS - 1:
                        v.tensor_scalar(mask_c[:, :], score[:, :], 0.5 * TAKEN, NEG, ALU.is_gt, ALU.mult)\
                            .then_inc(mask_ready, 1)

            def take_latent_query(j):
                h = j % NH
                scale = float((HD + ROPE) ** -0.5)
                if h:
                    dve.wait_ge(dq_lo, 2 * h - 1)
                dve.wait_ge(dq_ready, 2 * h + 1)
                v.scalar_tensor_tensor(tbuf[0:96, 0, :], latent_banks(h)[0][0:96, :], scale, rstd_q[0:96, :], ALU.mult, ALU.mult)
                v.scalar_tensor_tensor(sq[64:96, 0, :], latent_banks(h)[0][96:128, :], scale, rstd_q[96:128, :],
                                       ALU.mult, ALU.mult).then_inc(dq_taken, 1)

            def take_latent_key(j):
                h = j % NH
                if h:
                    dve.wait_ge(dq_lo, 2 * h)
                dve.wait_ge(dq_ready, 2 * h + 2)
                v.tensor_tensor(tbuf[0:HD, 1, :], latent_banks(h)[1][0:HD, :], rstd_k[0:HD, :], ALU.mult).then_inc(dq_taken, 1)

            def top8():
                for blk in (1, 2, 3):
                    c0, w = SC[blk]
                    last = v.max(best8[:, blk - 1, :], score[:, c0:c0 + w])
                own.link(last)
                for blk in (1, 2, 3):
                    c0, w = SC[blk]
                    last = v.match_replace(score[:, c0:c0 + w], best8[:, blk - 1, :], score[:, c0:c0 + w], TAKEN)
                own.link(last)

            def rotate(t, dst):
                a, b = sq[64:96, 0, :], sq[64:96, 1, :]
                v.tensor_tensor(a, t[64:96, :], rope[64:96, :], ALU.mult)
                own.link(v.tensor_tensor(b, t[96:128, :], rope[96:128, :], ALU.mult))
                return v.tensor_tensor(dst, a, b, ALU.add)

            v.memset(sinks[:, :, :], NEG)
            v.memset(table[BUCKETS:BUCKETS + 1, :], NEG)
            v.memset(ones[:, :], 1.0)
            v.memset(fl[0:64, :].bitcast(F32), 0.0)
            v.memset(fl[64:128, :].bitcast(F32), 1.0)
            v.memset(gb[0:64, :].bitcast(F32), 1.0)
            v.memset(gb[64:128, :].bitcast(F32), 0.0).then_inc(memsets_done, 1)
            for a in range(NQ):
                dve.wait_ge(x_turned, 2 * a + 2)
                v.tensor_copy(xT[:, 4:8, P * a:P * (a + 1)],
                              bank[2 * a + 1][:, :].rearrange("p (k c) -> p k c", k=4)).then_inc(x_copied_v, 1)
            dve.wait_ge(x_copied_v, NQ)
            dve.wait_ge(setup_act, 1)
            for m in range(KT):
                normed_lo("mix_e", m)
            for m in range(1, KT):
                add_squares("mix_e", m)

            rsqrt("mix_e", rstd[:, :])
            forget_gate()
            for n in range(1, len(EVEN) - 4):
                take_slab(n, HD ** -0.5 if EVEN[n][0][0] == "q" else 1.0)
                projected(n - 1, EVEN[n - 1][0], n - 1)
            projected(len(EVEN) - 5, "vb", len(EVEN) - 5)
            steps = head_steps(0, 2 * NH)
            dve.wait_ge(spread_done, 1)
            dve.wait_ge(bias_stored, 16)
            for i in range(4):
                if i == 3:
                    heads(0, 2 * NH, steps[:2])
                take_slab(N_OUT0 - 4 + i, HD ** -0.5, qb_raw[i])
            heads(0, 2 * NH, steps[2:3])
            heads(0, 2 * NH, steps[3:])
            out_projection(N_OUT0, "mlp0")
            mlp(N_MLP0, 0, "mlp0", "mix_o")

            p0 = SPLIT0
            rsqrt("mix_o", rstd[:, :])
            take_slab(N_IN1)
            dve.wait_ge(slab_taken, N_IN1 + 1)
            rotate(tbuf[:, N_IN1 % 2, :], kr32).then_inc(kr_rotated, 1)
            for i in (1, 2):
                take_slab(N_IN1 + i)
                projected(p0 + i - 1, ODD[i - 1][0], N_IN1 + i - 1)
            take_slab(N_IN1 + 3)
            projected(p0 + 2, "qi1", N_IN1 + 2)
            dve.wait_ge(wi_turned, 1)
            v.tensor_copy(widx[:, :, :].rearrange("p a b -> p (a b)"), bank[3][:, 0:NQ * N_IDX]).then_inc(widx_ready, 1)
            dve.wait_ge(widx_ready, 1)
            dve.wait_ge(low_lo, KT)
            projected(p0 + 3, "cq0", N_IN1 + 3)
            for i in range(N_IDX):
                for blk in (1, 2, 3):
                    c0, w = SC[blk]
                    dve.wait_ge(relu_ready, 3 * i + blk)
                    wcol = widx[:, blk, i:i + 1]
                    if i == 0:
                        e = v.tensor_scalar(score[:, c0:c0 + w], relu[:, c0:c0 + w], wcol, None, ALU.mult)
                    else:
                        dve.wait_ge(idx_added, 3 * (i - 1) + blk)
                        e = v.scalar_tensor_tensor(score[:, c0:c0 + w], relu[:, c0:c0 + w], wcol, score[:, c0:c0 + w],
                                                   ALU.mult, ALU.add)
                    e.then_inc(idx_added, 1)
                if i == 4:
                    take_slab(N_IN1 + 4)
                if i == 5:
                    projected(p0 + 4, "cq1", N_IN1 + 4)
            dve.wait_ge(kr_hi, 1)
            for slot in range(2):
                last = sub(kr[1][:, slot, :], kr32, kr[0][:, slot, :])
            last.then_inc(kr_ready, 1)
            dve.wait_ge(causal_cut, 1)

            def latent_values_lo(a):
                dve.wait_ge(dv_hi, a + 1)
                v.scalar_tensor_tensor(vd[1][:, a, :], bank[1 + a % 2][:, :], fin[:, 3, a:a + 1], f(vd[0][:, a, :]),
                                       ALU.mult, ALU.subtract).then_inc(dv_lo, 1)

            steps = head_steps(2 * NH, 4 * NH)
            for i in range(5, len(ODD)):
                n = N_IN1 + i
                if i >= 9:
                    heads(2 * NH, 4 * NH, steps[i - 9:i - 8])
                if i < 7:
                    take_slab(n)
                else:
                    take_slab(n, HD ** -0.5, qc_raw[i - 7])
                if i == 5:
                    projected(p0 + 5, "ckv", n)
                    spread_factors("cq")
                if i == 6:
                    take_factors("cq", rstd_q[:, :], rope[:, :])
                if i == 7:
                    spread_factors("ckv")
                    projected(p0 + 6, "kv", n - 1)
                if i == 8:
                    take_factors("ckv", rstd_k[:, :])
                    latent_values_lo(0)
                    latent_values_lo(1)
                if i == 9:
                    latent_values_lo(2)
                    latent_values_lo(3)
                for _ in range(ROUNDS_AT[i]):
                    top8()
            heads(2 * NH, 4 * NH, steps[2:])
            out_projection(N_OUT1, "mlp1")
            mlp(N_MLP1, KT * GROUPS, "mlp1", "final")

            token_factors("final", bank[0][:, 0:NQ])
            v.tensor_copy(fin[:, 0, :], fin[:, 3, :]).then_inc(fin_ready, 1)
            for a in range(NQ):
                dve.wait_ge(fin_turned, 2 * a + 1)
                if a >= 2:
                    dve.wait_ge(out_stored[a % 2], 16)
                v.tensor_scalar(otok[:, a % 2, 0:512], bank[1 + (2 * a) % 6][:, :], fin[:, 3, a:a + 1], None, ALU.mult)\
                    .then_inc(fin_v, 1)


_INS = ["x", "norm_mix_e", "w_in_e", "b_forget", "sink_logits", "w_out_e", "norm_mix_o", "w_in_o", "norm_cq",
        "norm_ckv", "w_uq", "w_ukv", "w_out_o", "norm_mlp", "w_mlp1", "w_mlp2", "rel_bias", "norm_final"]


def kernel(**inputs):
    import concourse.bacc as bacc
    from concourse.bass_utils import run_bass_kernel_spmd

    nc = bacc.Bacc("TRN2", target_bir_lowering=False, num_devices=1)
    given = {name: np.ascontiguousarray(inputs[name]) for name in _INS}
    given.update(shape_constants())
    arrays, args = {}, []
    for name, a in given.items():
        arrays[f"in_{name}"] = a
        args.append(nc.dram_tensor(f"in_{name}", a.shape, mybir.dt.from_np(a.dtype), kind="ExternalInput").ap())
    out = nc.dram_tensor("out", (1, S, D), F32, kind="ExternalOutput").ap()
    trunk(nc, *args, out)
    result = run_bass_kernel_spmd(nc, [arrays], core_ids=[0])
    return result.results[0]["out"]
```
